# Optimizing a Trainium2 kernel written in Bass

```python
import math
import jax, jax.numpy as jnp
from jax import lax
import numpy as np

D_MODEL = 1024
BATCH = 1
SEQ = 256
DEPTH = 2

HEAD_DIM = 64
N_MIXERS = 2
DSW_GROUPS = ((128, 1), (512, 4), (2048, 16))
DSW_N_GROUPS = len(DSW_GROUPS)
DSW_HEADS_PER_GROUP = D_MODEL // (2 * HEAD_DIM)
DSW_HEADS = DSW_N_GROUPS * DSW_HEADS_PER_GROUP
DSW_OUT_WIDTH = DSW_HEADS_PER_GROUP * HEAD_DIM
MOBA_HEADS = D_MODEL // HEAD_DIM
MOBA_BLOCK = 256
MOBA_TOPK = 3
MOBA_Q_CHUNK = 32
D_FF = 4 * D_MODEL
REL_BUCKETS = 32
REL_MAX_DISTANCE = 2048
BIAS_HEADS = max(DSW_HEADS, MOBA_HEADS)

N_A_LAYERS = (DEPTH + 1) // 2
N_B_LAYERS = DEPTH // 2
EPS = 1e-6
NEG = -1e30
SCALE = HEAD_DIM ** -0.5


def rmsnorm(x, g):
    xf = x.astype(jnp.float32)
    y = xf * lax.rsqrt(jnp.mean(xf * xf, axis=-1, keepdims=True) + EPS)
    return (y * g.astype(jnp.float32)).astype(x.dtype)

def t5_bucket(dist):
    n = jnp.maximum(dist, 0)
    max_exact = REL_BUCKETS // 2
    nf = jnp.maximum(n, 1).astype(jnp.float32)
    large = max_exact + (jnp.log(nf / max_exact) / math.log(REL_MAX_DISTANCE / max_exact)
                         * (REL_BUCKETS - max_exact)).astype(jnp.int32)
    large = jnp.minimum(large, REL_BUCKETS - 1)
    return jnp.where(n < max_exact, n, large)

def softmax_attend(logits, v, eq):
    m = jnp.max(logits, axis=-1, keepdims=True)
    p = jnp.exp(logits - m)
    den = jnp.sum(p, axis=-1, keepdims=True)
    o = jnp.einsum(eq, p / den, v.astype(jnp.float32))
    return o, (m + jnp.log(den))[..., 0]

def dsw_group(q, k, v, rel_bias, col0, window, dilation):
    B, H, S, hd = q.shape
    n = window // dilation
    blk = n
    L = S // dilation
    nb = -(-L // blk)
    Lp = nb * blk

    def to_sub(t):
        t = t.reshape(B, H, L, dilation, hd).transpose(0, 1, 3, 2, 4)
        return jnp.pad(t, ((0, 0), (0, 0), (0, 0), (0, Lp - L), (0, 0)))

    def band(t):
        t = jnp.pad(t, ((0, 0), (0, 0), (0, 0), (blk, 0), (0, 0))).reshape(B, H, dilation, nb + 1, blk, hd)
        return jnp.concatenate([t[:, :, :, :-1], t[:, :, :, 1:]], axis=4)

    qs, ks, vs = to_sub(q), to_sub(k), to_sub(v)
    qb = qs.reshape(B, H, dilation, nb, blk, hd)
    kb, vb = band(ks), band(vs)
    logits = jnp.einsum('bhrnid,bhrnjd->bhrnij', qb, kb, preferred_element_type=jnp.float32) * SCALE

    i = jnp.arange(blk)[:, None]
    j = jnp.arange(2 * blk)[None, :]
    dist = blk + i - j
    in_band = (dist >= 0) & (dist <= n)
    first = (jnp.arange(nb) == 0)[:, None, None] & (j < blk)[None]
    mask = in_band[None] & ~first
    bias = rel_bias[t5_bucket(dist * dilation)][..., col0:col0 + H].transpose(2, 0, 1)
    logits = jnp.where(mask[None, None, None], logits + bias[None, :, None, None], NEG)

    o, lse = softmax_attend(logits, vb, 'bhrnij,bhrnjd->bhrnid')
    o = o.reshape(B, H, dilation, Lp, hd)[:, :, :, :L].transpose(0, 1, 3, 2, 4).reshape(B, H, S, hd)
    lse = lse.reshape(B, H, dilation, Lp)[..., :L].transpose(0, 1, 3, 2).reshape(B, H, S)
    return o, lse

def dsw_mixer(h, w_qkv, q_gain, k_gain, w_o, rel_bias):
    B, S, _ = h.shape
    G, Hg = DSW_N_GROUPS, DSW_HEADS_PER_GROUP
    qkv = (h @ w_qkv).reshape(B, S, 3, G, Hg, HEAD_DIM)
    q = rmsnorm(qkv[:, :, 0], q_gain)
    k = rmsnorm(qkv[:, :, 1], k_gain)
    v = qkv[:, :, 2]
    outs, lses = [], []
    for g, (window, dilation) in enumerate(DSW_GROUPS):
        o, lse = dsw_group(q[:, :, g].transpose(0, 2, 1, 3), k[:, :, g].transpose(0, 2, 1, 3),
                           v[:, :, g].transpose(0, 2, 1, 3), rel_bias, g * Hg, window, dilation)
        outs.append(o)
        lses.append(lse)
    wts = jax.nn.softmax(jnp.stack(lses), axis=0)
    o = jnp.einsum('gbhs,gbhsd->bshd', wts, jnp.stack(outs)).reshape(B, S, DSW_OUT_WIDTH)
    return o.astype(h.dtype) @ w_o

def gather_blocks(blocks, idx):
    return jax.vmap(jax.vmap(lambda bl, ix: bl[ix]))(blocks, idx)

def moba_mixer(h, w_qkv, q_gain, k_gain, w_o, rel_bias):
    B, S, _ = h.shape
    H, hd, blk = MOBA_HEADS, HEAD_DIM, MOBA_BLOCK
    qkv = (h @ w_qkv).reshape(B, S, 3, H, hd)
    q = rmsnorm(qkv[:, :, 0], q_gain).transpose(0, 2, 1, 3)
    k = rmsnorm(qkv[:, :, 1], k_gain).transpose(0, 2, 1, 3)
    v = qkv[:, :, 2].transpose(0, 2, 1, 3)
    nblk = -(-S // blk)
    Sp = nblk * blk
    pad = ((0, 0), (0, 0), (0, Sp - S), (0, 0))
    q, k, v = jnp.pad(q, pad), jnp.pad(k, pad), jnp.pad(v, pad)
    qb = q.reshape(B, H, nblk, blk, hd)
    kb = k.reshape(B, H, nblk, blk, hd)
    vb = v.reshape(B, H, nblk, blk, hd)
    pos = jnp.arange(Sp)
    qblk = pos // blk
    table_h = rel_bias[:, :H].T

    ii = jnp.arange(blk)
    own_bias = table_h[:, t5_bucket(ii[:, None] - ii[None, :])]
    lo = jnp.einsum('bhnid,bhnjd->bhnij', qb, kb, preferred_element_type=jnp.float32) * SCALE
    lo = jnp.where(ii[:, None] >= ii[None, :], lo + own_bias[None, :, None], NEG)
    o_own, lse_own = softmax_attend(lo, vb, 'bhnij,bhnjd->bhnid')
    o_own = o_own.reshape(B, H, Sp, hd)
    lse_own = lse_own.reshape(B, H, Sp)

    kmean = jnp.mean(kb.astype(jnp.float32), axis=3)
    gate = jnp.einsum('bhsd,bhnd->bhsn', q.astype(jnp.float32), kmean)
    past = jnp.arange(nblk)[None, :] < qblk[:, None]
    gate = jnp.where(past, gate, -jnp.inf)
    topk = min(MOBA_TOPK, nblk)
    _, sel = lax.top_k(gate, topk)
    sel_valid = sel < qblk[:, None]

    C = MOBA_Q_CHUNK
    nC = Sp // C

    def chunk(t):
        return jnp.moveaxis(t.reshape(B, H, nC, C, *t.shape[3:]), 2, 0)

    jj = jnp.arange(blk)
    head_ix = jnp.arange(H)[None, :, None, None]

    def attend(args):
        qc, selc, validc, posc = args
        flat = selc.reshape(B, H, C * topk)
        kg = gather_blocks(kb, flat).reshape(B, H, C, topk * blk, hd)
        vg = gather_blocks(vb, flat).reshape(B, H, C, topk * blk, hd)
        logits = jnp.einsum('bhcd,bhckd->bhck', qc, kg, preferred_element_type=jnp.float32) * SCALE
        kpos = (selc[..., None] * blk + jj).reshape(B, H, C, topk * blk)
        bias = table_h[head_ix, t5_bucket(posc[None, None, :, None] - kpos)]
        valid = jnp.repeat(validc, blk, axis=-1)
        logits = jnp.where(valid, logits + bias, NEG)
        return softmax_attend(logits, vg, 'bhck,bhckd->bhcd')

    o_sel, lse_sel = lax.map(attend, (chunk(q), chunk(sel), chunk(sel_valid), pos.reshape(nC, C)))
    o_sel = jnp.moveaxis(o_sel, 0, 2).reshape(B, H, Sp, hd)
    lse_sel = jnp.moveaxis(lse_sel, 0, 2).reshape(B, H, Sp)

    lse = jnp.logaddexp(lse_own, lse_sel)
    o = jnp.exp(lse_own - lse)[..., None] * o_own + jnp.exp(lse_sel - lse)[..., None] * o_sel
    o = o[:, :, :S].transpose(0, 2, 1, 3).reshape(B, S, H * hd)
    return o.astype(h.dtype) @ w_o

def sq_relu_mlp(h, w1, w2):
    return jnp.square(jax.nn.relu(h @ w1)) @ w2

def first_inputs(seed: int = 0) -> dict:
    key = jax.random.key(seed)
    ks = jax.random.split(key, 16)
    D = D_MODEL
    nrm = lambda k, shape, s: jax.random.normal(k, shape, jnp.float32) * s
    a_qkv_cols = 3 * DSW_HEADS * HEAD_DIM
    b_qkv_cols = 3 * MOBA_HEADS * HEAD_DIM
    return {
        "x": nrm(ks[0], (BATCH, SEQ, D), 1.0),
        "rel_bias": nrm(ks[1], (REL_BUCKETS, BIAS_HEADS), 0.3),
        "norm_mix": 1.0 + nrm(ks[2], (DEPTH, D), 0.02),
        "norm_ffn": 1.0 + nrm(ks[3], (DEPTH, D), 0.02),
        "a_w_qkv": nrm(ks[4], (N_A_LAYERS, D, a_qkv_cols), D ** -0.5),
        "a_q_gain": 1.0 + nrm(ks[5], (N_A_LAYERS, HEAD_DIM), 0.02),
        "a_k_gain": 1.0 + nrm(ks[6], (N_A_LAYERS, HEAD_DIM), 0.02),
        "a_w_o": nrm(ks[7], (N_A_LAYERS, DSW_OUT_WIDTH, D), DSW_OUT_WIDTH ** -0.5),
        "b_w_qkv": nrm(ks[8], (N_B_LAYERS, D, b_qkv_cols), D ** -0.5),
        "b_q_gain": 1.0 + nrm(ks[9], (N_B_LAYERS, HEAD_DIM), 0.02),
        "b_k_gain": 1.0 + nrm(ks[10], (N_B_LAYERS, HEAD_DIM), 0.02),
        "b_w_o": nrm(ks[11], (N_B_LAYERS, MOBA_HEADS * HEAD_DIM, D), (MOBA_HEADS * HEAD_DIM) ** -0.5),
        "ffn_w1": nrm(ks[12], (DEPTH, D, D_FF), D ** -0.5),
        "ffn_w2": nrm(ks[13], (DEPTH, D_FF, D), 0.5 * D_FF ** -0.5),
    }

def first_block(x, rel_bias, norm_mix, norm_ffn, a_w_qkv, a_q_gain, a_k_gain, a_w_o,
              b_w_qkv, b_q_gain, b_k_gain, b_w_o, ffn_w1, ffn_w2):
    h = x
    for i in range(DEPTH):
        u = rmsnorm(h, norm_mix[i])
        li = i // N_MIXERS
        if i % N_MIXERS == 0:
            h = h + dsw_mixer(u, a_w_qkv[li], a_q_gain[li], a_k_gain[li], a_w_o[li], rel_bias)
        else:
            h = h + moba_mixer(u, b_w_qkv[li], b_q_gain[li], b_k_gain[li], b_w_o[li], rel_bias)
        h = h + sq_relu_mlp(rmsnorm(h, norm_ffn[i]), ffn_w1[i], ffn_w2[i])
    return h


N_META = 16
N_Q_HEADS = 8
N_KV_HEADS = 2
GROUP = N_Q_HEADS // N_KV_HEADS
ATTN_WIDTH = N_Q_HEADS * HEAD_DIM
KV_WIDTH = N_KV_HEADS * HEAD_DIM
WINDOW = 128
BLOCK = 128
CONV_CH = D_MODEL // 2
CONV_WIDTH = 31
N_BUCKETS = 32
MAX_DISTANCE = 128
D_FF_2 = 2816
N_EXPERTS = 8
TOP_K = 2
D_EXPERT = 1408
N_DENSE = (DEPTH + 1) // 2
N_MOE = DEPTH // 2
ALPHA = (2 * DEPTH) ** 0.25
BETA = (8 * DEPTH) ** -0.25
LN_EPS = 1e-5
Q_END = ATTN_WIDTH
K_END = Q_END + KV_WIDTH
V_END = K_END + KV_WIDTH
GLU_END = V_END + 2 * CONV_CH
GA_END = GLU_END + D_MODEL
GC_END = GA_END + D_MODEL
IN_WIDTH = GC_END


def layer_norm(x, g, b):
    xf = x.astype(jnp.float32)
    mu = jnp.mean(xf, -1, keepdims=True)
    var = jnp.mean(jnp.square(xf - mu), -1, keepdims=True)
    y = (xf - mu) * lax.rsqrt(var + LN_EPS) * g.astype(jnp.float32) + b.astype(jnp.float32)
    return y.astype(x.dtype)

def rel_bucket(dist):
    n = jnp.maximum(dist, 0)
    max_exact = N_BUCKETS // 2
    nf = jnp.maximum(n, 1).astype(jnp.float32)
    large = max_exact + (jnp.log(nf / max_exact) / math.log(MAX_DISTANCE / max_exact)
                         * (N_BUCKETS - max_exact)).astype(jnp.int32)
    large = jnp.minimum(large, N_BUCKETS - 1)
    return jnp.where(n < max_exact, n, large)

def head_bias(rel_bias, bucket):
    b = rel_bias.astype(jnp.float32)[bucket]
    b = jnp.moveaxis(b, -1, -3)
    return b.reshape(b.shape[:-3] + (N_KV_HEADS, GROUP) + b.shape[-2:])

def sink_softmax(s, sink):
    m = jnp.maximum(jnp.max(s, -1, keepdims=True), sink)
    p = jnp.exp(s - m)
    return p / (jnp.sum(p, -1, keepdims=True) + jnp.exp(sink - m))

def sliding_window_attention(q, k, v, sinks, rel_bias):
    B, L = q.shape[:2]
    S = L - N_META
    nb = S // BLOCK
    scale = HEAD_DIM ** -0.5
    sink = sinks.astype(jnp.float32).reshape(N_KV_HEADS, GROUP)[:, :, None, None]

    qm = q[:, :N_META].reshape(B, N_META, N_KV_HEADS, GROUP, HEAD_DIM)
    km, vm = k[:, :N_META], v[:, :N_META]

    pos_m = jnp.arange(N_META)
    dist_mm = pos_m[:, None] - pos_m[None, :]
    s_mm = jnp.einsum('bqhgd,bkhd->bhgqk', qm, km).astype(jnp.float32) * scale
    s_mm = s_mm + head_bias(rel_bias, rel_bucket(dist_mm))
    s_mm = jnp.where(dist_mm >= 0, s_mm, -jnp.inf)
    p_mm = sink_softmax(s_mm, sink).astype(v.dtype)
    o_m = jnp.einsum('bhgqk,bkhd->bqhgd', p_mm, vm).reshape(B, N_META, ATTN_WIDTH)

    qr = q[:, N_META:].reshape(B, nb, BLOCK, N_KV_HEADS, GROUP, HEAD_DIM)
    kr = k[:, N_META:].reshape(B, nb, BLOCK, N_KV_HEADS, HEAD_DIM)
    vr = v[:, N_META:].reshape(B, nb, BLOCK, N_KV_HEADS, HEAD_DIM)
    zpad = jnp.zeros_like(kr[:, :1])
    kb = jnp.concatenate([jnp.concatenate([zpad, kr[:, :-1]], 1), kr], 2)
    vb = jnp.concatenate([jnp.concatenate([zpad, vr[:, :-1]], 1), vr], 2)

    a = jnp.arange(BLOCK)
    kk = jnp.arange(2 * BLOCK)
    blk = jnp.arange(nb)
    dist_band = BLOCK + a[:, None] - kk[None, :]
    mask_band = ((dist_band >= 0) & (dist_band < WINDOW))[None] & \
        ((blk[:, None, None] > 0) | (kk[None, None, :] >= BLOCK))
    q_pos = N_META + blk[:, None] * BLOCK + a[None, :]
    dist_meta = q_pos[:, :, None] - pos_m[None, None, :]

    s_band = jnp.einsum('bnqhgd,bnkhd->bnhgqk', qr, kb).astype(jnp.float32) * scale
    s_band = s_band + head_bias(rel_bias, rel_bucket(dist_band))
    s_band = jnp.where(mask_band[None, :, None, None], s_band, -jnp.inf)
    s_meta = jnp.einsum('bnqhgd,bmhd->bnhgqm', qr, km).astype(jnp.float32) * scale
    s_meta = s_meta + head_bias(rel_bias, rel_bucket(dist_meta))
    p = sink_softmax(jnp.concatenate([s_meta, s_band], -1), sink).astype(v.dtype)
    o_r = jnp.einsum('bnhgqm,bmhd->bnqhgd', p[..., :N_META], vm) + \
        jnp.einsum('bnhgqk,bnkhd->bnqhgd', p[..., N_META:], vb)
    o_r = o_r.reshape(B, S, ATTN_WIDTH)
    return jnp.concatenate([o_m, o_r], 1)

def conformer_conv(u, dw, db, g, b):
    val, gate = jnp.split(u, 2, axis=-1)
    h = val * jax.nn.sigmoid(gate)
    h = lax.conv_general_dilated(h, dw[:, None, :].astype(h.dtype), window_strides=(1,),
                                 padding=[(CONV_WIDTH - 1, 0)],
                                 dimension_numbers=('NWC', 'WIO', 'NWC'),
                                 feature_group_count=CONV_CH) + db
    h = layer_norm(h, g, b)
    return jax.nn.silu(h)

def swiglu(t, wg, wu, wd):
    return (jax.nn.silu(t @ wg) * (t @ wu)) @ wd

def moe_swiglu(h, router, wg, wu, wd):
    B, L, D = h.shape
    t = h.reshape(B * L, D)
    logits = (t @ router).astype(jnp.float32)
    vals, idx = lax.top_k(logits, TOP_K)
    gates = jax.nn.softmax(vals, axis=-1)
    combine = jnp.sum(jax.nn.one_hot(idx, N_EXPERTS, dtype=jnp.float32) * gates[..., None], 1)
    out = jnp.zeros_like(t)
    for e in range(N_EXPERTS):
        out = out + combine[:, e:e + 1].astype(t.dtype) * swiglu(t, wg[e], wu[e], wd[e])
    return out.reshape(B, L, D)

def second_inputs(seed: int = 0) -> dict:
    key = jax.random.key(seed)
    ks = iter(jax.random.split(key, 32))
    n = lambda shape, s: jax.random.normal(next(ks), shape, jnp.float32) * s
    D = D_MODEL
    return {
        "x": n((BATCH, SEQ, D), 1.0),
        "meta_tokens": n((N_META, D), 1.0),
        "emb_ln_g": 1.0 + n((D,), 0.02),
        "emb_ln_b": n((D,), 0.02),
        "rel_bias": n((N_BUCKETS, N_Q_HEADS), 0.5),
        "w_in": n((DEPTH, D, IN_WIDTH), D ** -0.5),
        "conv_dw": n((DEPTH, CONV_WIDTH, CONV_CH), CONV_WIDTH ** -0.5),
        "conv_b": n((DEPTH, CONV_CH), 0.02),
        "conv_ln_g": 1.0 + n((DEPTH, CONV_CH), 0.02),
        "conv_ln_b": n((DEPTH, CONV_CH), 0.02),
        "sinks": n((DEPTH, N_Q_HEADS), 0.5),
        "w_attn_proj": n((DEPTH, ATTN_WIDTH, D), ATTN_WIDTH ** -0.5),
        "w_conv_proj": n((DEPTH, CONV_CH, D), CONV_CH ** -0.5),
        "w_out": n((DEPTH, D, D), BETA * D ** -0.5),
        "ln1_g": 1.0 + n((DEPTH, D), 0.02),
        "ln1_b": n((DEPTH, D), 0.02),
        "ffn_w_gate": n((N_DENSE, D, D_FF_2), D ** -0.5),
        "ffn_w_up": n((N_DENSE, D, D_FF_2), D ** -0.5),
        "ffn_w_down": n((N_DENSE, D_FF_2, D), BETA * D_FF_2 ** -0.5),
        "router": n((N_MOE, D, N_EXPERTS), D ** -0.5),
        "moe_w_gate": n((N_MOE, N_EXPERTS, D, D_EXPERT), D ** -0.5),
        "moe_w_up": n((N_MOE, N_EXPERTS, D, D_EXPERT), D ** -0.5),
        "moe_w_down": n((N_MOE, N_EXPERTS, D_EXPERT, D), BETA * D_EXPERT ** -0.5),
        "ln2_g": 1.0 + n((DEPTH, D), 0.02),
        "ln2_b": n((DEPTH, D), 0.02),
    }

def second_block(x, meta_tokens, emb_ln_g, emb_ln_b, rel_bias, w_in, conv_dw, conv_b,
              conv_ln_g, conv_ln_b, sinks, w_attn_proj, w_conv_proj, w_out, ln1_g, ln1_b,
              ffn_w_gate, ffn_w_up, ffn_w_down, router, moe_w_gate, moe_w_up, moe_w_down,
              ln2_g, ln2_b):
    B = x.shape[0]
    meta = jnp.broadcast_to(meta_tokens[None].astype(x.dtype), (B, N_META, D_MODEL))
    h = layer_norm(jnp.concatenate([meta, x], axis=1), emb_ln_g, emb_ln_b)
    L = h.shape[1]
    for i in range(DEPTH):
        u = h @ w_in[i]
        q = u[..., :Q_END].reshape(B, L, N_Q_HEADS, HEAD_DIM)
        k = u[..., Q_END:K_END].reshape(B, L, N_KV_HEADS, HEAD_DIM)
        v = u[..., K_END:V_END].reshape(B, L, N_KV_HEADS, HEAD_DIM)
        y_attn = sliding_window_attention(q, k, v, sinks[i], rel_bias) @ w_attn_proj[i]
        y_conv = conformer_conv(u[..., V_END:GLU_END], conv_dw[i], conv_b[i],
                                conv_ln_g[i], conv_ln_b[i]) @ w_conv_proj[i]
        mix = (jax.nn.sigmoid(u[..., GLU_END:GA_END]) * y_attn
               + jax.nn.sigmoid(u[..., GA_END:GC_END]) * y_conv) @ w_out[i]
        h = layer_norm(ALPHA * h + mix, ln1_g[i], ln1_b[i])
        j = i // 2
        if i % 2 == 0:
            f = swiglu(h, ffn_w_gate[j], ffn_w_up[j], ffn_w_down[j])
        else:
            f = moe_swiglu(h, router[j], moe_w_gate[j], moe_w_up[j], moe_w_down[j])
        h = layer_norm(ALPHA * h + f, ln2_g[i], ln2_b[i])
    return h[:, N_META:]


def setup_inputs(seed=0):
    out = dict(first_inputs(seed))
    for name, value in second_inputs(seed + 1).items():
        if name != "x":
            out[name + "_2"] = value
    return out


def reference(
    x, rel_bias, norm_mix, norm_ffn, a_w_qkv, a_q_gain, a_k_gain, a_w_o, b_w_qkv, b_q_gain,
    b_k_gain, b_w_o, ffn_w1, ffn_w2, meta_tokens_2, emb_ln_g_2, emb_ln_b_2, rel_bias_2, w_in_2,
    conv_dw_2, conv_b_2, conv_ln_g_2, conv_ln_b_2, sinks_2, w_attn_proj_2, w_conv_proj_2,
    w_out_2, ln1_g_2, ln1_b_2, ffn_w_gate_2, ffn_w_up_2, ffn_w_down_2, router_2, moe_w_gate_2,
    moe_w_up_2, moe_w_down_2, ln2_g_2, ln2_b_2,
):
    x = first_block(
        x, rel_bias, norm_mix, norm_ffn, a_w_qkv, a_q_gain, a_k_gain, a_w_o, b_w_qkv, b_q_gain,
        b_k_gain, b_w_o, ffn_w1, ffn_w2,
    )
    return second_block(
        x, meta_tokens_2, emb_ln_g_2, emb_ln_b_2, rel_bias_2, w_in_2, conv_dw_2, conv_b_2,
        conv_ln_g_2, conv_ln_b_2, sinks_2, w_attn_proj_2, w_conv_proj_2, w_out_2, ln1_g_2,
        ln1_b_2, ffn_w_gate_2, ffn_w_up_2, ffn_w_down_2, router_2, moe_w_gate_2, moe_w_up_2,
        moe_w_down_2, ln2_g_2, ln2_b_2,
    )


_drawn_inputs = setup_inputs


def setup_inputs(seed=0):
    import zlib

    import numpy as np

    out = dict(_drawn_inputs(seed))
    spreads = {}
    factors = {'norm_mix': 3.956,
     'a_q_gain': 8.0,
     'a_k_gain': 8.0,
     'b_q_gain': 8.0,
     'b_k_gain': 8.0,
     'conv_b_2': 4.421,
     'conv_ln_g_2': 6.049,
     'conv_ln_b_2': 8.0,
     'sinks_2': 8.0,
     'rel_bias_2': 2.677}
    for name, (base, spread) in spreads.items():
        noise = np.random.default_rng([zlib.crc32(name.encode()), seed]).standard_normal(out[name].shape)
        drawn = base * np.exp(spread * noise) if base else spread * noise
        out[name] = __import__('jax').numpy.asarray(drawn.astype(out[name].dtype))
    for name, factor in factors.items():
        out[name] = (out[name] * factor).astype(out[name].dtype)
    return out
```

```python
import math
from contextlib import ExitStack

import numpy as np

import concourse.bass as bass
from concourse import mybir

F32 = mybir.dt.float32
F32R = mybir.dt.float32r
I32 = mybir.dt.int32
ALU = mybir.AluOpType
ACT = mybir.ActivationFunctionType
AX = mybir.AxisListType.X

P = 128
D = 1024
KD = D // P
S = 256
M = 16
T = S + M
NEG = -1e30
EPS = 1e-6
LN_EPS = 1e-5
ALPHA = 4 ** 0.25
SCALE = 64 ** -0.5
UT = 16
MAGIC = float(0x5F3759DF)

SMALL = [("nmix", 16), ("nffn", 16), ("embg", 8), ("embb", 8), ("ln1g", 16), ("ln1b", 16),
         ("ln2g", 16), ("ln2b", 16), ("dw", 2 * 4 * 31), ("cb", 8), ("clg", 8), ("clb", 8),
         ("gains", 4), ("sinks", 16), ("router", 64)]
OFF = {}
_o = 0
for _n, _w in SMALL:
    OFF[_n] = _o
    _o += _w
NSMALL = _o

CONSTS = [("ident", 128), ("ones", 128), ("iota", 8), ("flip", 128)]
COFF = {}
_o = 0
for _n, _w in CONSTS:
    COFF[_n] = _o
    _o += _w
NCONST = _o

JB = 384
N_UNITS = 311


def t5_bucket(n, n_buckets, max_distance):
    n = np.maximum(n, 0)
    exact = n_buckets // 2
    nf = np.maximum(n, 1).astype(np.float32)
    large = exact + (np.log(nf / np.float32(exact)) / np.float32(math.log(max_distance / exact))
                     * np.float32(n_buckets - exact)).astype(np.int32)
    return np.where(n < exact, n, np.minimum(large, n_buckets - 1))


def lookup(dists, keep, max_distance):
    b = t5_bucket(dists, 32, max_distance)
    out = np.zeros((33, dists.size), np.float32)
    out[b, np.arange(dists.size)] = 1.0
    out[:, ~keep] = 0.0
    out[32, ~keep] = NEG
    return out


def lookups():
    d = 255 - np.arange(JB)
    a = [lookup(d, (d >= 0) & (d <= 128), 2048), lookup(d, (d >= 0) & (d % 4 == 0), 2048),
         lookup(d, (d >= 0) & (d % 16 == 0), 2048), lookup(d, d >= 0, 2048)]
    w = [lookup(d, (d >= 0) & (d < 128), 128)]
    dm = 271 - np.arange(JB)
    c = [lookup(dm, dm >= 0, 128)]
    return np.concatenate(a + w + c, axis=1)


class Tok:
    def __init__(self):
        self.sem, self.value, self.used, self.dma = None, None, False, False


class Queue:

    def __init__(self, sem):
        self.sem, self.ops = sem, []

    def __call__(self, after, method, *args, **kw):
        waits = []
        flatten(after, waits)
        for t in waits:
            t.used = True
        tok = Tok()
        self.ops.append((method, args, kw, waits, tok))
        return tok

    def count(self):
        n = 0
        for *_, tok in self.ops:
            if tok.used and not tok.dma:
                n += 1
                tok.sem, tok.value = self.sem, n

    def emit(self, eng):
        seen = {}
        for method, args, kw, waits, tok in self.ops:
            best = {}
            for t in waits:
                k = id(t.sem)
                if seen.get(k, 0) < t.value and best.get(k, (0, None))[0] < t.value:
                    best[k] = (t.value, t.sem)
            for k, (v, s) in best.items():
                eng.wait_ge(s, v)
                seen[k] = v
            if method is None:
                continue
            ins = method(*args, **kw)
            if tok.dma:
                ins.then_inc(tok.sem, 16)
            elif tok.used:
                ins.then_inc(self.sem, 1)


def flatten(x, out):
    if x is None:
        return
    if isinstance(x, Tok):
        out.append(x)
        return
    for y in x:
        flatten(y, out)


def model_kernel(nc, w_d, x_d, meta_d, small_d, const_d, look_d, tab1_d, tab2_d, out_d, upto=99):
    bias_d = nc.dram_tensor("bias_scratch", (56, JB), F32, kind="Internal").ap()

    ctx = ExitStack()
    with ctx:
        def sb(name, shape, dt=F32, st=ctx):
            return st.enter_context(nc.sbuf_tensor(name, shape, dt))

        def sem(name):
            return ctx.enter_context(nc.semaphore(name))

        NS, NW = 4, 3
        stg = [sb(f"stg{i}", [P, UT * P]) for i in range(NS)]
        WH = [sb(f"wh{i}", [P, UT * P], F32R) for i in range(NW)]
        WL = [sb(f"wl{i}", [P, UT * P], F32R) for i in range(NW)]
        RES = sb("res", [P, KD, T])
        XH = sb("xh", [P, KD, T], F32R)
        XL = sb("xl", [P, KD, T], F32R)
        XC = sb("xc", [P, KD, T])
        SQ = sb("sq", [P, KD, T])
        SM = sb("small", [P, NSMALL])
        CS = sb("consts", [P, NCONST])
        st6 = sb("st6", [P, 6, 64])
        DG = sb("dg", [P, 3, P])
        BC = sb("bc", [P, T])
        T1 = sb("tab1", [33, 24])
        T2 = sb("tab2", [33, 8])
        ident = CS[:, COFF["ident"]:COFF["ident"] + P]
        ones = CS[:, COFF["ones"]:COFF["ones"] + P]
        flip = CS[:, COFF["flip"]:COFF["flip"] + P]
        iota = CS[:, COFF["iota"]:COFF["iota"] + 8]

        banks = [ctx.enter_context(nc.psum_tensor(f"bank{i}", [P, 512], F32)) for i in range(8)]
        free = [None] * 8
        turn = [0]

        s_pe, s_act, s_dve, s_pool, s_sp = (sem(n) for n in ("s_pe", "s_act", "s_dve", "s_pool", "s_sp"))
        s_w = [sem(f"s_w{i}") for i in range(NS)]
        PE, AC, V, G, SP = Queue(s_pe), Queue(s_act), Queue(s_dve), Queue(s_pool), Queue(s_sp)
        block = ctx.enter_context(nc.Block())

        def small(name, i, n=1):
            return SM[:, OFF[name] + i:OFF[name] + i + n]

        def start(q, eng, dst, src, s, value, *after):
            tok = q(after, eng.dma_start, dst, src)
            tok.sem, tok.value, tok.dma = s, value, True
            return tok

        def dma(dst, src, name, *after):
            return start(SP, nc.sync, dst, src, sem(name), 16, *after)

        def side_dma(dst, src, name, *after):
            return start(G, nc.gpsimd, dst, src, sem(name), 16, *after)

        def bank():
            i = turn[0] % 8
            turn[0] += 1
            return i

        load_tok, split_tok, done_tok = [], [], []

        def load_unit():
            u = len(load_tok)
            if u >= N_UNITS:
                return
            after = split_tok[u - NS] if u >= NS else None
            load_tok.append(start(SP, nc.sync, stg[u % NS][:, :], w_d[u], s_w[u % NS], 16 * (u // NS + 1), after))

        def split_unit():
            u = len(split_tok)
            if u >= N_UNITS:
                return
            while len(load_tok) <= u:
                load_unit()
            h, l, s = WH[u % NW], WL[u % NW], stg[u % NS]
            a = AC([load_tok[u], done_tok[u - NW] if u >= NW else None], nc.scalar.activation, h[:, :], s[:, :], ACT.Copy)
            b = V([a], nc.vector.tensor_tensor, l[:, :], s[:, :], h[:, :].bitcast(F32), ALU.subtract)
            split_tok.append([a, b])
            load_unit()

        at = [0]

        def tile_of(n):
            i = at[0]
            u, k = divmod(i, UT)
            if k == 0:
                while len(split_tok) < min(u + NW, N_UNITS):
                    split_unit()
            at[0] += n
            sl = slice(k * P, (k + n) * P)
            return WH[u % NW][:, sl], WL[u % NW][:, sl], split_tok[u]

        def tile_done(tok):
            if at[0] % UT == 0:
                done_tok.append(tok)

        def mm(out, a, b, start, stop, *after):
            return PE([*after], nc.tensor.matmul, out, a, b, start=start, stop=stop)

        def gemm(KT, NT, xh, xl, xt, n, evac, pump=None):
            for nt in range(NT):
                b = bank()
                out = banks[b][:, 0:n]
                for kt in range(KT):
                    wh, wl, wt = tile_of(1)
                    first, last = kt == 0, kt == KT - 1
                    mm(out, wh, xh(kt), first, False, wt, free[b], xt(kt))
                    mm(out, wh, xl(kt), False, False)
                    tok = mm(out, wl, xh(kt), False, last)
                    tile_done(tok)
                free[b] = evac(nt, out, tok)
                if pump is not None:
                    pump(nt)

        def rsqrt(a, r, tmp, after):
            t = V([after], nc.vector.tensor_scalar, tmp.bitcast(I32), a.bitcast(I32), 1, None, ALU.logical_shift_right)
            t = V([t], nc.vector.tensor_scalar, r.bitcast(I32), tmp.bitcast(I32), -1.0, MAGIC, ALU.mult, ALU.add)
            for _ in range(3):
                t = V([t], nc.vector.tensor_tensor, tmp, r, r, ALU.mult)
                t = V([t], nc.vector.scalar_tensor_tensor, tmp, tmp, -0.5, a, ALU.mult, ALU.mult)
                t = V([t], nc.vector.scalar_tensor_tensor, r, tmp, 1.5, r, ALU.add, ALU.mult)
            return t

        tiles1 = [(16, 128), (144, 128)]
        tiles2 = [(16, 128), (144, 128), (0, 16)]

        def token_sums(src, kts, tiles, dst, after, scale, eps):
            b = bank()
            for i, (c, n) in enumerate(tiles):
                for kt in range(kts):
                    tok = mm(banks[b][0:n, i:i + 1], src[:, kt, c:c + n], ones[:, 0:1], kt == 0, kt == kts - 1,
                             after[kt], free[b])
            outs = []
            for n, lo, hi in ((128, 0, 2), (16, 2, 3)):
                if len(tiles) == 2 and lo == 2:
                    continue
                outs.append(V([tok], nc.vector.tensor_scalar, dst[0:n, lo:hi], banks[b][0:n, lo:hi], scale, eps, ALU.mult, ALU.add))
            free[b] = outs
            return outs

        def along_columns(col, tiles, dst, after, wait_dst):
            b = bank()
            for i, (c, n) in enumerate(tiles):
                d = V([after, dg_read], nc.vector.tensor_scalar, DG[0:n, i, 0:n], ident[0:n, 0:n], col[0:n, i:i + 1], None, ALU.mult)
                tok = mm(banks[b][:, c:c + n], ones[0:n, :], DG[0:n, i, 0:n], True, True, d, free[b])
            dg_read.append(tok)
            lo = min(c for c, _ in tiles)
            free[b] = AC([tok, wait_dst], nc.scalar.activation, dst[:, lo:T], banks[b][:, lo:T], ACT.Copy)
            return free[b]

        dg_read = []

        def rms_input(gname, layer, after, xwait):
            xt, sq = [], []
            for kt in range(KD):
                g = small(gname, layer * 8 + kt)
                r = RES[:, kt, M:T]
                h = AC([after[kt], xwait], nc.scalar.activation, XH[:, kt, M:T], r, ACT.Copy, scale=g)
                l = V([h], nc.vector.scalar_tensor_tensor, XL[:, kt, M:T], r, g, XH[:, kt, M:T].bitcast(F32), ALU.mult, ALU.subtract)
                xt.append([h, l])
                sq.append(G([after[kt], xwait], nc.gpsimd.tensor_tensor, SQ[:, kt, M:T], r, r, ALU.mult))
            return xt, sq

        res_t = dma(RES[:, :, M:T], x_d, "s_x")
        after_s = dma(SM[:, :], small_d, "s_s")
        after_c = dma(CS[:, :], const_d, "s_c")
        first = ExitStack()
        LOOK = sb("look", [33, 6 * JB], F32, first)
        base = [after_c, after_s]
        for q in (PE, AC, V, G):
            q(base, None)
        for _ in range(NW):
            split_unit()
        dw_all = SM[:, OFF["dw"]:OFF["dw"] + 248]
        prep = [V(base, nc.vector.tensor_scalar, small("gains", 2 * l), small("gains", 2 * l), SCALE, None, ALU.mult) for l in range(2)]
        prep.append(V(base, nc.vector.tensor_scalar, dw_all, dw_all, 0.5, None, ALU.mult))
        lt = [side_dma(T1[:, :], tab1_d, "s_t1"), side_dma(T2[:, :], tab2_d, "s_t2"), side_dma(LOOK[:, :], look_d, "s_lk")]
        meta_t = side_dma(RES[:, :, 0:M], meta_d, "s_m")

        bias_t = []
        bufs = [sb(f"bb{i}", [16, JB], F32, first) for i in range(6)]

        def prepare_bias():
            for i, (tab, c0, n, row) in enumerate([(T1, 0, 8, 0), (T1, 8, 8, 8), (T1, 16, 8, 16), (T1, 0, 16, 24),
                                                   (T2, 0, 8, 40), (T2, 0, 8, 48)]):
                b = bank()
                tok = mm(banks[b][0:n, 0:JB], tab[0:33, c0:c0 + n], LOOK[:, i * JB:(i + 1) * JB], True, True, lt, free[b])
                buf = bufs[i]
                free[b] = AC([tok], nc.scalar.activation, buf[0:n, :], banks[b][0:n, 0:JB], ACT.Copy)
                bias_t.append(side_dma(bias_d[row:row + n, :], buf[0:n, :], f"s_bw{i}", free[b]))

        first.close()

        def toeplitz(dst, row, heads, at, n, rows, name, *after):
            src = bass.AP(bias_d.tensor, row * JB + at - (rows - 1), [[1, rows], [JB, heads], [1, n]])
            return side_dma(dst, src, name, after)

        def attention(jobs, st, NKmax, NCH, tag):
            
            L = [sb(f"L{tag}{i}", [P, NKmax], F32, st) for i in range(2)]
            PT = [sb(f"PT{tag}{i}", [P, NCH, P], F32, st) for i in range(2)]
            z = sb(f"z{tag}", [P, 2, 8], F32, st)
            lread, ptread, zread = [None, None], [None, None], [None, None]
            keep = {}
            outs = []

            def front(i, j):
                k = i % 2
                nq, nk = j["nq"], j["nk"]
                groups, col = [], 512
                for lhs, rhs, bias, o in j["segs"]:
                    w = rhs.shape[1]
                    if col + w > 512:
                        groups.append([bank(), o, 0, None])
                        col = 0
                    b = groups[-1][0]
                    src = banks[b][0:nq, col:col + w]
                    mm(src, lhs, rhs, True, False, free[b], j["after"])
                    groups[-1][3] = mm(src, flip[0:nq, P - nq:P], bias, False, True)
                    col += w
                    groups[-1][2] = col
                nm, r, ri = z[0:nq, k, 0:1], z[0:nq, k, 3:4], z[0:nq, k, 4:5]
                parts = []
                one = len(groups) == 1 and j["sink"] is None
                for n, (b, o, w, tok) in enumerate(groups):
                    parts.append(V([tok, zread[k]], nc.vector.tensor_reduce, nm if one else z[0:nq, k, 1 + n:2 + n],
                                   banks[b][0:nq, 0:w], AX, ALU.max, negate=True))
                t = parts
                if not one:
                    other = j["sink"] if j["sink"] is not None else z[0:nq, k, 2:3]
                    t = V(parts, nc.vector.tensor_tensor, nm, z[0:nq, k, 1:2], other, ALU.min)
                xs = []
                for n, (b, o, w, _) in enumerate(groups):
                    x = AC([t, lread[k]], nc.scalar.activation, L[k][0:nq, o:o + w], banks[b][0:nq, 0:w], ACT.Exp, bias=nm,
                           accum_out=r if one else z[0:nq, k, 5 + n:6 + n])
                    free[b] = x
                    xs.append(x)
                y = xs
                if j["sink"] is not None:
                    y = [xs, AC([t], nc.scalar.activation, z[0:nq, k, 6:7], j["sink"], ACT.Exp, bias=nm, scale=-1.0)]
                if not one:
                    y = V([y], nc.vector.tensor_tensor, r, z[0:nq, k, 5:6], z[0:nq, k, 6:7], ALU.add)
                y = V([y], nc.vector.reciprocal, ri, r)
                keep[i] = (xs, y)

            def turn_over(i, j):
                k = i % 2
                nq, ch = j["nq"], j["chunks"]
                x, y = keep[i]
                pt = []
                n0 = 0
                while n0 < len(ch):
                    wide = ch[n0][1]
                    n1 = n0
                    while n1 < len(ch) and n1 < n0 + 4 and ch[n1][1] == wide:
                        n1 += 1
                    b = bank()
                    for c in range(n0, n1):
                        tok = PE([x, free[b]], nc.tensor.transpose, banks[b][0:wide, (c - n0) * P:(c - n0) * P + nq],
                                 L[k][0:nq, ch[c][0]:ch[c][0] + wide], ident[0:nq, 0:nq])
                    n = n1 - n0
                    if nq == P:
                        dst, src = PT[k][0:wide, n0:n1, :].rearrange("p a b -> p (a b)"), banks[b][0:wide, 0:n * P]
                    else:
                        dst, src = PT[k][0:wide, n0, 0:nq], banks[b][0:wide, 0:nq]
                        assert n == 1
                    free[b] = AC([tok, ptread[k]], nc.scalar.activation, dst, src, ACT.Copy)
                    pt.append(free[b])
                    n0 = n1
                lread[k] = tok
                keep[i] = (pt, y)

            def values(i, j):
                k = i % 2
                nq, ch = j["nq"], j["chunks"]
                pt, y = keep.pop(i)
                b = bank()
                for c, (_, wide, vap) in enumerate(ch):
                    tok = mm(banks[b][0:nq, 0:64], PT[k][0:wide, c, 0:nq], vap, c == 0, c == len(ch) - 1, pt, free[b], j["vafter"])
                ptread[k] = tok
                free[b] = AC([tok, y], nc.scalar.activation, j["out"], banks[b][0:nq, 0:64], ACT.Copy, scale=z[0:nq, k, 4:5])
                zread[k] = free[b]
                outs.append(free[b])

            def step(i):
                if i >= 2:
                    values(i - 2, jobs[i - 2])
                if 1 <= i <= len(jobs):
                    turn_over(i - 1, jobs[i - 1])
                if i < len(jobs):
                    front(i, jobs[i])

            return step, outs

        def to_features(O, NT, tiles, n, after, xwait, kt0=0):
            xt = []
            for nt in range(NT):
                b = bank()
                for i, (c, w) in enumerate(tiles):
                    tok = PE([after, free[b]], nc.tensor.transpose, banks[b][:, c:c + w], O[0:w, i, nt * P:(nt + 1) * P], ident[0:w, 0:w])
                lo = min(c for c, _ in tiles)
                h = AC([tok, xwait], nc.scalar.activation, XH[:, kt0 + nt, lo:T], banks[b][:, lo:T], ACT.Copy)
                l = V([h], nc.vector.tensor_tensor, XL[:, kt0 + nt, lo:T], banks[b][:, lo:T], XH[:, kt0 + nt, lo:T].bitcast(F32), ALU.subtract)
                free[b] = [l]
                xt.append([h, l])
            return xt

        xh_f = lambda kt: XH[:, kt, M:T]
        xl_f = lambda kt: XL[:, kt, M:T]
        xh_t = lambda kt, tt: XH[:, kt, M + tt * P:M + (tt + 1) * P]
        xl_t = lambda kt, tt: XL[:, kt, M + tt * P:M + (tt + 1) * P]

        def last(q):
            return q.ops[-1][-1]

        def everyone():
            return [last(q) for q in (PE, AC, V, G) if q.ops]

        res_after = [res_t] * KD

        def mixer(layer, NGR, HG, row0):
            nonlocal res_after
            st = ExitStack()
            nh = NGR * 8
            BT = sb(f"BT{layer}", [P, nh, S], F32, st)
            bt = []
            QT = sb(f"QT{layer}", [P, 2, NGR * 4, S], F32, st)
            VT = sb(f"VT{layer}", [P, 2, NGR, 512], F32, st)
            O = sb(f"O{layer}", [P, 2, HG * 64], F32, st)
            NK, NCH = (768, 6) if layer == 0 else (256, 2)
            jobs, ready = [], []
            step, outs = attention(jobs, st, NK, NCH, f"m{layer}")
            xt, sq = rms_input("nmix", layer, res_after, phase_end)
            stt = st6[:, 0, 0:2]
            rst = st6[:, 1, 0:2]
            rstd = []
            ssq, rr, rtmp = st6[:, 3, :], st6[:, 4, :], st6[:, 5, :]
            flat = lambda b: b[:, :, :].rearrange("p a b -> p (a b)")
            raw = [flat(XC)[:, i * 256:(i + 1) * 256] for i in range(8)]
            sqr = [flat(SQ)[:, i * 256:(i + 1) * 256] for i in range(8)]
            rawread, sqread = [None] * 8, [None] * 8
            ssread = [None, None]
            sums, pend = [], []
            done = [0]

            def evac(kind, g, half, tt, ps, tok, turn):
                if kind == 2:
                    t = AC([tok, rstd, bt], nc.scalar.activation, VT[:, tt, g, half * 256:(half + 1) * 256], ps, ACT.Copy,
                           scale=rst[:, tt:tt + 1])
                    ready.append(t)
                    return t
                i = turn * 4 + kind * 2 + tt
                a = AC([tok, rstd, rawread[i]], nc.scalar.activation, raw[i], ps, ACT.Copy, scale=rst[:, tt:tt + 1])
                q = G([a, sqread[i], rstd], nc.gpsimd.tensor_tensor, sqr[i], raw[i], raw[i], ALU.mult)
                so = turn * 16 + kind * 8 + tt * 4
                r = V([q, ssread[turn]], nc.vector.reduce_sum, ssq[:, so:so + 4], sqr[i].rearrange("p (h d) -> p h d", h=4), AX)
                sqread[i] = r
                sums.append(r)
                return a

            def head_norms(g, half, turn):
                o = turn * 16
                t = V([sums], nc.vector.tensor_scalar, ssq[:, o:o + 16], ssq[:, o:o + 16], 1.0 / 64, EPS, ALU.mult, ALU.add)
                t = rsqrt(ssq[:, o:o + 16], rr[:, o:o + 16], rtmp[:, o:o + 16], t)
                sums.clear()
                ns = []
                for kind in range(2):
                    for tt in range(2):
                        i = turn * 4 + kind * 2 + tt
                        v = raw[i].rearrange("p (h d) -> p h d", h=4)
                        rb = rr[:, o + kind * 8 + tt * 4:o + kind * 8 + tt * 4 + 4].unsqueeze(2).to_broadcast([P, 4, 64])
                        n = V([t], nc.vector.tensor_tensor, v, v, rb, ALU.mult)
                        ns.append(n)
                        pend.append((kind, g, half, tt, i, n))
                ssread[turn] = ns

            def transposes():
                while pend:
                    kind, g, half, tt, i, n = pend.pop(0)
                    b = bank()
                    for c in range(2):
                        tok = PE([n, free[b]], nc.tensor.transpose, banks[b][:, c * P:(c + 1) * P], raw[i][:, c * P:(c + 1) * P], ident)
                    rawread[i] = tok
                    p0 = g * 4 + half * 2
                    free[b] = AC([tok, bt, prep], nc.scalar.activation, QT[:, kind, p0:p0 + 2, tt * P:(tt + 1) * P],
                                 banks[b][:, 0:256].rearrange("p (c n) -> p c n", c=2), ACT.Copy,
                                 scale=small("gains", 2 * layer + kind))
                    ready.append(free[b])

            def make_jobs(hq):
                after = [list(ready), bt]
                for hh in range(4 * hq, 4 * hq + 4):
                    lst = [(g, hh) for g in range(3)] if layer == 0 else [(hh // 8, hh % 8)]
                    for tt in range(2):
                        nk = P * (tt + 1)
                        segs, chunks = [], []
                        for si, (g, h) in enumerate(lst):
                            po, pr = 64 * (h % 2), g * 4 + h // 2
                            segs.append((QT[po:po + 64, 0, pr, tt * P:(tt + 1) * P], QT[po:po + 64, 1, pr, 0:nk],
                                         BT[:, g * 8 + h, S - nk:S], si * nk))
                            for c in range(tt + 1):
                                chunks.append((si * nk + c * P, P, VT[:, c, g, h * 64:(h + 1) * 64]))
                        jobs.append(dict(nq=P, nk=nk * len(lst), segs=segs, chunks=chunks, sink=None,
                                         out=O[:, tt, hh * 64:(hh + 1) * 64], after=after, vafter=after))

            def advance(n):
                for _ in range(n):
                    if done[0] < len(jobs):
                        step(done[0])
                        done[0] += 1

            if layer == 0:
                groups = [(half, g, half) for half in range(2) for g in range(3)]
            else:
                groups = [(hq, hq // 2, hq % 2) for hq in range(4)]
            rate = 1 if layer == 0 else 3
            for gi, (hq, g, half) in enumerate(groups):
                for kind in range(3):
                    bs = [bank(), bank()]
                    toks = [None, None]
                    for kt in range(KD):
                        wh, wl, wt = tile_of(2)
                        start_, lastk = kt == 0, kt == KD - 1
                        for tt in range(2):
                            out = banks[bs[tt]][:, 0:256]
                            mm(out, xh_t(kt, tt), wh, start_, False, wt, free[bs[tt]], xt[kt])
                            mm(out, xl_t(kt, tt), wh, False, False)
                            toks[tt] = mm(out, xh_t(kt, tt), wl, False, lastk)
                        tile_done(toks[1])
                    if gi == 0 and kind == 0:
                        t = token_sums(SQ, KD, tiles1, stt, sq, 1.0 / D, EPS)
                        rstd.append(rsqrt(stt, rst, st6[:, 2, 0:2], t))
                    transposes()
                    for tt in range(2):
                        free[bs[tt]] = evac(kind, g, half, tt, banks[bs[tt]][:, 0:256], toks[tt], gi % 2)
                    if gi == 0 and kind == 0:
                        if layer == 0:
                            prepare_bias()
                            for g3 in range(3):
                                bt.append(toeplitz(BT[:, g3 * 8:(g3 + 1) * 8, :], row0 + g3 * 8, 8, 127, S, P, f"s_bt{layer}{g3}", bias_t))
                        else:
                            bt.append(toeplitz(BT[:, :, :], row0, 16, 127, S, P, f"s_bt{layer}", bias_t, phase_end))
                    if kind == 1:
                        head_norms(g, half, gi % 2)
                    advance(rate)
                if layer == 1 or g == 2:
                    make_jobs(hq)
            last_jobs = len(jobs)
            while done[0] < last_jobs + 2:
                step(done[0])
                done[0] += 1
            ot = to_features(O, HG // 2, tiles1, S, outs, None)
            new = []

            def evac_o(nt, ps, tok):
                t = V([tok], nc.vector.tensor_tensor, RES[:, nt, M:T], RES[:, nt, M:T], ps, ALU.add)
                new.append(t)
                return t

            gemm(HG // 2, KD, xh_f, xl_f, lambda kt: ot[kt], S, evac_o)
            res_after = new
            st.close()

        def ffn1(layer):
            nonlocal res_after
            st = ExitStack()
            HH = sb(f"HH{layer}", [P, 32, S], F32R, st)
            HL = sb(f"HL{layer}", [P, 32, S], F32R, st)
            NR = 3
            tmp = [sb(f"ft{layer}{i}", [P, S], F32, st) for i in range(NR)]
            tm2 = [sb(f"fu{layer}{i}", [P, S], F32, st) for i in range(NR)]
            pend = everyone()
            xt, sq = rms_input("nffn", layer, res_after, pend)
            ht = []
            tr, sr = [None] * NR, [None] * NR

            def evac_h(nt, ps, tok):
                i = nt % NR
                a = AC([tok, tr[i], pend], nc.scalar.activation, tmp[i][:, :], ps, ACT.Relu)
                h = AC([a], nc.scalar.activation, HH[:, nt, :], tmp[i][:, :], ACT.Square)
                s = G([a, sr[i]], nc.gpsimd.tensor_tensor, tm2[i][:, :], tmp[i][:, :], tmp[i][:, :], ALU.mult)
                l = V([s, h], nc.vector.tensor_tensor, HL[:, nt, :], tm2[i][:, :], HH[:, nt, :].bitcast(F32), ALU.subtract)
                tr[i] = [h, s]
                sr[i] = l
                ht.append([h, l])
                return a

            gemm(KD, 32, xh_f, xl_f, lambda kt: xt[kt], S, evac_h)
            t = token_sums(SQ, KD, tiles1, st6[:, 0, 0:2], sq, 1.0 / D, EPS)
            t = V([t], nc.vector.reciprocal, st6[:, 1, 0:2], st6[:, 0, 0:2])
            bc = along_columns(st6[:, 1, 0:2], tiles1, BC, t, None)
            new = []

            def evac_y(nt, ps, tok):
                t = V([tok, bc, res_xc], nc.vector.tensor_tensor, XC[:, nt, M:T], ps, BC[:, M:T], ALU.mult)
                new.append(V([t], nc.vector.tensor_tensor, RES[:, nt, M:T], RES[:, nt, M:T], XC[:, nt, M:T], ALU.add))
                return t

            res_xc = None
            gemm(32, KD, lambda kt: HH[:, kt, :], lambda kt: HL[:, kt, :], lambda kt: ht[kt], S, evac_y)
            res_after = new
            st.close()

        phase_end = None
        mixer(0, 3, 8, 0)
        if upto >= 2:
            ffn1(0)
        if upto >= 3:
            phase_end = everyone()
            mixer(1, 2, 16, 24)
        if upto >= 4:
            ffn1(1)

        def layer_norm(X, kts, gname, bname, li, eps, after, wait, post):
            b = bank()
            for kt in range(kts):
                tok = mm(banks[b][:, 0:T], ones, X[:, kt, 0:T], kt == 0, kt == kts - 1, after[kt], free[b])
            mu = AC([tok, wait], nc.scalar.activation, BC[:, :], banks[b][:, 0:T], ACT.Copy, scale=1.0 / (kts * P))
            free[b] = mu
            sq, xc = [], []
            for kt in range(kts):
                c = V([mu, wait, after[kt]], nc.vector.tensor_tensor, XC[:, kt, :], X[:, kt, 0:T], BC[:, :], ALU.subtract)
                xc.append(c)
                sq.append(AC([c, wait], nc.scalar.activation, SQ[:, kt, :], XC[:, kt, :], ACT.Square))
            t = token_sums(SQ, kts, tiles2, st6[:, 0, 0:3], sq, 1.0 / (kts * P), eps)
            pe_sq = last(PE)
            t = rsqrt(st6[:, 0, 0:3], st6[:, 1, 0:3], st6[:, 2, 0:3], [t, st_init])
            bc = along_columns(st6[:, 1, 0:3], tiles2, BC, t, xc)
            out = []
            for kt in range(kts):
                y = V([bc, pe_sq], nc.vector.scalar_tensor_tensor, SQ[:, kt, :], XC[:, kt, :], small(gname, li * kts + kt), BC[:, :], ALU.mult, ALU.mult)
                out.append(post(kt, SQ[:, kt, :], small(bname, li * kts + kt), y))
            return out

        st_init = V([everyone()], nc.vector.memset, st6[:, 0:2, 0:8], 1.0)

        def split_norm(X, wait):
            def post(kt, y, bias, tok):
                h = AC([tok, wait], nc.scalar.activation, XH[:, kt, :], y, ACT.Identity, bias=bias)
                l = V([h], nc.vector.scalar_tensor_tensor, XL[:, kt, :], y, bias, XH[:, kt, :].bitcast(F32), ALU.add, ALU.subtract)
                r = G([tok], nc.gpsimd.tensor_scalar, X[:, kt, :], y, bias, None, ALU.add)
                return [r, h, l]
            return post

        res_after = [[t, meta_t] for t in res_after]
        xt = None
        if upto >= 5:
            pend = everyone()
            xt = layer_norm(RES, KD, "embg", "embb", 0, LN_EPS, res_after, pend, split_norm(RES, pend))
        xh_a = lambda kt: XH[:, kt, :]
        xl_a = lambda kt: XL[:, kt, :]

        def mix_layer(li, xt):
            st = ExitStack()
            pend = everyone()
            BW = sb(f"BW{li}", [P, 8, S], F32, st)
            BM = sb(f"BM{li}", [P, 3, 8, M], F32, st)
            bt = [toeplitz(BW[:, :, :], 40, 8, 127, S, P, f"s_bw2{li}", bias_t, pend),
                  toeplitz(BM[:, 0, :, :], 48, 8, 271 - 16, M, P, f"s_bm0{li}", bias_t, pend),
                  toeplitz(BM[:, 1, :, :], 48, 8, 271 - 144, M, P, f"s_bm1{li}", bias_t, pend),
                  toeplitz(BM[0:M, 2, :, :], 48, 8, 271, M, M, f"s_bm2{li}", bias_t, pend)]
            QT = sb(f"Q2{li}", [P, 4, T], F32, st)
            KT = sb(f"K2{li}", [P, T], F32, st)
            VF = sb(f"VF{li}", [P, T], F32, st)
            V2 = sb(f"V2{li}", [P, 3, P], F32, st)
            HC = sb(f"HC{li}", [P, 4, 30 + T], F32, st)
            AC4 = sb(f"CA{li}", [P, 4, T], F32, st)
            SG = sb(f"SG{li}", [P, 2, KD, T], F32, st)
            MH = sb(f"MH{li}", [P, KD, T], F32R, st)
            ML = sb(f"ML{li}", [P, KD, T], F32R, st)
            O = sb(f"O2{li}", [P, 3, 512], F32, st)
            nsink = sb(f"ns{li}", [P, 8], F32, st)
            nst = V([pend], nc.vector.tensor_scalar, nsink[:, :], small("sinks", li * 8, 8), -1.0, None, ALU.mult)
            zt = G([pend], nc.gpsimd.memset, HC[:, :, 0:30], 0.0)
            qk, vt, sgt = [], [], {}

            tg = [None] * 4

            def evac(nt, ps, tok):
                if nt < 8:
                    c = nt // 2
                    if nt % 2 == 0:
                        tg[c] = AC([tok, pend], nc.scalar.activation, HC[:, c, 30:30 + T], ps, ACT.Tanh, scale=0.5)
                        return tg[c]
                    hc[c] = V([tok, tg[c], zt], nc.vector.scalar_tensor_tensor, HC[:, c, 30:30 + T], HC[:, c, 30:30 + T], 1.0, ps,
                              ALU.add, ALU.mult)
                    return hc[c]
                if nt < 12:
                    t = AC([tok, pend], nc.scalar.activation, QT[:, nt - 8, :], ps, ACT.Copy, scale=SCALE)
                    qk.append(t)
                elif nt == 12:
                    t = AC([tok, pend], nc.scalar.activation, KT[:, :], ps, ACT.Copy)
                    qk.append(t)
                elif nt == 13:
                    t = AC([tok, pend], nc.scalar.activation, VF[:, :], ps, ACT.Copy)
                    vt.append(t)
                else:
                    w, c = divmod(nt - 14, 8)
                    t = AC([tok, pend], nc.scalar.activation, SG[:, w, c, :], ps, ACT.Tanh, scale=0.5)
                    sgt[(w, c)] = t
                return t

            acc, taps = [None] * 4, [0] * 4
            NPR = 4
            PR = SQ[:, :, :].rearrange("p (c i) t -> p c i t", c=2)
            prr = [[None] * NPR, [None] * NPR]

            def tap(c):
                k = taps[c]
                if k == 31:
                    return
                taps[c] += 1
                w = small("dw", (li * 4 + c) * 31 + k)
                src = HC[:, c, k:k + T]
                cb = small("cb", li * 4 + c)
                if c < VC:
                    if k == 0:
                        acc[c] = V([hc[c], pend, prep], nc.vector.tensor_scalar, AC4[:, c, :], src, w, cb, ALU.mult, ALU.add)
                    else:
                        acc[c] = V([acc[c]], nc.vector.scalar_tensor_tensor, AC4[:, c, :], src, w, AC4[:, c, :], ALU.mult, ALU.add)
                elif k == 0:
                    acc[c] = AC([hc[c], pend, prep], nc.scalar.activation, AC4[:, c, :], src, ACT.Identity, scale=w, bias=cb)
                else:
                    i = k % NPR
                    a = AC([hc[c], pend, prr[c - VC][i]], nc.scalar.activation, PR[:, c - VC, i, :], src, ACT.Copy, scale=w)
                    acc[c] = G([a, acc[c]], nc.gpsimd.tensor_tensor, AC4[:, c, :], AC4[:, c, :], PR[:, c - VC, i, :], ALU.add)
                    prr[c - VC][i] = acc[c]

            VC = 3
            hc = [None] * 4
            jobs = []
            step, outs = attention(jobs, st, T, 3, f"b{li}")
            done = [0]

            def make_jobs():
                b = bank()
                for i, (c, w) in enumerate(tiles2):
                    tok = PE([vt, free[b]], nc.tensor.transpose, banks[b][0:w, i * P:(i + 1) * P], VF[:, c:c + w], ident)
                v1 = AC([tok, pend], nc.scalar.activation, V2[:, 0:2, :].rearrange("p a b -> p (a b)"), banks[b][:, 0:2 * P], ACT.Copy)
                v2 = AC([tok, pend], nc.scalar.activation, V2[0:M, 2, :], banks[b][0:M, 2 * P:3 * P], ACT.Copy)
                free[b] = [v1, v2]
                for h in range(8):
                    po, pr = 64 * (h // 4), h % 4
                    vh = slice(64 * (h // 4), 64 * (h // 4) + 64)
                    for tt, (c0, nq) in ((2, tiles2[2]), (0, tiles2[0]), (1, tiles2[1])):
                        q = QT[po:po + 64, pr, c0:c0 + nq]
                        segs = [(q, KT[po:po + 64, 0:M], BM[0:nq, tt, h, :], 0)]
                        chunks = [(0, M, V2[0:M, 2, vh])]
                        nk = M
                        if tt < 2:
                            w = P * (tt + 1)
                            segs.append((q, KT[po:po + 64, M:M + w], BW[:, h, S - w:S], M))
                            chunks += [(M + c * P, P, V2[:, c, vh]) for c in range(tt + 1)]
                            nk += w
                        jobs.append(dict(nq=nq, nk=nk, segs=segs, chunks=chunks, sink=nsink[0:nq, h:h + 1],
                                         out=O[0:nq, tt, h * 64:(h + 1) * 64], after=[qk, bt, nst], vafter=[v1, v2]))

            def pump(nt):
                for c in range(4):
                    if hc[c] is not None:
                        for _ in range(2):
                            tap(c)
                if nt == 14:
                    make_jobs()
                if nt >= 14:
                    for _ in range(2):
                        if done[0] < len(jobs) + 2:
                            step(done[0])
                            done[0] += 1

            gemm(KD, 30, xh_a, xl_a, lambda kt: xt[kt], T, evac, pump)
            xdone = last(PE)
            while min(taps) < 31:
                for c in range(4):
                    tap(c)
            while done[0] < len(jobs) + 2:
                step(done[0])
                done[0] += 1
            ot = to_features(O, 4, tiles2, T, outs, xdone)

            def post(kt, y, bias, tok):
                r = AC([tok], nc.scalar.activation, XC[:, kt, :], y, ACT.Silu, bias=bias)
                h = AC([r, xdone], nc.scalar.activation, XH[:, 4 + kt, :], XC[:, kt, :], ACT.Copy)
                l = V([h], nc.vector.tensor_tensor, XL[:, 4 + kt, :], XC[:, kt, :], XH[:, 4 + kt, :].bitcast(F32), ALU.subtract)
                return [h, l]

            ct = layer_norm(AC4, 4, "clg", "clb", li, LN_EPS, acc, None, post)
            mt = []

            def evac_a(nt, ps, tok):
                sgt[(0, nt)] = V([tok, sgt[(0, nt)]], nc.vector.scalar_tensor_tensor, SG[:, 0, nt, :], SG[:, 0, nt, :], 1.0, ps,
                                 ALU.add, ALU.mult)
                return sgt[(0, nt)]

            gemm(4, KD, xh_a, xl_a, lambda kt: ot[kt], T, evac_a)

            def evac_c(nt, ps, tok):
                t = V([tok, sgt[(1, nt)]], nc.vector.scalar_tensor_tensor, SG[:, 1, nt, :], SG[:, 1, nt, :], 1.0, ps, ALU.add, ALU.mult)
                m = V([t, sgt[(0, nt)]], nc.vector.tensor_tensor, SG[:, 0, nt, :], SG[:, 0, nt, :], SG[:, 1, nt, :], ALU.add)
                h = AC([m, pend], nc.scalar.activation, MH[:, nt, :], SG[:, 0, nt, :], ACT.Copy, scale=0.5)
                l = V([h], nc.vector.scalar_tensor_tensor, ML[:, nt, :], SG[:, 0, nt, :], 0.5, MH[:, nt, :].bitcast(F32),
                      ALU.mult, ALU.subtract)
                mt.append([h, l])
                return t

            gemm(4, KD, lambda kt: XH[:, 4 + kt, :], lambda kt: XL[:, 4 + kt, :], lambda kt: ct[kt], T, evac_c)
            new = []

            def evac_o(nt, ps, tok):
                t = V([tok, xt[nt]], nc.vector.scalar_tensor_tensor, RES[:, nt, :], RES[:, nt, :], ALPHA, ps, ALU.mult, ALU.add)
                new.append(t)
                return t

            gemm(KD, KD, lambda kt: MH[:, kt, :], lambda kt: ML[:, kt, :], lambda kt: mt[kt], T, evac_o)
            st.close()
            pend = everyone()
            return layer_norm(RES, KD, "ln1g", "ln1b", li, LN_EPS, new, pend, split_norm(RES, pend))

        def swiglu_hidden(NT, lo, xt, HH, HL, tmp, tm2, pend, ht, rd):
            n = T - lo

            def evac(i, ps, tok):
                nt, up = divmod(i, 2)
                k = nt % len(tmp)
                if not up:
                    t = AC([tok, rd[k], pend], nc.scalar.activation, tmp[k][:, 0:n], ps, ACT.Silu)
                    rd[k] = [t]
                    return t
                t = V([tok, rd[k]], nc.vector.tensor_tensor, tm2[k][:, 0:n], tmp[k][:, 0:n], ps, ALU.mult)
                h = AC([t, pend], nc.scalar.activation, HH[:, nt, 0:n], tm2[k][:, 0:n], ACT.Copy)
                l = V([h], nc.vector.tensor_tensor, HL[:, nt, 0:n], tm2[k][:, 0:n], HH[:, nt, 0:n].bitcast(F32), ALU.subtract)
                ht.append([h, l])
                rd[k] = [h, l]
                return t

            gemm(KD, 2 * NT, lambda kt: XH[:, kt, lo:T], lambda kt: XL[:, kt, lo:T], lambda kt: xt[kt], n, evac)

        def dense(xt):
            st = ExitStack()
            HH = sb("DHH", [P, 22, T], F32R, st)
            HL = sb("DHL", [P, 22, T], F32R, st)
            tmp = [sb(f"dt{i}", [P, T], F32, st) for i in range(3)]
            tm2 = [sb(f"du{i}", [P, T], F32, st) for i in range(3)]
            ht, new = [], []
            swiglu_hidden(22, 0, xt, HH, HL, tmp, tm2, xt, ht, [None] * 3)

            def evac(nt, ps, tok):
                t = V([tok, xt[nt]], nc.vector.scalar_tensor_tensor, RES[:, nt, :], RES[:, nt, :], ALPHA, ps, ALU.mult, ALU.add)
                new.append(t)
                return t

            gemm(22, KD, lambda kt: HH[:, kt, :], lambda kt: HL[:, kt, :], lambda kt: ht[kt], T, evac)
            st.close()
            pend = everyone()
            return layer_norm(RES, KD, "ln2g", "ln2b", 0, LN_EPS, new, pend, split_norm(RES, pend))

        def moe(xt):
            st = ExitStack()
            HH = [sb(f"EHH{i}", [P, 11, S], F32R, st) for i in range(2)]
            HL = [sb(f"EHL{i}", [P, 11, S], F32R, st) for i in range(2)]
            tmp = [sb(f"et{i}", [P, S], F32, st) for i in range(3)]
            tm2 = [sb(f"eu{i}", [P, S], F32, st) for i in range(3)]
            CB = sb("CB", [P, 2, S], F32, st)
            C8 = sb("C8", [P, 8, 2, 8], F32, st)
            b = bank()
            for tt in range(2):
                for kt in range(KD):
                    tok = mm(banks[b][:, tt * 8:tt * 8 + 8], RES[:, kt, M + tt * P:M + (tt + 1) * P], small("router", kt * 8, 8),
                             kt == 0, kt == KD - 1, xt, free[b])
            lg, e1, e2, q1, q2, cm = (C8[:, i, :, :] for i in range(6))
            s1 = C8[:, 6, :, :]
            s2 = C8[:, 7, :, :]
            io = iota.unsqueeze(1).to_broadcast([P, 2, 8])
            t = V([tok, xt], nc.vector.tensor_copy, lg, banks[b][:, 0:16].rearrange("p (a b) -> p a b", a=2))
            free[b] = t

            def pick(src, val, onehot, t):
                bc = lambda a: a.to_broadcast([P, 2, 8])
                t = V([t], nc.vector.tensor_reduce, val, src, AX, ALU.max)
                t = V([t], nc.vector.tensor_tensor, q1, src, bc(val), ALU.is_lt)
                t = V([t], nc.vector.scalar_tensor_tensor, q1, q1, 100.0, io, ALU.mult, ALU.add)
                t = V([t], nc.vector.tensor_reduce, s2[:, :, 0:1], q1, AX, ALU.min)
                return V([t], nc.vector.tensor_tensor, onehot, io, bc(s2[:, :, 0:1]), ALU.is_equal)

            v1, v2, g1, g2, den = (s1[:, :, i:i + 1] for i in range(5))
            t = pick(lg, v1, e1, t)
            t = V([t], nc.vector.scalar_tensor_tensor, q2, e1, -3.0e38, lg, ALU.mult, ALU.add)
            t = pick(q2, v2, e2, t)
            t = V([t], nc.vector.tensor_tensor, den, v2, v1, ALU.subtract)
            t = AC([t], nc.scalar.activation, g2, den, ACT.Exp)
            t = V([t], nc.vector.tensor_scalar, den, g2, 1.0, None, ALU.add)
            t = V([t], nc.vector.reciprocal, g1, den)
            t = V([t], nc.vector.tensor_tensor, g2, g2, g1, ALU.mult)
            t = V([t], nc.vector.tensor_tensor, e1, e1, g1.to_broadcast([P, 2, 8]), ALU.mult)
            t = V([t], nc.vector.tensor_tensor, e2, e2, g2.to_broadcast([P, 2, 8]), ALU.mult)
            comb = V([t], nc.vector.tensor_tensor, cm, e1, e2, ALU.add)

            acc = [V([xt[kt], tok], nc.vector.tensor_scalar, RES[:, kt, M:T], RES[:, kt, M:T], ALPHA, None, ALU.mult)
                   for kt in range(KD)]
            hread = [None, None]
            cread = [None, None]
            rd = [None] * 3
            for x in range(8):
                k = x % 2
                ht = []
                b = bank()
                for tt in range(2):
                    d = V([comb, dg_read], nc.vector.tensor_scalar, DG[:, tt, :], ident, cm[:, tt, x:x + 1], None, ALU.mult)
                    tok = mm(banks[b][:, tt * P:(tt + 1) * P], ones, DG[:, tt, :], True, True, d, free[b])
                dg_read.append(tok)
                cb = AC([tok, cread[k], xt], nc.scalar.activation, CB[:, k, :], banks[b][:, 0:S], ACT.Copy)
                free[b] = cb
                swiglu_hidden(11, M, xt, HH[k], HL[k], tmp, tm2, [xt, hread[k]], ht, rd)
                cr = []

                def evac(nt, ps, tok):
                    t = V([tok, cb, acc[nt], xt], nc.vector.tensor_tensor, XC[:, nt, M:T], ps, CB[:, k, :], ALU.mult)
                    acc[nt] = G([t, acc[nt]], nc.gpsimd.tensor_tensor, RES[:, nt, M:T], RES[:, nt, M:T], XC[:, nt, M:T], ALU.add)
                    cr.append(t)
                    return t

                gemm(11, KD, lambda kt: HH[k][:, kt, :], lambda kt: HL[k][:, kt, :], lambda kt: ht[kt], S, evac)
                hread[k] = last(PE)
                cread[k] = cr
            st.close()
            pend = everyone()
            outs = []

            def post(kt, y, bias, tok):
                r = AC([tok], nc.scalar.activation, RES[:, kt, :], y, ACT.Identity, bias=bias)
                outs.append(r)
                return r

            return layer_norm(RES, KD, "ln2g", "ln2b", 1, LN_EPS, acc, pend, post)

        if upto >= 6:
            xt = mix_layer(0, xt)
        if upto >= 7:
            xt = dense(xt)
        if upto >= 8:
            xt = mix_layer(1, xt)
        if upto >= 9:
            xt = moe(xt)

        end = everyone()
        out_t = dma(out_d, RES[:, :, M:T], "s_out", end, xt, res_after)
        SP([out_t], None)

        for q in (PE, AC, V, G, SP):
            q.count()

        @block.sync
        def _(eng):
            SP.emit(eng)

        @block.gpsimd
        def _(eng):
            G.emit(eng)

        @block.scalar
        def _(eng):
            AC.emit(eng)

        @block.vector
        def _(eng):
            V.emit(eng)

        @block.tensor
        def _(eng):
            PE.emit(eng)


def feature_tiles(w):
    k, n = w.shape
    return w.reshape(k // P, P, n // P, P).transpose(2, 0, 1, 3).reshape(-1, P, P)


def head_tiles(w, groups, order):
    k, n = w.shape
    t = w.reshape(k // P, P, 3, groups, 2, 2, P)
    return np.concatenate([t[:, :, kind, g, half].transpose(0, 2, 1, 3).reshape(-1, P, P)
                           for g, half in order for kind in range(3)])


def paired_tiles(a, b):
    k, n = a.shape
    return np.stack([feature_tiles(a).reshape(n // P, k // P, P, P), feature_tiles(b).reshape(n // P, k // P, P, P)],
                    axis=1).reshape(-1, P, P)


def weight_stream(i):
    parts = [head_tiles(i["a_w_qkv"][0], 3, [(g, h) for h in range(2) for g in range(3)]), feature_tiles(i["a_w_o"][0]),
             feature_tiles(i["ffn_w1"][0]), feature_tiles(i["ffn_w2"][0]),
             head_tiles(i["b_w_qkv"][0], 2, [(g, h) for g in range(2) for h in range(2)]), feature_tiles(i["b_w_o"][0]),
             feature_tiles(i["ffn_w1"][1]), feature_tiles(i["ffn_w2"][1])]
    heads = np.arange(512).reshape(2, 4, 64).transpose(1, 0, 2).reshape(-1)
    for l in range(2):
        w = i["w_in_2"][l]
        parts += [paired_tiles(w[:, 1280:1792], w[:, 768:1280]), feature_tiles(w[:, heads]), feature_tiles(w[:, 512:768]),
                  feature_tiles(w[:, 1792:])]
        parts += [feature_tiles(i["w_attn_proj_2"][l]), feature_tiles(i["w_conv_proj_2"][l]), feature_tiles(i["w_out_2"][l])]
        if l == 0:
            parts += [paired_tiles(i["ffn_w_gate_2"][0], i["ffn_w_up_2"][0]), feature_tiles(i["ffn_w_down_2"][0])]
        else:
            for e in range(8):
                parts += [paired_tiles(i["moe_w_gate_2"][0, e], i["moe_w_up_2"][0, e]), feature_tiles(i["moe_w_down_2"][0, e])]
    w = np.concatenate(parts)
    return np.ascontiguousarray(w.reshape(-1, UT, P, P).transpose(0, 2, 1, 3)).reshape(-1, P, UT * P)


def columns(v):
    return v.reshape(-1, P).T


def small_params(i):
    c = [columns(i["norm_mix"]), columns(i["norm_ffn"]), columns(i["emb_ln_g_2"]), columns(i["emb_ln_b_2"]),
         columns(i["ln1_g_2"]), columns(i["ln1_b_2"]), columns(i["ln2_g_2"]), columns(i["ln2_b_2"]),
         i["conv_dw_2"].reshape(2, 31, 4, P).transpose(3, 0, 2, 1).reshape(P, -1),
         columns(i["conv_b_2"]), columns(i["conv_ln_g_2"]), columns(i["conv_ln_b_2"]),
         np.stack([np.tile(i[n][0], 2) for n in ("a_q_gain", "a_k_gain", "b_q_gain", "b_k_gain")], axis=1),
         np.broadcast_to(i["sinks_2"].reshape(1, -1), (P, 16)),
         i["router_2"][0].reshape(KD, P, 8).transpose(1, 0, 2).reshape(P, -1)]
    return np.ascontiguousarray(np.concatenate(c, axis=1))


def layout(i):
    ident = np.eye(P, dtype=np.float32)
    consts = np.concatenate([ident, np.ones((P, P), np.float32),
                             np.broadcast_to(np.arange(8, dtype=np.float32), (P, 8)), ident[::-1]], axis=1)
    one = np.ones((1, 24), np.float32)
    feat = lambda a: np.ascontiguousarray(a.T.reshape(KD, P, -1).transpose(1, 0, 2))
    return {"w": weight_stream(i), "x": feat(i["x"][0]), "meta": feat(i["meta_tokens_2"]),
            "small": small_params(i), "consts": consts, "look": lookups(),
            "tab1": np.concatenate([i["rel_bias"], one]), "tab2": np.concatenate([i["rel_bias_2"], one[:, :8]])}


def kernel(**inputs):
    import concourse.bacc as _bacc
    from concourse.bass_utils import run_bass_kernel_spmd as _run

    arrays = layout({k: np.asarray(v) for k, v in inputs.items()})
    nc = _bacc.Bacc("TRN2", target_bir_lowering=False, num_devices=1)
    args = [nc.dram_tensor(f"in_{n}", a.shape, F32, kind="ExternalInput").ap() for n, a in arrays.items()]
    out = nc.dram_tensor("out", (P, KD, S), F32, kind="ExternalOutput").ap()
    model_kernel(nc, *args, out)
    r = _run(nc, [{f"in_{n}": np.ascontiguousarray(a) for n, a in arrays.items()}], core_ids=[0])
    y = r.results[0]["out"]
    return np.ascontiguousarray(y.transpose(2, 1, 0).reshape(1, S, D))
```

```python
import math
from contextlib import ExitStack

import numpy as np

import concourse.bass as bass
from concourse import mybir

F32 = mybir.dt.float32
F32R = mybir.dt.float32r
I32 = mybir.dt.int32
ALU = mybir.AluOpType
ACT = mybir.ActivationFunctionType
AX = mybir.AxisListType.X

P = 128
D = 1024
KD = D // P
S = 256
M = 16
T = S + M
NEG = -1e30
EPS = 1e-6
LN_EPS = 1e-5
ALPHA = 4 ** 0.25
SCALE = 64 ** -0.5
UT = 16
MAGIC = float(0x5F3759DF)

SMALL = [("nmix", 16), ("nffn", 16), ("embg", 8), ("embb", 8), ("ln1g", 16), ("ln1b", 16),
         ("ln2g", 16), ("ln2b", 16), ("dw", 2 * 4 * 31), ("cb", 8), ("clg", 8), ("clb", 8),
         ("gains", 4), ("sinks", 16), ("router", 64)]
OFF = {}
_o = 0
for _n, _w in SMALL:
    OFF[_n] = _o
    _o += _w
NSMALL = _o

CONSTS = [("ident", 128), ("ones", 128), ("iota", 128), ("flip", 128), ("upper", 128)]
COFF = {}
_o = 0
for _n, _w in CONSTS:
    COFF[_n] = _o
    _o += _w
NCONST = _o

JB = 384
N_UNITS = 311


def t5_bucket(n, n_buckets, max_distance):
    n = np.maximum(n, 0)
    exact = n_buckets // 2
    nf = np.maximum(n, 1).astype(np.float32)
    large = exact + (np.log(nf / np.float32(exact)) / np.float32(math.log(max_distance / exact))
                     * np.float32(n_buckets - exact)).astype(np.int32)
    return np.where(n < exact, n, np.minimum(large, n_buckets - 1))


def lookup(dists, keep, max_distance):
    b = t5_bucket(dists, 32, max_distance)
    out = np.zeros((33, dists.size), np.float32)
    out[b, np.arange(dists.size)] = 1.0
    out[:, ~keep] = 0.0
    out[32, ~keep] = NEG
    return out


def lookups():
    d = 255 - np.arange(JB)
    a = [lookup(d, (d >= 0) & (d <= 128), 2048), lookup(d, (d >= 0) & (d % 4 == 0), 2048),
         lookup(d, (d >= 0) & (d % 16 == 0), 2048), lookup(d, d >= 0, 2048)]
    w = [lookup(d, (d >= 0) & (d < 128), 128)]
    dm = 271 - np.arange(JB)
    c = [lookup(dm, dm >= 0, 128)]
    return np.concatenate(a + w + c, axis=1)


BRANCH = "branch"


class Tok:
    def __init__(self):
        self.sem, self.value, self.used, self.dma = None, None, False, False


class Queue:

    def __init__(self, sem):
        self.sem, self.ops = sem, []

    def __call__(self, after, method, *args, **kw):
        waits = []
        flatten(after, waits)
        for t in waits:
            t.used = True
        tok = Tok()
        self.ops.append((method, args, kw, waits, tok))
        return tok

    def count(self):
        self.count_ops(self.ops, 0)

    def count_ops(self, ops, n):
        for method, args, _, _, tok in ops:
            if method is BRANCH:
                a, b = (self.count_ops(arm, n) for arm in args[1:])
                n = max(a, b) + 1
                tok.sem, tok.value, tok.fill = self.sem, n, (n - a, n - b)
            elif tok.used and tok.sem is None:
                n += 1
                tok.sem, tok.value = self.sem, n
        return n

    def emit(self, eng, ops=None, seen=None):
        ops, seen = (self.ops, {}) if ops is None else (ops, seen)
        for method, args, kw, waits, tok in ops:
            best = {}
            for t in waits:
                k = id(t.sem)
                if seen.get(k, 0) < t.value and best.get(k, (0, None))[0] < t.value:
                    best[k] = (t.value, t.sem)
            for k, (v, s) in best.items():
                eng.wait_ge(s, v)
                seen[k] = v
            if method is None:
                continue
            if method is BRANCH:
                value = eng.value_load(args[0])
                with eng.If(value <= P):
                    self.emit(eng, args[1], dict(seen))
                    eng.drain().then_inc(self.sem, tok.fill[0])
                with eng.Else():
                    self.emit(eng, args[2], dict(seen))
                    eng.drain().then_inc(self.sem, tok.fill[1])
                continue
            ins = method(*args, **kw)
            if tok.dma:
                ins.then_inc(tok.sem, 16)
            elif tok.used:
                ins.then_inc(tok.sem, 1)


def flatten(x, out):
    if x is None:
        return
    if isinstance(x, Tok):
        out.append(x)
        return
    for y in x:
        flatten(y, out)


def model_kernel(nc, w_d, x_d, meta_d, small_d, const_d, look_d, tab1_d, tab2_d, out_d, upto=99):
    bias_d = nc.dram_tensor("bias_scratch", (56, JB), F32, kind="Internal").ap()

    ctx = ExitStack()
    with ctx:
        def sb(name, shape, dt=F32, st=ctx):
            return st.enter_context(nc.sbuf_tensor(name, shape, dt))

        def sem(name):
            return ctx.enter_context(nc.semaphore(name))

        NS, NW = 4, 3
        stg = [sb(f"stg{i}", [P, UT * P]) for i in range(NS)]
        WH = [sb(f"wh{i}", [P, UT * P], F32R) for i in range(NW)]
        WL = [sb(f"wl{i}", [P, UT * P], F32R) for i in range(NW)]
        RES = sb("res", [P, KD, T])
        XH = sb("xh", [P, KD, T], F32R)
        XL = sb("xl", [P, KD, T], F32R)
        XC = sb("xc", [P, KD, T])
        SQ = sb("sq", [P, KD, T])
        SM = sb("small", [P, NSMALL])
        CS = sb("consts", [P, NCONST])
        st6 = sb("st6", [P, 6, 64])
        DG = sb("dg", [P, 3, P])
        BC = sb("bc", [P, T])
        T1 = sb("tab1", [33, 24])
        T2 = sb("tab2", [33, 8])
        ident = CS[:, COFF["ident"]:COFF["ident"] + P]
        ones = CS[:, COFF["ones"]:COFF["ones"] + P]
        flip = CS[:, COFF["flip"]:COFF["flip"] + P]
        iota = CS[:, COFF["iota"]:COFF["iota"] + P]
        upper = CS[:, COFF["upper"]:COFF["upper"] + P]

        banks = [ctx.enter_context(nc.psum_tensor(f"bank{i}", [P, 512], F32)) for i in range(8)]
        free = [None] * 8
        turn = [0]
        held = set()

        s_pe, s_act, s_dve, s_pool, s_sp = (sem(n) for n in ("s_pe", "s_act", "s_dve", "s_pool", "s_sp"))
        s_wh, s_wl, s_wp = sem("s_wh"), sem("s_wl"), sem("s_wp")
        s_w = [sem(f"s_w{i}") for i in range(NS)]
        PE, AC, V, G, SP = Queue(s_pe), Queue(s_act), Queue(s_dve), Queue(s_pool), Queue(s_sp)
        block = ctx.enter_context(nc.Block())

        def small(name, i, n=1):
            return SM[:, OFF[name] + i:OFF[name] + i + n]

        def start(q, eng, dst, src, s, value, *after):
            tok = q(after, eng.dma_start, dst, src)
            tok.sem, tok.value, tok.dma = s, value, True
            return tok

        def dma(dst, src, name, *after):
            return start(SP, nc.sync, dst, src, sem(name), 16, *after)

        def side_dma(dst, src, name, *after):
            return start(G, nc.gpsimd, dst, src, sem(name), 16, *after)

        def bank():
            while turn[0] % 8 in held:
                turn[0] += 1
            i = turn[0] % 8
            turn[0] += 1
            return i

        load_tok, split_tok, done_tok = [], [], []

        def load_unit():
            u = len(load_tok)
            if u >= N_UNITS:
                return
            after = split_tok[u - NS] if u >= NS else None
            load_tok.append(start(SP, nc.sync, stg[u % NS][:, :], w_d[u], s_w[u % NS], 16 * (u // NS + 1), after))

        def own(tok, s, value):
            tok.sem, tok.value, tok.used = s, value, True
            return tok

        VW = 1536

        def split_unit():
            u = len(split_tok)
            if u >= N_UNITS:
                return
            while len(load_tok) <= u:
                load_unit()
            h, l, s = WH[u % NW], WL[u % NW], stg[u % NS]
            a = own(AC([load_tok[u], done_tok[u - NW] if u >= NW else None], nc.scalar.activation, h[:, :], s[:, :], ACT.Copy), s_wh, u + 1)
            b = own(V([a], nc.vector.tensor_tensor, l[:, 0:VW], s[:, 0:VW], h[:, 0:VW].bitcast(F32), ALU.subtract), s_wl, u + 1)
            c = own(G([a], nc.gpsimd.tensor_tensor, l[:, VW:], s[:, VW:], h[:, VW:].bitcast(F32), ALU.subtract), s_wp, u + 1)
            split_tok.append([a, b, c])
            load_unit()

        at = [0]

        def tile_of(n, entered=False):
            i = at[0]
            u, k = divmod(i, UT)
            if k == 0 or entered:
                while len(split_tok) < min(u + NW, N_UNITS):
                    split_unit()
            at[0] += n
            sl = slice(k * P, (k + n) * P)
            return WH[u % NW][:, sl], WL[u % NW][:, sl], split_tok[u]

        def tile_done(tok):
            if at[0] % UT == 0:
                done_tok.append(tok)

        def run_of(n):
            pieces, o = [], 0
            if at[0] % UT == 0:
                tile_of(0)
            while o < n:
                u, k = divmod(at[0] + o, UT)
                m = min(n - o, UT - k)
                sl = slice(k * P, (k + m) * P)
                pieces.append((WH[u % NW][:, sl], WL[u % NW][:, sl], split_tok[u], o * P, m * P))
                o += m
            at[0] += n
            return pieces

        def run_done(n, tok):
            if at[0] // UT > (at[0] - n) // UT:
                done_tok.append(tok)
                if at[0] < N_UNITS * UT:
                    tile_of(0, True)

        def mm(out, a, b, start, stop, *after):
            return PE([after], nc.tensor.matmul, out, a, b, start=start, stop=stop)

        def gemm(KT, NT, xh, xl, xt, n, evac, pump=None):
            for nt in range(NT):
                b = bank()
                out = banks[b][:, 0:n]
                for kt in range(KT):
                    wh, wl, wt = tile_of(1)
                    first, last = kt == 0, kt == KT - 1
                    mm(out, wh, xh(kt), first, False, wt, free[b], xt(kt))
                    mm(out, wh, xl(kt), False, False)
                    tok = mm(out, wl, xh(kt), False, last)
                    tile_done(tok)
                free[b] = evac(nt, out, tok)
                if pump is not None:
                    pump(nt)

        def branch(count, after, few, many):
            qs = (PE, AC, V, G)
            before = [q.ops for q in qs]
            state = (at[0], list(split_tok), list(done_tok), list(free), turn[0])
            arms = []
            for arm in (few, many):
                for q in qs:
                    q.ops = []
                at[0], turn[0] = state[0], state[4]
                split_tok[:], done_tok[:], free[:] = state[1], state[2], state[3]
                arm()
                arms.append([q.ops for q in qs])
            joined = []
            for i, q in enumerate(qs):
                q.ops = before[i]
                joined.append(q(after, BRANCH, count, arms[0][i], arms[1][i]))
            free[:] = [joined] * 8
            return joined

        def rsqrt(a, r, tmp, after):
            t = V([after], nc.vector.tensor_scalar, tmp.bitcast(I32), a.bitcast(I32), 1, None, ALU.logical_shift_right)
            t = V([t], nc.vector.tensor_scalar, r.bitcast(I32), tmp.bitcast(I32), -1.0, MAGIC, ALU.mult, ALU.add)
            for _ in range(3):
                t = V([t], nc.vector.tensor_tensor, tmp, r, r, ALU.mult)
                t = V([t], nc.vector.scalar_tensor_tensor, tmp, tmp, -0.5, a, ALU.mult, ALU.mult)
                t = V([t], nc.vector.scalar_tensor_tensor, r, tmp, 1.5, r, ALU.add, ALU.mult)
            return t

        tiles1 = [(16, 128), (144, 128)]
        tiles2 = [(16, 128), (144, 128), (0, 16)]

        def token_sums(src, kts, tiles, dst, after, scale, eps):
            b = bank()
            for i, (c, n) in enumerate(tiles):
                for kt in range(kts):
                    tok = mm(banks[b][0:n, i:i + 1], src[:, kt, c:c + n], ones[:, 0:1], kt == 0, kt == kts - 1,
                             after[kt], free[b])
            outs = []
            for n, lo, hi in ((128, 0, 2), (16, 2, 3)):
                if len(tiles) == 2 and lo == 2:
                    continue
                outs.append(V([tok], nc.vector.tensor_scalar, dst[0:n, lo:hi], banks[b][0:n, lo:hi], scale, eps, ALU.mult, ALU.add))
            free[b] = outs
            return outs

        def along_columns(col, tiles, dst, after, wait_dst):
            b = bank()
            for i, (c, n) in enumerate(tiles):
                d = V([after, dg_read], nc.vector.tensor_scalar, DG[0:n, i, 0:n], ident[0:n, 0:n], col[0:n, i:i + 1], None, ALU.mult)
                tok = mm(banks[b][:, c:c + n], ones[0:n, :], DG[0:n, i, 0:n], True, True, d, free[b])
            dg_read.append(tok)
            lo = min(c for c, _ in tiles)
            free[b] = AC([tok, wait_dst], nc.scalar.activation, dst[:, lo:T], banks[b][:, lo:T], ACT.Copy)
            return free[b]

        dg_read = []

        def rms_input(gname, layer, after, xwait):
            xt, sq = [], []
            for kt in range(KD):
                g = small(gname, layer * 8 + kt)
                r = RES[:, kt, M:T]
                h = AC([after[kt], xwait], nc.scalar.activation, XH[:, kt, M:T], r, ACT.Copy, scale=g)
                l = V([h], nc.vector.scalar_tensor_tensor, XL[:, kt, M:T], r, g, XH[:, kt, M:T].bitcast(F32), ALU.mult, ALU.subtract)
                xt.append([h, l])
                sq.append(G([after[kt], xwait], nc.gpsimd.tensor_tensor, SQ[:, kt, M:T], r, r, ALU.mult))
            return xt, sq

        res_t = dma(RES[:, :, M:T], x_d, "s_x")
        after_s = dma(SM[:, :], small_d, "s_s")
        after_c = dma(CS[:, :], const_d, "s_c")
        first = ExitStack()
        LOOK = sb("look", [33, 6 * JB], F32, first)
        base = [after_c, after_s]
        for q in (PE, AC, V, G):
            q(base, None)
        for _ in range(NW):
            split_unit()
        dw_all = SM[:, OFF["dw"]:OFF["dw"] + 248]
        prep = [V(base, nc.vector.tensor_scalar, small("gains", 2 * l), small("gains", 2 * l), SCALE, None, ALU.mult) for l in range(2)]
        prep.append(V(base, nc.vector.tensor_scalar, dw_all, dw_all, 0.5, None, ALU.mult))
        lt = [side_dma(T1[:, :], tab1_d, "s_t1"), side_dma(T2[:, :], tab2_d, "s_t2"), side_dma(LOOK[:, :], look_d, "s_lk")]
        meta_t = side_dma(RES[:, :, 0:M], meta_d, "s_m")

        bias_t = []
        bufs = [sb(f"bb{i}", [16, JB], F32, first) for i in range(6)]

        def prepare_bias():
            for i, (tab, c0, n, row) in enumerate([(T1, 0, 8, 0), (T1, 8, 8, 8), (T1, 16, 8, 16), (T1, 0, 16, 24),
                                                   (T2, 0, 8, 40), (T2, 0, 8, 48)]):
                b = bank()
                tok = mm(banks[b][0:n, 0:JB], tab[0:33, c0:c0 + n], LOOK[:, i * JB:(i + 1) * JB], True, True, lt, free[b])
                buf = bufs[i]
                free[b] = AC([tok], nc.scalar.activation, buf[0:n, :], banks[b][0:n, 0:JB], ACT.Copy)
                bias_t.append(side_dma(bias_d[row:row + n, :], buf[0:n, :], f"s_bw{i}", free[b]))

        first.close()

        def toeplitz(dst, row, heads, at, n, rows, name, *after):
            src = bass.AP(bias_d.tensor, row * JB + at - (rows - 1), [[1, rows], [JB, heads], [1, n]])
            return side_dma(dst, src, name, after)

        LAG = 2

        def attention(jobs, st, NKmax, NCH, tag):
            
            L = [sb(f"L{tag}{i}", [P, NKmax], F32, st) for i in range(2)]
            PT = [sb(f"PT{tag}{i}", [P, NCH, P], F32, st) for i in range(2)]
            z = sb(f"z{tag}", [P, 2 * LAG + 1, 8], F32, st)
            lread, ptread, zread = [None, None], [None, None], [None] * (2 * LAG + 1)
            keep = {}
            outs = []

            def front(i, j):
                k, kz = i % 2, i % (2 * LAG + 1)
                nq, nk = j["nq"], j["nk"]
                groups, col = [], 512
                for lhs, rhs, bias, o in j["segs"]:
                    w = rhs.shape[1]
                    if col + w > 512:
                        groups.append([bank(), o, 0, None])
                        col = 0
                    b = groups[-1][0]
                    src = banks[b][0:nq, col:col + w]
                    mm(src, lhs, rhs, True, False, free[b], j["after"])
                    groups[-1][3] = mm(src, flip[0:nq, P - nq:P], bias, False, True)
                    col += w
                    groups[-1][2] = col
                nm, r, ri = z[0:nq, kz, 0:1], z[0:nq, kz, 3:4], z[0:nq, kz, 4:5]
                parts = []
                one = len(groups) == 1 and j["sink"] is None
                for n, (b, o, w, tok) in enumerate(groups):
                    parts.append(V([tok, zread[kz]], nc.vector.tensor_reduce, nm if one else z[0:nq, kz, 1 + n:2 + n],
                                   banks[b][0:nq, 0:w], AX, ALU.max, negate=True))
                t = parts
                if not one:
                    other = j["sink"] if j["sink"] is not None else z[0:nq, kz, 2:3]
                    t = V(parts, nc.vector.tensor_tensor, nm, z[0:nq, kz, 1:2], other, ALU.min)
                xs = []
                for n, (b, o, w, _) in enumerate(groups):
                    x = AC([t, lread[k]], nc.scalar.activation, L[k][0:nq, o:o + w], banks[b][0:nq, 0:w], ACT.Exp, bias=nm,
                           accum_out=r if one else z[0:nq, kz, 5 + n:6 + n])
                    free[b] = x
                    xs.append(x)
                y = xs
                if j["sink"] is not None:
                    y = [xs, AC([t], nc.scalar.activation, z[0:nq, kz, 6:7], j["sink"], ACT.Exp, bias=nm, scale=-1.0)]
                if not one:
                    y = V([y], nc.vector.tensor_tensor, r, z[0:nq, kz, 5:6], z[0:nq, kz, 6:7], ALU.add)
                y = V([y], nc.vector.reciprocal, ri, r)
                keep[i] = (xs, y)

            def turn_over(i, j):
                k = i % 2
                nq, ch = j["nq"], j["chunks"]
                x, y = keep[i]
                pt = []
                n0 = 0
                while n0 < len(ch):
                    wide = ch[n0][1]
                    n1 = n0
                    while n1 < len(ch) and n1 < n0 + 4 and ch[n1][1] == wide:
                        n1 += 1
                    b = bank()
                    for c in range(n0, n1):
                        tok = PE([x, free[b]], nc.tensor.transpose, banks[b][0:wide, (c - n0) * P:(c - n0) * P + nq],
                                 L[k][0:nq, ch[c][0]:ch[c][0] + wide], ident[0:nq, 0:nq])
                    n = n1 - n0
                    if nq == P:
                        dst, src = PT[k][0:wide, n0:n1, :].rearrange("p a b -> p (a b)"), banks[b][0:wide, 0:n * P]
                    else:
                        dst, src = PT[k][0:wide, n0, 0:nq], banks[b][0:wide, 0:nq]
                        assert n == 1
                    free[b] = AC([tok, ptread[k]], nc.scalar.activation, dst, src, ACT.Copy)
                    pt.append(free[b])
                    n0 = n1
                lread[k] = tok
                keep[i] = (pt, y)

            def values(i, j):
                k, kz = i % 2, i % (2 * LAG + 1)
                nq, ch = j["nq"], j["chunks"]
                pt, y = keep.pop(i)
                b = bank()
                for c, (_, wide, vap) in enumerate(ch):
                    tok = mm(banks[b][0:nq, 0:64], PT[k][0:wide, c, 0:nq], vap, c == 0, c == len(ch) - 1, pt, free[b], j["vafter"])
                ptread[k] = tok
                free[b] = AC([tok, y], nc.scalar.activation, j["out"], banks[b][0:nq, 0:64], ACT.Copy, scale=z[0:nq, kz, 4:5])
                zread[kz] = free[b]
                outs.append(free[b])

            def step(i):
                if i >= 2 * LAG:
                    values(i - 2 * LAG, jobs[i - 2 * LAG])
                if LAG <= i < len(jobs) + LAG:
                    turn_over(i - LAG, jobs[i - LAG])
                if i < len(jobs):
                    front(i, jobs[i])

            return step, outs

        def to_features(O, NT, tiles, n, after, xwait, kt0=0):
            xt = []
            for nt in range(NT):
                b = bank()
                for i, (c, w) in enumerate(tiles):
                    tok = PE([after, free[b]], nc.tensor.transpose, banks[b][:, c:c + w], O[0:w, i, nt * P:(nt + 1) * P], ident[0:w, 0:w])
                lo = min(c for c, _ in tiles)
                h = AC([tok, xwait], nc.scalar.activation, XH[:, kt0 + nt, lo:T], banks[b][:, lo:T], ACT.Copy)
                l = V([h], nc.vector.tensor_tensor, XL[:, kt0 + nt, lo:T], banks[b][:, lo:T], XH[:, kt0 + nt, lo:T].bitcast(F32), ALU.subtract)
                free[b] = [l]
                xt.append([h, l])
            return xt

        xh_f = lambda kt: XH[:, kt, M:T]
        xl_f = lambda kt: XL[:, kt, M:T]
        xh_t = lambda kt, tt: XH[:, kt, M + tt * P:M + (tt + 1) * P]
        xl_t = lambda kt, tt: XL[:, kt, M + tt * P:M + (tt + 1) * P]

        def last(q):
            return q.ops[-1][-1]

        def everyone():
            return [last(q) for q in (PE, AC, V, G) if q.ops]

        res_after = [res_t] * KD

        def mixer(layer, NGR, HG, row0):
            nonlocal res_after
            st = ExitStack()
            nh = NGR * 8
            BT = sb(f"BT{layer}", [P, nh, S], F32, st)
            bt = []
            QT = sb(f"QT{layer}", [P, 2, NGR * 4, S], F32, st)
            VT = sb(f"VT{layer}", [P, 2, NGR, 512], F32, st)
            O = sb(f"O{layer}", [P, 2, HG * 64], F32, st)
            NK, NCH = (768, 6) if layer == 0 else (256, 2)
            jobs, ready = [], []
            step, outs = attention(jobs, st, NK, NCH, f"m{layer}")
            xt, sq = rms_input("nmix", layer, res_after, phase_end)
            stt = st6[:, 0, 0:2]
            rst = st6[:, 1, 0:2]
            rstd = []
            ssq, rr, rtmp = st6[:, 3, :], st6[:, 4, :], st6[:, 5, :]
            flat = lambda b: b[:, :, :].rearrange("p a b -> p (a b)")
            raw = [flat(XC)[:, i * 256:(i + 1) * 256] for i in range(8)]
            sqr = [flat(SQ)[:, i * 256:(i + 1) * 256] for i in range(8)]
            rawread, sqread = [None] * 8, [None] * 8
            ssread = [None, None]
            sums, pend = [], []
            done = [0]

            def evac(kind, g, half, tt, ps, tok, turn):
                if kind == 2:
                    t = AC([tok, rstd, bt], nc.scalar.activation, VT[:, tt, g, half * 256:(half + 1) * 256], ps, ACT.Copy,
                           scale=rst[:, tt:tt + 1])
                    ready.append(t)
                    return t
                i = turn * 4 + kind * 2 + tt
                a = AC([tok, rstd, rawread[i]], nc.scalar.activation, raw[i], ps, ACT.Copy, scale=rst[:, tt:tt + 1])
                q = G([a, sqread[i], rstd], nc.gpsimd.tensor_tensor, sqr[i], raw[i], raw[i], ALU.mult)
                so = turn * 16 + kind * 8 + tt * 4
                r = V([q, ssread[turn]], nc.vector.reduce_sum, ssq[:, so:so + 4], sqr[i].rearrange("p (h d) -> p h d", h=4), AX)
                sqread[i] = r
                sums.append(r)
                return a

            def head_norms(g, half, turn):
                o = turn * 16
                t = V([sums], nc.vector.tensor_scalar, ssq[:, o:o + 16], ssq[:, o:o + 16], 1.0 / 64, EPS, ALU.mult, ALU.add)
                t = rsqrt(ssq[:, o:o + 16], rr[:, o:o + 16], rtmp[:, o:o + 16], t)
                sums.clear()
                ns = []
                for kind in range(2):
                    for tt in range(2):
                        i = turn * 4 + kind * 2 + tt
                        v = raw[i].rearrange("p (h d) -> p h d", h=4)
                        rb = rr[:, o + kind * 8 + tt * 4:o + kind * 8 + tt * 4 + 4].unsqueeze(2).to_broadcast([P, 4, 64])
                        n = V([t], nc.vector.tensor_tensor, v, v, rb, ALU.mult)
                        ns.append(n)
                        pend.append((kind, g, half, tt, i, n))
                ssread[turn] = ns

            def transposes():
                while pend:
                    kind, g, half, tt, i, n = pend.pop(0)
                    b = bank()
                    for c in range(2):
                        tok = PE([n, free[b]], nc.tensor.transpose, banks[b][:, c * P:(c + 1) * P], raw[i][:, c * P:(c + 1) * P], ident)
                    rawread[i] = tok
                    p0 = g * 4 + half * 2
                    free[b] = AC([tok, bt, prep], nc.scalar.activation, QT[:, kind, p0:p0 + 2, tt * P:(tt + 1) * P],
                                 banks[b][:, 0:256].rearrange("p (c n) -> p c n", c=2), ACT.Copy,
                                 scale=small("gains", 2 * layer + kind))
                    ready.append(free[b])

            def make_jobs(hq):
                after = [list(ready), bt]
                for hh in range(4 * hq, 4 * hq + 4):
                    lst = [(g, hh) for g in range(3)] if layer == 0 else [(hh // 8, hh % 8)]
                    for tt in range(2):
                        nk = P * (tt + 1)
                        segs, chunks = [], []
                        for si, (g, h) in enumerate(lst):
                            po, pr = 64 * (h % 2), g * 4 + h // 2
                            segs.append((QT[po:po + 64, 0, pr, tt * P:(tt + 1) * P], QT[po:po + 64, 1, pr, 0:nk],
                                         BT[:, g * 8 + h, S - nk:S], si * nk))
                            for c in range(tt + 1):
                                chunks.append((si * nk + c * P, P, VT[:, c, g, h * 64:(h + 1) * 64]))
                        jobs.append(dict(nq=P, nk=nk * len(lst), segs=segs, chunks=chunks, sink=None,
                                         out=O[:, tt, hh * 64:(hh + 1) * 64], after=after, vafter=after))

            def advance(n):
                for _ in range(n):
                    if done[0] < len(jobs):
                        step(done[0])
                        done[0] += 1

            if layer == 0:
                groups = [(half, g, half) for half in range(2) for g in range(3)]
            else:
                groups = [(hq, hq // 2, hq % 2) for hq in range(4)]
            steps_at = (4,) if layer == 0 else (2, 4, 7)
            for gi, (hq, g, half) in enumerate(groups):
                for kind in range(3):
                    bs = [bank(), bank()]
                    held.update(bs)
                    toks = [None, None]
                    for kt in range(KD):
                        wh, wl, wt = tile_of(2)
                        start_, lastk = kt == 0, kt == KD - 1
                        for tt in range(2):
                            out = banks[bs[tt]][:, 0:256]
                            mm(out, xh_t(kt, tt), wh, start_, False, wt, free[bs[tt]], xt[kt])
                            mm(out, xl_t(kt, tt), wh, False, False)
                            toks[tt] = mm(out, xh_t(kt, tt), wl, False, lastk)
                        tile_done(toks[1])
                        if kt in steps_at:
                            advance(1)
                    if gi == 0 and kind == 0:
                        t = token_sums(SQ, KD, tiles1, stt, sq, 1.0 / D, EPS)
                        rstd.append(rsqrt(stt, rst, st6[:, 2, 0:2], t))
                    transposes()
                    for tt in range(2):
                        free[bs[tt]] = evac(kind, g, half, tt, banks[bs[tt]][:, 0:256], toks[tt], gi % 2)
                    held.clear()
                    if gi == 0 and kind == 0:
                        if layer == 0:
                            prepare_bias()
                            for g3 in range(3):
                                bt.append(toeplitz(BT[:, g3 * 8:(g3 + 1) * 8, :], row0 + g3 * 8, 8, 127, S, P, f"s_bt{layer}{g3}", bias_t))
                        else:
                            bt.append(toeplitz(BT[:, :, :], row0, 16, 127, S, P, f"s_bt{layer}", bias_t, phase_end))
                    if kind == 1:
                        head_norms(g, half, gi % 2)
                if layer == 1 or g == 2:
                    make_jobs(hq)
            last_jobs = len(jobs)
            while done[0] < last_jobs + 2 * LAG:
                step(done[0])
                done[0] += 1
            ot = to_features(O, HG // 2, tiles1, S, outs, None)
            new = []

            def evac_o(nt, ps, tok):
                t = V([tok], nc.vector.tensor_tensor, RES[:, nt, M:T], RES[:, nt, M:T], ps, ALU.add)
                new.append(t)
                return t

            gemm(HG // 2, KD, xh_f, xl_f, lambda kt: ot[kt], S, evac_o)
            res_after = new
            st.close()

        def ffn1(layer):
            nonlocal res_after
            st = ExitStack()
            HH = sb(f"HH{layer}", [P, 32, S], F32R, st)
            HL = sb(f"HL{layer}", [P, 32, S], F32R, st)
            NR = 3
            tmp = [sb(f"ft{layer}{i}", [P, S], F32, st) for i in range(NR)]
            tm2 = [sb(f"fu{layer}{i}", [P, S], F32, st) for i in range(NR)]
            pend = everyone()
            xt, sq = rms_input("nffn", layer, res_after, pend)
            ht = []
            tr, sr = [None] * NR, [None] * NR

            def evac_h(nt, ps, tok):
                i = nt % NR
                a = AC([tok, tr[i], pend], nc.scalar.activation, tmp[i][:, :], ps, ACT.Relu)
                h = AC([a], nc.scalar.activation, HH[:, nt, :], tmp[i][:, :], ACT.Square)
                s = G([a, sr[i]], nc.gpsimd.tensor_tensor, tm2[i][:, :], tmp[i][:, :], tmp[i][:, :], ALU.mult)
                l = V([s, h], nc.vector.tensor_tensor, HL[:, nt, :], tm2[i][:, :], HH[:, nt, :].bitcast(F32), ALU.subtract)
                tr[i] = [h, s]
                sr[i] = l
                ht.append([h, l])
                return a

            gemm(KD, 32, xh_f, xl_f, lambda kt: xt[kt], S, evac_h)
            t = token_sums(SQ, KD, tiles1, st6[:, 0, 0:2], sq, 1.0 / D, EPS)
            t = V([t], nc.vector.reciprocal, st6[:, 1, 0:2], st6[:, 0, 0:2])
            bc = along_columns(st6[:, 1, 0:2], tiles1, BC, t, None)
            new = []

            def evac_y(nt, ps, tok):
                t = V([tok, bc, res_xc], nc.vector.tensor_tensor, XC[:, nt, M:T], ps, BC[:, M:T], ALU.mult)
                new.append(V([t], nc.vector.tensor_tensor, RES[:, nt, M:T], RES[:, nt, M:T], XC[:, nt, M:T], ALU.add))
                return t

            res_xc = None
            gemm(32, KD, lambda kt: HH[:, kt, :], lambda kt: HL[:, kt, :], lambda kt: ht[kt], S, evac_y)
            res_after = new
            st.close()

        phase_end = None
        mixer(0, 3, 8, 0)
        if upto >= 2:
            ffn1(0)
        if upto >= 3:
            phase_end = everyone()
            mixer(1, 2, 16, 24)
        if upto >= 4:
            ffn1(1)

        def layer_norm(X, kts, gname, bname, li, eps, after, wait, post):
            b = bank()
            for kt in range(kts):
                tok = mm(banks[b][:, 0:T], ones, X[:, kt, 0:T], kt == 0, kt == kts - 1, after[kt], free[b])
            mu = AC([tok, wait], nc.scalar.activation, BC[:, :], banks[b][:, 0:T], ACT.Copy, scale=1.0 / (kts * P))
            free[b] = mu
            sq, xc = [], []
            for kt in range(kts):
                c = V([mu, wait, after[kt]], nc.vector.tensor_tensor, XC[:, kt, :], X[:, kt, 0:T], BC[:, :], ALU.subtract)
                xc.append(c)
                sq.append(AC([c, wait], nc.scalar.activation, SQ[:, kt, :], XC[:, kt, :], ACT.Square))
            t = token_sums(SQ, kts, tiles2, st6[:, 0, 0:3], sq, 1.0 / (kts * P), eps)
            pe_sq = last(PE)
            t = rsqrt(st6[:, 0, 0:3], st6[:, 1, 0:3], st6[:, 2, 0:3], [t, st_init])
            bc = along_columns(st6[:, 1, 0:3], tiles2, BC, t, xc)
            out = []
            for kt in range(kts):
                y = V([bc, pe_sq], nc.vector.scalar_tensor_tensor, SQ[:, kt, :], XC[:, kt, :], small(gname, li * kts + kt), BC[:, :], ALU.mult, ALU.mult)
                out.append(post(kt, SQ[:, kt, :], small(bname, li * kts + kt), y))
            return out

        st_init = V([everyone()], nc.vector.memset, st6[:, 0:2, 0:8], 1.0)

        def split_norm(X, wait):
            def post(kt, y, bias, tok):
                h = AC([tok, wait], nc.scalar.activation, XH[:, kt, :], y, ACT.Identity, bias=bias)
                l = V([h], nc.vector.scalar_tensor_tensor, XL[:, kt, :], y, bias, XH[:, kt, :].bitcast(F32), ALU.add, ALU.subtract)
                r = G([tok], nc.gpsimd.tensor_scalar, X[:, kt, :], y, bias, None, ALU.add)
                return [r, h, l]
            return post

        res_after = [[t, meta_t] for t in res_after]
        xt = None
        if upto >= 5:
            pend = everyone()
            xt = layer_norm(RES, KD, "embg", "embb", 0, LN_EPS, res_after, pend, split_norm(RES, pend))
        xh_a = lambda kt: XH[:, kt, :]
        xl_a = lambda kt: XL[:, kt, :]

        def mix_layer(li, xt):
            st = ExitStack()
            pend = everyone()
            BW = sb(f"BW{li}", [P, 8, S], F32, st)
            BM = sb(f"BM{li}", [P, 3, 8, M], F32, st)
            bt = [toeplitz(BW[:, :, :], 40, 8, 127, S, P, f"s_bw2{li}", bias_t, pend),
                  toeplitz(BM[:, 0, :, :], 48, 8, 271 - 16, M, P, f"s_bm0{li}", bias_t, pend),
                  toeplitz(BM[:, 1, :, :], 48, 8, 271 - 144, M, P, f"s_bm1{li}", bias_t, pend),
                  toeplitz(BM[0:M, 2, :, :], 48, 8, 271, M, M, f"s_bm2{li}", bias_t, pend)]
            QT = sb(f"Q2{li}", [P, 4, T], F32, st)
            KT = sb(f"K2{li}", [P, T], F32, st)
            VF = sb(f"VF{li}", [P, T], F32, st)
            V2 = sb(f"V2{li}", [P, 3, P], F32, st)
            HC = sb(f"HC{li}", [P, 4, 30 + T], F32, st)
            AC4 = sb(f"CA{li}", [P, 4, T], F32, st)
            SG = sb(f"SG{li}", [P, 2, KD, T], F32, st)
            MH = sb(f"MH{li}", [P, KD, T], F32R, st)
            ML = sb(f"ML{li}", [P, KD, T], F32R, st)
            O = sb(f"O2{li}", [P, 3, 512], F32, st)
            nsink = sb(f"ns{li}", [P, 8], F32, st)
            nst = V([pend], nc.vector.tensor_scalar, nsink[:, :], small("sinks", li * 8, 8), -1.0, None, ALU.mult)
            zt = G([pend], nc.gpsimd.memset, HC[:, :, 0:30], 0.0)
            qk, vt, sgt = [], [], {}

            tg = [None] * 4

            def evac(nt, ps, tok):
                if nt < 8:
                    c = nt // 2
                    if nt % 2 == 0:
                        tg[c] = AC([tok, pend], nc.scalar.activation, HC[:, c, 30:30 + T], ps, ACT.Tanh, scale=0.5)
                        return tg[c]
                    hc[c] = V([tok, tg[c], zt], nc.vector.scalar_tensor_tensor, HC[:, c, 30:30 + T], HC[:, c, 30:30 + T], 1.0, ps,
                              ALU.add, ALU.mult)
                    return hc[c]
                if nt < 12:
                    t = AC([tok, pend], nc.scalar.activation, QT[:, nt - 8, :], ps, ACT.Copy, scale=SCALE)
                    qk.append(t)
                elif nt == 12:
                    t = AC([tok, pend], nc.scalar.activation, KT[:, :], ps, ACT.Copy)
                    qk.append(t)
                elif nt == 13:
                    t = AC([tok, pend], nc.scalar.activation, VF[:, :], ps, ACT.Copy)
                    vt.append(t)
                else:
                    w, c = divmod(nt - 14, 8)
                    t = AC([tok, pend], nc.scalar.activation, SG[:, w, c, :], ps, ACT.Tanh, scale=0.5)
                    sgt[(w, c)] = t
                return t

            acc, taps = [None] * 4, [0] * 4
            NPR = 4
            PR = SQ[:, :, :].rearrange("p (c i) t -> p c i t", c=2)
            prr = [[None] * NPR, [None] * NPR]

            def tap(c):
                k = taps[c]
                if k == 31:
                    return
                taps[c] += 1
                w = small("dw", (li * 4 + c) * 31 + k)
                src = HC[:, c, k:k + T]
                cb = small("cb", li * 4 + c)
                if c < VC:
                    if k == 0:
                        acc[c] = V([hc[c], pend, prep], nc.vector.tensor_scalar, AC4[:, c, :], src, w, cb, ALU.mult, ALU.add)
                    else:
                        acc[c] = V([acc[c]], nc.vector.scalar_tensor_tensor, AC4[:, c, :], src, w, AC4[:, c, :], ALU.mult, ALU.add)
                elif k == 0:
                    acc[c] = AC([hc[c], pend, prep], nc.scalar.activation, AC4[:, c, :], src, ACT.Identity, scale=w, bias=cb)
                else:
                    i = k % NPR
                    a = AC([hc[c], pend, prr[c - VC][i]], nc.scalar.activation, PR[:, c - VC, i, :], src, ACT.Copy, scale=w)
                    acc[c] = G([a, acc[c]], nc.gpsimd.tensor_tensor, AC4[:, c, :], AC4[:, c, :], PR[:, c - VC, i, :], ALU.add)
                    prr[c - VC][i] = acc[c]

            VC, TAPS_END = 2, 28
            hc = [None] * 4
            jobs = []
            step, outs = attention(jobs, st, T, 3, f"b{li}")
            done = [0]

            def make_jobs():
                b = bank()
                for i, (c, w) in enumerate(tiles2):
                    tok = PE([vt, free[b]], nc.tensor.transpose, banks[b][0:w, i * P:(i + 1) * P], VF[:, c:c + w], ident)
                v1 = AC([tok, pend], nc.scalar.activation, V2[:, 0:2, :].rearrange("p a b -> p (a b)"), banks[b][:, 0:2 * P], ACT.Copy)
                v2 = AC([tok, pend], nc.scalar.activation, V2[0:M, 2, :], banks[b][0:M, 2 * P:3 * P], ACT.Copy)
                free[b] = [v1, v2]
                for h in range(8):
                    po, pr = 64 * (h // 4), h % 4
                    vh = slice(64 * (h // 4), 64 * (h // 4) + 64)
                    for tt, (c0, nq) in ((2, tiles2[2]), (0, tiles2[0]), (1, tiles2[1])):
                        q = QT[po:po + 64, pr, c0:c0 + nq]
                        segs = [(q, KT[po:po + 64, 0:M], BM[0:nq, tt, h, :], 0)]
                        chunks = [(0, M, V2[0:M, 2, vh])]
                        nk = M
                        if tt < 2:
                            w = P * (tt + 1)
                            segs.append((q, KT[po:po + 64, M:M + w], BW[:, h, S - w:S], M))
                            chunks += [(M + c * P, P, V2[:, c, vh]) for c in range(tt + 1)]
                            nk += w
                        jobs.append(dict(nq=nq, nk=nk, segs=segs, chunks=chunks, sink=nsink[0:nq, h:h + 1],
                                         out=O[0:nq, tt, h * 64:(h + 1) * 64], after=[qk, bt, nst], vafter=[v1, v2]))

            def pump(nt):
                for c in range(4):
                    while hc[c] is not None and taps[c] < min(31, 31 * (nt - 2 * c) // (TAPS_END - 2 * c)):
                        tap(c)
                if nt == 14:
                    make_jobs()
                if nt >= 14:
                    for _ in range(2):
                        if done[0] < len(jobs) + 2 * LAG:
                            step(done[0])
                            done[0] += 1

            gemm(KD, 30, xh_a, xl_a, lambda kt: xt[kt], T, evac, pump)
            xdone = last(PE)
            while min(taps) < 31:
                for c in range(4):
                    tap(c)
            while done[0] < len(jobs) + 2 * LAG:
                step(done[0])
                done[0] += 1
            ot = to_features(O, 4, tiles2, T, outs, xdone)

            def post(kt, y, bias, tok):
                r = AC([tok], nc.scalar.activation, XC[:, kt, :], y, ACT.Silu, bias=bias)
                h = AC([r, xdone], nc.scalar.activation, XH[:, 4 + kt, :], XC[:, kt, :], ACT.Copy)
                l = V([h], nc.vector.tensor_tensor, XL[:, 4 + kt, :], XC[:, kt, :], XH[:, 4 + kt, :].bitcast(F32), ALU.subtract)
                return [h, l]

            ct = layer_norm(AC4, 4, "clg", "clb", li, LN_EPS, acc, None, post)
            mt = []

            def evac_a(nt, ps, tok):
                sgt[(0, nt)] = V([tok, sgt[(0, nt)]], nc.vector.scalar_tensor_tensor, SG[:, 0, nt, :], SG[:, 0, nt, :], 1.0, ps,
                                 ALU.add, ALU.mult)
                return sgt[(0, nt)]

            gemm(4, KD, xh_a, xl_a, lambda kt: ot[kt], T, evac_a)

            def evac_c(nt, ps, tok):
                t = V([tok, sgt[(1, nt)]], nc.vector.scalar_tensor_tensor, SG[:, 1, nt, :], SG[:, 1, nt, :], 1.0, ps, ALU.add, ALU.mult)
                m = V([t, sgt[(0, nt)]], nc.vector.tensor_tensor, SG[:, 0, nt, :], SG[:, 0, nt, :], SG[:, 1, nt, :], ALU.add)
                h = AC([m, pend], nc.scalar.activation, MH[:, nt, :], SG[:, 0, nt, :], ACT.Copy, scale=0.5)
                l = V([h], nc.vector.scalar_tensor_tensor, ML[:, nt, :], SG[:, 0, nt, :], 0.5, MH[:, nt, :].bitcast(F32),
                      ALU.mult, ALU.subtract)
                mt.append([h, l])
                return t

            gemm(4, KD, lambda kt: XH[:, 4 + kt, :], lambda kt: XL[:, 4 + kt, :], lambda kt: ct[kt], T, evac_c)
            new = []

            def evac_o(nt, ps, tok):
                t = V([tok, xt[nt]], nc.vector.scalar_tensor_tensor, RES[:, nt, :], RES[:, nt, :], ALPHA, ps, ALU.mult, ALU.add)
                new.append(t)
                return t

            gemm(KD, KD, lambda kt: MH[:, kt, :], lambda kt: ML[:, kt, :], lambda kt: mt[kt], T, evac_o)
            st.close()
            pend = everyone()
            return layer_norm(RES, KD, "ln1g", "ln1b", li, LN_EPS, new, pend, split_norm(RES, pend))

        def swiglu_hidden(NT, lo, xt, HH, HL, tmp, tm2, pend, ht, rd):
            n = T - lo

            def evac(i, ps, tok):
                nt, up = divmod(i, 2)
                k = nt % len(tmp)
                if not up:
                    t = AC([tok, rd[k], pend], nc.scalar.activation, tmp[k][:, 0:n], ps, ACT.Silu)
                    rd[k] = [t]
                    return t
                t = V([tok, rd[k]], nc.vector.tensor_tensor, tm2[k][:, 0:n], tmp[k][:, 0:n], ps, ALU.mult)
                h = AC([t, pend], nc.scalar.activation, HH[:, nt, 0:n], tm2[k][:, 0:n], ACT.Copy)
                l = V([h], nc.vector.tensor_tensor, HL[:, nt, 0:n], tm2[k][:, 0:n], HH[:, nt, 0:n].bitcast(F32), ALU.subtract)
                ht.append([h, l])
                rd[k] = [h, l]
                return t

            gemm(KD, 2 * NT, lambda kt: XH[:, kt, lo:T], lambda kt: XL[:, kt, lo:T], lambda kt: xt[kt], n, evac)

        def dense(xt):
            st = ExitStack()
            HH = sb("DHH", [P, 22, T], F32R, st)
            HL = sb("DHL", [P, 22, T], F32R, st)
            tmp = [sb(f"dt{i}", [P, T], F32, st) for i in range(3)]
            tm2 = [sb(f"du{i}", [P, T], F32, st) for i in range(3)]
            ht, new = [], []
            swiglu_hidden(22, 0, xt, HH, HL, tmp, tm2, xt, ht, [None] * 3)

            def evac(nt, ps, tok):
                t = V([tok, xt[nt]], nc.vector.scalar_tensor_tensor, RES[:, nt, :], RES[:, nt, :], ALPHA, ps, ALU.mult, ALU.add)
                new.append(t)
                return t

            gemm(22, KD, lambda kt: HH[:, kt, :], lambda kt: HL[:, kt, :], lambda kt: ht[kt], T, evac)
            st.close()
            pend = everyone()
            return layer_norm(RES, KD, "ln2g", "ln2b", 0, LN_EPS, new, pend, split_norm(RES, pend))

        def moe(xt):
            st = ExitStack()
            C8 = sb("C8", [P, 10, 2, 8], F32, st)
            CNT = sb("CNT", [P, 9], F32, st)
            CNI = sb("CNI", [P, 1], I32, st)
            b = bank()
            for tt in range(2):
                for kt in range(KD):
                    tok = mm(banks[b][:, tt * 8:tt * 8 + 8], RES[:, kt, M + tt * P:M + (tt + 1) * P], small("router", kt * 8, 8),
                             kt == 0, kt == KD - 1, xt, free[b])
            lg, e1, e2, q1, q2, cm = (C8[:, i, :, :] for i in range(6))
            s1 = C8[:, 6, :, :]
            s2 = C8[:, 7, :, :]
            io = iota[:, 0:8].unsqueeze(1).to_broadcast([P, 2, 8])
            msk, rk = C8[:, 8, :, :], C8[:, 9, :, :]
            t = V([tok, xt], nc.vector.tensor_copy, lg, banks[b][:, 0:16].rearrange("p (a b) -> p a b", a=2))
            free[b] = t

            def pick(src, val, onehot, t):
                bc = lambda a: a.to_broadcast([P, 2, 8])
                t = V([t], nc.vector.tensor_reduce, val, src, AX, ALU.max)
                t = V([t], nc.vector.tensor_tensor, q1, src, bc(val), ALU.is_lt)
                t = V([t], nc.vector.scalar_tensor_tensor, q1, q1, 100.0, io, ALU.mult, ALU.add)
                t = V([t], nc.vector.tensor_reduce, s2[:, :, 0:1], q1, AX, ALU.min)
                return V([t], nc.vector.tensor_tensor, onehot, io, bc(s2[:, :, 0:1]), ALU.is_equal)

            v1, v2, g1, g2, den = (s1[:, :, i:i + 1] for i in range(5))
            t = pick(lg, v1, e1, t)
            t = V([t], nc.vector.scalar_tensor_tensor, q2, e1, -3.0e38, lg, ALU.mult, ALU.add)
            t = pick(q2, v2, e2, t)
            t = V([t], nc.vector.tensor_tensor, den, v2, v1, ALU.subtract)
            t = AC([t], nc.scalar.activation, g2, den, ACT.Exp)
            t = V([t], nc.vector.tensor_scalar, den, g2, 1.0, None, ALU.add)
            t = V([t], nc.vector.reciprocal, g1, den)
            t = V([t], nc.vector.tensor_tensor, g2, g2, g1, ALU.mult)
            m_t = V([t], nc.vector.tensor_tensor, msk, e1, e2, ALU.add)
            t = V([t, m_t], nc.vector.tensor_tensor, e1, e1, g1.to_broadcast([P, 2, 8]), ALU.mult)
            t = V([t], nc.vector.tensor_tensor, e2, e2, g2.to_broadcast([P, 2, 8]), ALU.mult)
            comb = V([t], nc.vector.tensor_tensor, cm, e1, e2, ALU.add)

            b = bank()
            mm(banks[b][:, 0:8], upper, msk[:, 0, :], True, True, m_t, free[b])
            mm(banks[b][:, 8:16], ones, msk[:, 0, :], True, False)
            mm(banks[b][:, 8:16], upper, msk[:, 1, :], False, True)
            mm(banks[b][:, 16:24], ones, msk[:, 0, :], True, False)
            tok = mm(banks[b][:, 16:24], ones, msk[:, 1, :], False, True)
            rk_t = V([tok], nc.vector.tensor_copy, rk, banks[b][:, 0:16].rearrange("p (a b) -> p a b", a=2))
            t = V([tok], nc.vector.reduce_max, CNT[:, 8:9], banks[b][:, 16:24], AX)
            free[b] = [rk_t, t]
            cnt_t = V([t], nc.vector.tensor_copy, CNI[:, :], CNT[:, 8:9])
            ready = [xt, comb, rk_t, cnt_t, m_t]

            flat = lambda b: b[:, :, :].rearrange("p a b -> p (a b)")
            tmp = [flat(XC)[:, i * 512:(i + 1) * 512] for i in range(2)]
            tm2 = [flat(XC)[:, 1024 + i * 512:1024 + (i + 1) * 512] for i in range(2)]

            def gate_up(nT, lh, ll, lt, HH, HL, hread, rd, between={}):
                ht = [[] for _ in range(11)]
                pend = []

                def turn():
                    while pend:
                        n0, nn, i, j, t = pend.pop(0)
                        b = bank()
                        for c in range(nn):
                            tok = PE([t, free[b]], nc.tensor.transpose, banks[b][:, c * P:(c + 1) * P], tm2[j][:, c * P:(c + 1) * P], ident)
                        src = banks[b][:, 0:nn * P].rearrange("p (a b) -> p a b", a=nn)
                        hh = HH[:, n0:n0 + nn, i * P:(i + 1) * P]
                        h = AC([tok, hread], nc.scalar.activation, hh, src, ACT.Copy)
                        l = V([h, hread], nc.vector.tensor_tensor, HL[:, n0:n0 + nn, i * P:(i + 1) * P], src, hh.bitcast(F32), ALU.subtract)
                        free[b] = l
                        rd[j] = [rd[j], tok]
                        for n in range(n0, n0 + nn):
                            ht[n] += [h, l]

                for gi, (n0, nn) in enumerate(((0, 4), (4, 4), (8, 3))):
                    w = nn * P
                    two = []
                    for up in range(2):
                        bs = [bank() for _ in range(nT)]
                        toks = [None] * nT
                        for kt in range(KD):
                            pieces = run_of(nn)
                            for i in range(nT):
                                for wh, wl, wt, o, m in pieces:
                                    out = banks[bs[i]][:, o:o + m]
                                    mm(out, lh(kt, i), wh, kt == 0, False, wt, free[bs[i]], lt(kt))
                                    mm(out, ll(kt, i), wh, False, False)
                                    toks[i] = mm(out, lh(kt, i), wl, False, kt == KD - 1)
                            run_done(nn, toks[-1])
                        two.append((bs, toks))
                        if up == 0:
                            turn()
                            for f in between.get((gi, 0), ()):
                                f()
                    (gb, gt), (ub, ut) = two
                    for i in range(nT):
                        j = i if nT == 2 else gi % 2
                        t = AC([gt[i], rd[j], ready], nc.scalar.activation, tmp[j][:, 0:w], banks[gb[i]][:, 0:w], ACT.Silu)
                        free[gb[i]] = t
                        t = V([ut[i], t, rd[j]], nc.vector.tensor_tensor, tm2[j][:, 0:w], tmp[j][:, 0:w], banks[ub[i]][:, 0:w], ALU.mult)
                        free[ub[i]] = t
                        rd[j] = t
                        pend.append((n0, nn, i, j, t))
                    for f in between.get((gi, 1), ()):
                        f()
                return ht, toks[-1], turn

            def sparse():
                sp = ExitStack()
                XTH = sb("XTH", [P, 2, D], F32R, sp)
                XTL = sb("XTL", [P, 2, D], F32R, sp)
                SE = [sb(f"SE{i}", [P, 2, P], F32R, sp) for i in range(2)]
                ST = [sb(f"ST{i}", [P, S], F32R, sp) for i in range(2)]
                GH = [sb(f"GH{i}", [P, KD, P], F32R, sp) for i in range(2)]
                GL = [sb(f"GL{i}", [P, KD, P], F32R, sp) for i in range(2)]
                HH = [sb(f"SHH{i}", [P, 11, P], F32R, sp) for i in range(2)]
                HL = [sb(f"SHL{i}", [P, 11, P], F32R, sp) for i in range(2)]
                CO = sb("CO", [P, 2], F32, sp)
                OF = SQ[:, :, :].rearrange("p a b -> p (a b)")
                OH = XH[:, :, :].rearrange("p a b -> p (a b)")
                OL = XL[:, :, :].rearrange("p a b -> p (a b)")
                xtt, turned = [], []
                for tt in range(2):
                    for q in range(2):
                        b = bank()
                        for c in range(4):
                            tok = PE([ready, free[b]], nc.tensor.transpose, banks[b][:, c * P:(c + 1) * P],
                                     RES[:, q * 4 + c, M + tt * P:M + (tt + 1) * P], ident)
                        turned.append(tok)
                        sl = slice(q * 512, (q + 1) * 512)
                        h = AC([tok], nc.scalar.activation, XTH[:, tt, sl], banks[b][:, :], ACT.Copy)
                        l = V([h], nc.vector.tensor_tensor, XTL[:, tt, sl], banks[b][:, :], XTH[:, tt, sl].bitcast(F32), ALU.subtract)
                        free[b] = l
                        xtt.append([h, l])
                acc = [V([ready, turned], nc.vector.tensor_scalar, RES[:, 2 * i:2 * i + 2, M:T], RES[:, 2 * i:2 * i + 2, M:T], ALPHA, None, ALU.mult)
                       for i in range(4)]
                sread, stread, gread, hread, coread = ([None, None] for _ in range(5))
                oread, ofread, rd = [None, None], [None, None], [None, None]
                chosen, selected = {}, {}

                def choose(x):
                    k = x % 2
                    s_t = [V([ready, sread[k]], nc.vector.tensor_scalar, SE[k][:, tt, :], iota, rk[:, tt, x:x + 1], msk[:, tt, x:x + 1],
                             ALU.is_equal, ALU.mult) for tt in range(2)]
                    chosen[x] = s_t

                def select(x):
                    k = x % 2
                    s_t = chosen.pop(x)
                    b = bank()
                    for tt in range(2):
                        tok = PE([s_t, free[b]], nc.tensor.transpose, banks[b][:, tt * P:(tt + 1) * P], SE[k][:, tt, :].bitcast(F32), ident)
                    for tt in range(2):
                        tok = mm(banks[b][:, 256:257], SE[k][:, tt, :].bitcast(F32), cm[:, tt, x:x + 1], tt == 0, tt == 1)
                    st_t = AC([tok, stread[k]], nc.scalar.activation, ST[k][:, :], banks[b][:, 0:256], ACT.Copy)
                    co_t = AC([tok, coread[k]], nc.scalar.activation, CO[:, k:k + 1], banks[b][:, 256:257], ACT.Copy)
                    free[b] = [st_t, co_t]
                    selected[x] = (s_t, st_t, co_t, [])

                def gather(x, q):
                    k = x % 2
                    s_t, st_t, co_t, gt = selected[x]
                    two = []
                    for src, dst in ((XTH, GH), (XTL, GL)):
                        b = bank()
                        for c in range(4):
                            kt = q * 4 + c
                            for tt in range(2):
                                tok = mm(banks[b][:, c * P:(c + 1) * P], src[:, tt, kt * P:(kt + 1) * P], SE[k][:, tt, :],
                                         tt == 0, tt == 1, xtt, s_t, free[b])
                        out = dst[k][:, q * 4:q * 4 + 4, :].rearrange("p a b -> p (a b)")
                        if src is XTH:
                            free[b] = AC([tok, gread[k]], nc.scalar.activation, out, banks[b][:, :], ACT.Copy)
                        else:
                            free[b] = V([tok, gread[k]], nc.vector.tensor_copy, out, banks[b][:, :])
                        two.append(free[b])
                    gt += [two] * 4
                    sread[k] = tok

                def scatter(x, ot, st_t, js):
                    k = x % 2
                    for j in js:
                        b = bank()
                        for i in range(2):
                            nt = 2 * j + i
                            o = k * 1024 + nt * P
                            mm(banks[b][:, i * S:(i + 1) * S], OH[:, o:o + P], ST[k][:, :], True, False, ot[nt // 4], st_t, free[b])
                            tok = mm(banks[b][:, i * S:(i + 1) * S], OL[:, o:o + P], ST[k][:, :], False, True)
                        r = RES[:, 2 * j:2 * j + 2, M:T]
                        acc[j] = V([tok, acc[j]], nc.vector.tensor_tensor, r, r, banks[b][:, :].rearrange("p (a b) -> p a b", a=2), ALU.add)
                        free[b] = acc[j]
                    oread[k] = tok
                    stread[k] = tok

                choose(0)
                select(0)
                gather(0, 0)
                gather(0, 1)
                late = None
                for x in range(8):
                    k = x % 2
                    _, st_t, co_t, gt = selected.pop(x)
                    between = {(0, 0): [], (0, 1): []}
                    if late is not None:
                        between[(0, 0)].append(lambda: scatter(*late, (0, 1)))
                        between[(0, 1)].append(lambda: scatter(*late, (2, 3)))
                    if x < 7:
                        between[(0, 0)].append(lambda: choose(x + 1))
                        between[(1, 0)] = [lambda: select(x + 1)]
                        between[(1, 1)] = [lambda: gather(x + 1, 0)]
                        between[(2, 0)] = [lambda: gather(x + 1, 1)]
                    ht, gread[k], turn = gate_up(1, lambda kt, i: GH[k][:, kt, :], lambda kt, i: GL[k][:, kt, :], lambda kt: gt[kt],
                                                 HH[k], HL[k], hread[k], rd, between)
                    ot = []
                    for g in range(2):
                        b = bank()
                        for kt in range(11):
                            if g == 0 and kt == 8:
                                turn()
                            wh, wl, wt = tile_of(4)
                            mm(banks[b][:, :], HH[k][:, kt, :], wh, kt == 0, False, wt, free[b], ht[kt])
                            mm(banks[b][:, :], HL[k][:, kt, :], wh, False, False)
                            tok = mm(banks[b][:, :], HH[k][:, kt, :], wl, False, kt == 10)
                            tile_done(tok)
                        o = slice(k * 1024 + g * 512, k * 1024 + (g + 1) * 512)
                        f = AC([tok, co_t, ofread[g]], nc.scalar.activation, OF[:, g * 512:(g + 1) * 512], banks[b][:, :], ACT.Copy, scale=CO[:, k:k + 1])
                        free[b] = f
                        h = AC([f, oread[k], ready], nc.scalar.activation, OH[:, o], OF[:, g * 512:(g + 1) * 512], ACT.Copy)
                        l = V([h, oread[k]], nc.vector.tensor_tensor, OL[:, o], OF[:, g * 512:(g + 1) * 512], OH[:, o].bitcast(F32), ALU.subtract)
                        ofread[g] = [h, l]
                        coread[k] = f
                        ot.append([h, l])
                    hread[k] = tok
                    late = (x, ot, st_t)
                scatter(*late, range(4))
                sp.close()

            def every_token():
                sp = ExitStack()
                HH = [sb(f"EHH{i}", [P, 11, S], F32R, sp) for i in range(2)]
                HL = [sb(f"EHL{i}", [P, 11, S], F32R, sp) for i in range(2)]
                ACC = sb("ACC", [P, 2, D], F32, sp)
                hread = [None, None]
                rd = [None, None]
                acc = {}
                scaled = [V([ready], nc.vector.tensor_scalar, RES[:, kt, M:T], RES[:, kt, M:T], ALPHA, None, ALU.mult) for kt in range(KD)]
                for x in range(8):
                    k = x % 2
                    ht, _, turn = gate_up(2, xh_t, xl_t, lambda kt: xt[kt], HH[k], HL[k], hread[k], rd)
                    turn()
                    for g in range(2):
                        bs = [bank(), bank()]
                        toks = [None, None]
                        for kt in range(11):
                            wh, wl, wt = tile_of(4)
                            for tt in range(2):
                                hh, hl = (a[k][:, kt, tt * P:(tt + 1) * P] for a in (HH, HL))
                                mm(banks[bs[tt]][:, :], hh, wh, kt == 0, False, wt, free[bs[tt]], ht[kt])
                                mm(banks[bs[tt]][:, :], hl, wh, False, False)
                                toks[tt] = mm(banks[bs[tt]][:, :], hh, wl, False, kt == 10)
                            tile_done(toks[1])
                        for tt in range(2):
                            a = ACC[:, tt, g * 512:(g + 1) * 512]
                            c = cm[:, tt, x:x + 1]
                            if x == 0:
                                t = V([toks[tt], ready], nc.vector.tensor_scalar, a, banks[bs[tt]][:, :], c, None, ALU.mult)
                            else:
                                t = V([toks[tt], acc[(g, tt)]], nc.vector.scalar_tensor_tensor, a, banks[bs[tt]][:, :], c, a, ALU.mult, ALU.add)
                            acc[(g, tt)] = t
                            free[bs[tt]] = t
                    hread[k] = toks[1]
                for tt in range(2):
                    for g in range(2):
                        b = bank()
                        for c in range(4):
                            tok = PE([acc[(g, tt)], free[b]], nc.tensor.transpose, banks[b][:, c * P:(c + 1) * P],
                                     ACC[:, tt, (g * 4 + c) * P:(g * 4 + c + 1) * P], ident)
                        r = RES[:, g * 4:g * 4 + 4, M + tt * P:M + (tt + 1) * P]
                        free[b] = V([tok, scaled], nc.vector.tensor_tensor, r, r, banks[b][:, :].rearrange("p (a b) -> p a b", a=4), ALU.add)
                sp.close()

            joined = branch(CNI[0:1, 0:1], ready, sparse, every_token)
            st.close()
            outs = []

            def post(kt, y, bias, tok):
                r = AC([tok], nc.scalar.activation, RES[:, kt, :], y, ACT.Identity, bias=bias)
                outs.append(r)
                return r

            return layer_norm(RES, KD, "ln2g", "ln2b", 1, LN_EPS, [joined] * KD, joined, post)

        if upto >= 6:
            xt = mix_layer(0, xt)
        if upto >= 7:
            xt = dense(xt)
        if upto >= 8:
            xt = mix_layer(1, xt)
        if upto >= 9:
            xt = moe(xt)

        end = everyone()
        out_t = dma(out_d, RES[:, :, M:T], "s_out", end, xt, res_after)
        SP([out_t], None)

        for q in (PE, AC, V, G, SP):
            q.count()

        @block.sync
        def _(eng):
            SP.emit(eng)

        @block.gpsimd
        def _(eng):
            G.emit(eng)

        @block.scalar
        def _(eng):
            AC.emit(eng)

        @block.vector
        def _(eng):
            V.emit(eng)

        @block.tensor
        def _(eng):
            PE.emit(eng)


def feature_tiles(w):
    k, n = w.shape
    return w.reshape(k // P, P, n // P, P).transpose(2, 0, 1, 3).reshape(-1, P, P)


def head_tiles(w, groups, order):
    k, n = w.shape
    t = w.reshape(k // P, P, 3, groups, 2, 2, P)
    return np.concatenate([t[:, :, kind, g, half].transpose(0, 2, 1, 3).reshape(-1, P, P)
                           for g, half in order for kind in range(3)])


def token_tiles(w):
    k, n = w.shape
    return w.reshape(k // P, P, n // 512, 4, P).transpose(2, 0, 3, 1, 4).reshape(-1, P, P)


def gate_up_tiles(a, b):
    parts = []
    for n0, n1 in ((0, 4), (4, 8), (8, 11)):
        for w in (a, b):
            t = w[:, n0 * P:n1 * P]
            parts.append(t.reshape(KD, P, n1 - n0, P).transpose(0, 2, 1, 3).reshape(-1, P, P))
    return np.concatenate(parts)


def paired_tiles(a, b):
    k, n = a.shape
    return np.stack([feature_tiles(a).reshape(n // P, k // P, P, P), feature_tiles(b).reshape(n // P, k // P, P, P)],
                    axis=1).reshape(-1, P, P)


def weight_stream(i):
    parts = [head_tiles(i["a_w_qkv"][0], 3, [(g, h) for h in range(2) for g in range(3)]), feature_tiles(i["a_w_o"][0]),
             feature_tiles(i["ffn_w1"][0]), feature_tiles(i["ffn_w2"][0]),
             head_tiles(i["b_w_qkv"][0], 2, [(g, h) for g in range(2) for h in range(2)]), feature_tiles(i["b_w_o"][0]),
             feature_tiles(i["ffn_w1"][1]), feature_tiles(i["ffn_w2"][1])]
    heads = np.arange(512).reshape(2, 4, 64).transpose(1, 0, 2).reshape(-1)
    for l in range(2):
        w = i["w_in_2"][l]
        parts += [paired_tiles(w[:, 1280:1792], w[:, 768:1280]), feature_tiles(w[:, heads]), feature_tiles(w[:, 512:768]),
                  feature_tiles(w[:, 1792:])]
        parts += [feature_tiles(i["w_attn_proj_2"][l]), feature_tiles(i["w_conv_proj_2"][l]), feature_tiles(i["w_out_2"][l])]
        if l == 0:
            parts += [paired_tiles(i["ffn_w_gate_2"][0], i["ffn_w_up_2"][0]), feature_tiles(i["ffn_w_down_2"][0])]
        else:
            for e in range(8):
                parts += [gate_up_tiles(i["moe_w_gate_2"][0, e], i["moe_w_up_2"][0, e]), token_tiles(i["moe_w_down_2"][0, e])]
    w = np.concatenate(parts)
    return np.ascontiguousarray(w.reshape(-1, UT, P, P).transpose(0, 2, 1, 3)).reshape(-1, P, UT * P)


def columns(v):
    return v.reshape(-1, P).T


def small_params(i):
    c = [columns(i["norm_mix"]), columns(i["norm_ffn"]), columns(i["emb_ln_g_2"]), columns(i["emb_ln_b_2"]),
         columns(i["ln1_g_2"]), columns(i["ln1_b_2"]), columns(i["ln2_g_2"]), columns(i["ln2_b_2"]),
         i["conv_dw_2"].reshape(2, 31, 4, P).transpose(3, 0, 2, 1).reshape(P, -1),
         columns(i["conv_b_2"]), columns(i["conv_ln_g_2"]), columns(i["conv_ln_b_2"]),
         np.stack([np.tile(i[n][0], 2) for n in ("a_q_gain", "a_k_gain", "b_q_gain", "b_k_gain")], axis=1),
         np.broadcast_to(i["sinks_2"].reshape(1, -1), (P, 16)),
         i["router_2"][0].reshape(KD, P, 8).transpose(1, 0, 2).reshape(P, -1)]
    return np.ascontiguousarray(np.concatenate(c, axis=1))


def layout(i):
    ident = np.eye(P, dtype=np.float32)
    consts = np.concatenate([ident, np.ones((P, P), np.float32),
                             np.broadcast_to(np.arange(P, dtype=np.float32), (P, P)), ident[::-1],
                             np.triu(np.ones((P, P), np.float32), 1)], axis=1)
    one = np.ones((1, 24), np.float32)
    feat = lambda a: np.ascontiguousarray(a.T.reshape(KD, P, -1).transpose(1, 0, 2))
    return {"w": weight_stream(i), "x": feat(i["x"][0]), "meta": feat(i["meta_tokens_2"]),
            "small": small_params(i), "consts": consts, "look": lookups(),
            "tab1": np.concatenate([i["rel_bias"], one]), "tab2": np.concatenate([i["rel_bias_2"], one[:, :8]])}


def kernel(**inputs):
    import concourse.bacc as _bacc
    from concourse.bass_utils import run_bass_kernel_spmd as _run

    arrays = layout({k: np.asarray(v) for k, v in inputs.items()})
    nc = _bacc.Bacc("TRN2", target_bir_lowering=False, num_devices=1)
    args = [nc.dram_tensor(f"in_{n}", a.shape, F32, kind="ExternalInput").ap() for n, a in arrays.items()]
    out = nc.dram_tensor("out", (P, KD, S), F32, kind="ExternalOutput").ap()
    model_kernel(nc, *args, out)
    r = _run(nc, [{f"in_{n}": np.ascontiguousarray(a) for n, a in arrays.items()}], core_ids=[0])
    y = r.results[0]["out"]
    return np.ascontiguousarray(y.transpose(2, 1, 0).reshape(1, S, D))
```

```python
import math
from contextlib import ExitStack

import numpy as np

import concourse.bass as bass
from concourse import mybir

F32 = mybir.dt.float32
F32R = mybir.dt.float32r
I32 = mybir.dt.int32
ALU = mybir.AluOpType
ACT = mybir.ActivationFunctionType
AX = mybir.AxisListType.X

P = 128
D = 1024
KD = D // P
S = 256
M = 16
T = S + M
NEG = -1e30
EPS = 1e-6
LN_EPS = 1e-5
ALPHA = 4 ** 0.25
SCALE = 64 ** -0.5
UT = 16
MAGIC = float(0x5F3759DF)

SMALL = [("nmix", 16), ("nffn", 16), ("embg", 8), ("embb", 8), ("ln1g", 16), ("ln1b", 16),
         ("ln2g", 16), ("ln2b", 16), ("dw", 2 * 4 * 31), ("cb", 8), ("clg", 8), ("clb", 8),
         ("gains", 4), ("sinks", 16), ("router", 64)]
OFF = {}
_o = 0
for _n, _w in SMALL:
    OFF[_n] = _o
    _o += _w
NSMALL = _o

CONSTS = [("ident", 128), ("ones", 128), ("iota", 128), ("flip", 128), ("upper", 128)]
COFF = {}
_o = 0
for _n, _w in CONSTS:
    COFF[_n] = _o
    _o += _w
NCONST = _o

JB = 384
N_UNITS = 311


def t5_bucket(n, n_buckets, max_distance):
    n = np.maximum(n, 0)
    exact = n_buckets // 2
    nf = np.maximum(n, 1).astype(np.float32)
    large = exact + (np.log(nf / np.float32(exact)) / np.float32(math.log(max_distance / exact))
                     * np.float32(n_buckets - exact)).astype(np.int32)
    return np.where(n < exact, n, np.minimum(large, n_buckets - 1))


def lookup(dists, keep, max_distance):
    b = t5_bucket(dists, 32, max_distance)
    out = np.zeros((33, dists.size), np.float32)
    out[b, np.arange(dists.size)] = 1.0
    out[:, ~keep] = 0.0
    out[32, ~keep] = NEG
    return out


def lookups():
    d = 255 - np.arange(JB)
    a = [lookup(d, (d >= 0) & (d <= 128), 2048), lookup(d, (d >= 0) & (d % 4 == 0), 2048),
         lookup(d, (d >= 0) & (d % 16 == 0), 2048), lookup(d, d >= 0, 2048)]
    w = [lookup(d, (d >= 0) & (d < 128), 128)]
    dm = 271 - np.arange(JB)
    c = [lookup(dm, dm >= 0, 128)]
    return np.concatenate(a + w + c, axis=1)


BRANCH = "branch"


class Tok:
    def __init__(self):
        self.sem, self.value, self.used, self.dma = None, None, False, False


class Queue:

    def __init__(self, sem):
        self.sem, self.ops = sem, []

    def __call__(self, after, method, *args, **kw):
        waits = []
        flatten(after, waits)
        for t in waits:
            t.used = True
        tok = Tok()
        self.ops.append((method, args, kw, waits, tok))
        return tok

    def count(self):
        self.count_ops(self.ops, 0)

    def count_ops(self, ops, n):
        for method, args, _, _, tok in ops:
            if method is BRANCH:
                a, b = (self.count_ops(arm, n) for arm in args[1:])
                n = max(a, b) + 1
                tok.sem, tok.value, tok.fill = self.sem, n, (n - a, n - b)
            elif tok.used and tok.sem is None:
                n += 1
                tok.sem, tok.value = self.sem, n
        return n

    def emit(self, eng, ops=None, seen=None):
        ops, seen = (self.ops, {}) if ops is None else (ops, seen)
        for method, args, kw, waits, tok in ops:
            best = {}
            for t in waits:
                k = id(t.sem)
                if seen.get(k, 0) < t.value and best.get(k, (0, None))[0] < t.value:
                    best[k] = (t.value, t.sem)
            for k, (v, s) in best.items():
                eng.wait_ge(s, v)
                seen[k] = v
            if method is None:
                continue
            if method is BRANCH:
                value = eng.value_load(args[0])
                with eng.If(value <= P):
                    self.emit(eng, args[1], dict(seen))
                    eng.drain().then_inc(self.sem, tok.fill[0])
                with eng.Else():
                    self.emit(eng, args[2], dict(seen))
                    eng.drain().then_inc(self.sem, tok.fill[1])
                continue
            ins = method(*args, **kw)
            if tok.dma:
                ins.then_inc(tok.sem, 16)
            elif tok.used:
                ins.then_inc(tok.sem, 1)


def flatten(x, out):
    if x is None:
        return
    if isinstance(x, Tok):
        out.append(x)
        return
    for y in x:
        flatten(y, out)


def model_kernel(nc, w_d, x_d, meta_d, small_d, const_d, look_d, tab1_d, tab2_d, out_d, upto=99):
    bias_d = nc.dram_tensor("bias_scratch", (56, JB), F32, kind="Internal").ap()

    ctx = ExitStack()
    with ctx:
        def sb(name, shape, dt=F32, st=ctx):
            return st.enter_context(nc.sbuf_tensor(name, shape, dt))

        def sem(name):
            return ctx.enter_context(nc.semaphore(name))

        NS, NW = 4, 3
        stg = [sb(f"stg{i}", [P, UT * P]) for i in range(NS)]
        WH = [sb(f"wh{i}", [P, UT * P], F32R) for i in range(NW)]
        WL = [sb(f"wl{i}", [P, UT * P], F32R) for i in range(NW)]
        RES = sb("res", [P, KD, T])
        XH = sb("xh", [P, KD, T], F32R)
        XL = sb("xl", [P, KD, T], F32R)
        XC = sb("xc", [P, KD, T])
        SQ = sb("sq", [P, KD, T])
        SM = sb("small", [P, NSMALL])
        CS = sb("consts", [P, NCONST])
        st6 = sb("st6", [P, 6, 64])
        DG = sb("dg", [P, 3, P])
        BC = sb("bc", [P, T])
        T1 = sb("tab1", [33, 24])
        T2 = sb("tab2", [33, 8])
        ident = CS[:, COFF["ident"]:COFF["ident"] + P]
        ones = CS[:, COFF["ones"]:COFF["ones"] + P]
        flip = CS[:, COFF["flip"]:COFF["flip"] + P]
        iota = CS[:, COFF["iota"]:COFF["iota"] + P]
        upper = CS[:, COFF["upper"]:COFF["upper"] + P]

        banks = [ctx.enter_context(nc.psum_tensor(f"bank{i}", [P, 512], F32)) for i in range(8)]
        free = [None] * 8
        turn = [0]
        held = set()

        s_pe, s_act, s_dve, s_pool, s_sp = (sem(n) for n in ("s_pe", "s_act", "s_dve", "s_pool", "s_sp"))
        s_wh, s_wl, s_wp = sem("s_wh"), sem("s_wl"), sem("s_wp")
        s_w = [sem(f"s_w{i}") for i in range(NS)]
        PE, AC, V, G, SP = Queue(s_pe), Queue(s_act), Queue(s_dve), Queue(s_pool), Queue(s_sp)
        block = ctx.enter_context(nc.Block())

        def small(name, i, n=1):
            return SM[:, OFF[name] + i:OFF[name] + i + n]

        def start(q, eng, dst, src, s, value, *after):
            tok = q(after, eng.dma_start, dst, src)
            tok.sem, tok.value, tok.dma = s, value, True
            return tok

        def dma(dst, src, name, *after):
            return start(SP, nc.sync, dst, src, sem(name), 16, *after)

        def side_dma(dst, src, name, *after):
            return start(G, nc.gpsimd, dst, src, sem(name), 16, *after)

        def bank():
            while turn[0] % 8 in held:
                turn[0] += 1
            i = turn[0] % 8
            turn[0] += 1
            return i

        load_tok, split_tok, done_tok = [], [], []

        def load_unit():
            u = len(load_tok)
            if u >= N_UNITS:
                return
            after = split_tok[u - NS] if u >= NS else None
            load_tok.append(start(SP, nc.sync, stg[u % NS][:, :], w_d[u], s_w[u % NS], 16 * (u // NS + 1), after))

        def own(tok, s, value):
            tok.sem, tok.value, tok.used = s, value, True
            return tok

        VW = 1536

        def split_unit():
            u = len(split_tok)
            if u >= N_UNITS:
                return
            while len(load_tok) <= u:
                load_unit()
            h, l, s = WH[u % NW], WL[u % NW], stg[u % NS]
            a = own(AC([load_tok[u], done_tok[u - NW] if u >= NW else None], nc.scalar.activation, h[:, :], s[:, :], ACT.Copy), s_wh, u + 1)
            b = own(V([a], nc.vector.tensor_tensor, l[:, 0:VW], s[:, 0:VW], h[:, 0:VW].bitcast(F32), ALU.subtract), s_wl, u + 1)
            c = own(G([a], nc.gpsimd.tensor_tensor, l[:, VW:], s[:, VW:], h[:, VW:].bitcast(F32), ALU.subtract), s_wp, u + 1)
            split_tok.append([a, b, c])
            load_unit()

        at = [0]

        def tile_of(n, entered=False):
            i = at[0]
            u, k = divmod(i, UT)
            if k == 0 or entered:
                while len(split_tok) < min(u + NW, N_UNITS):
                    split_unit()
            at[0] += n
            sl = slice(k * P, (k + n) * P)
            return WH[u % NW][:, sl], WL[u % NW][:, sl], split_tok[u]

        def tile_done(tok):
            if at[0] % UT == 0:
                done_tok.append(tok)

        def run_of(n):
            pieces, o = [], 0
            if at[0] % UT == 0:
                tile_of(0)
            while o < n:
                u, k = divmod(at[0] + o, UT)
                m = min(n - o, UT - k)
                sl = slice(k * P, (k + m) * P)
                pieces.append((WH[u % NW][:, sl], WL[u % NW][:, sl], split_tok[u], o * P, m * P))
                o += m
            at[0] += n
            return pieces

        def run_done(n, tok):
            if at[0] // UT > (at[0] - n) // UT:
                done_tok.append(tok)
                if at[0] < N_UNITS * UT:
                    tile_of(0, True)

        def mm(out, a, b, start, stop, *after):
            return PE([after], nc.tensor.matmul, out, a, b, start=start, stop=stop)

        def gemm(KT, NT, xh, xl, xt, n, evac, pump=None):
            for nt in range(NT):
                b = bank()
                out = banks[b][:, 0:n]
                for kt in range(KT):
                    wh, wl, wt = tile_of(1)
                    first, last = kt == 0, kt == KT - 1
                    mm(out, wh, xh(kt), first, False, wt, free[b], xt(kt))
                    mm(out, wh, xl(kt), False, False)
                    tok = mm(out, wl, xh(kt), False, last)
                    tile_done(tok)
                free[b] = evac(nt, out, tok)
                if pump is not None:
                    pump(nt)

        def branch(count, after, few, many):
            qs = (PE, AC, V, G)
            before = [q.ops for q in qs]
            state = (at[0], list(split_tok), list(done_tok), list(free), turn[0])
            arms = []
            for arm in (few, many):
                for q in qs:
                    q.ops = []
                at[0], turn[0] = state[0], state[4]
                split_tok[:], done_tok[:], free[:] = state[1], state[2], state[3]
                arm()
                arms.append([q.ops for q in qs])
            joined = []
            for i, q in enumerate(qs):
                q.ops = before[i]
                joined.append(q(after, BRANCH, count, arms[0][i], arms[1][i]))
            free[:] = [joined] * 8
            return joined

        def rsqrt(a, r, tmp, after):
            t = V([after], nc.vector.tensor_scalar, tmp.bitcast(I32), a.bitcast(I32), 1, None, ALU.logical_shift_right)
            t = V([t], nc.vector.tensor_scalar, r.bitcast(I32), tmp.bitcast(I32), -1.0, MAGIC, ALU.mult, ALU.add)
            for _ in range(3):
                t = V([t], nc.vector.tensor_tensor, tmp, r, r, ALU.mult)
                t = V([t], nc.vector.scalar_tensor_tensor, tmp, tmp, -0.5, a, ALU.mult, ALU.mult)
                t = V([t], nc.vector.scalar_tensor_tensor, r, tmp, 1.5, r, ALU.add, ALU.mult)
            return t

        tiles1 = [(16, 128), (144, 128)]
        tiles2 = [(16, 128), (144, 128), (0, 16)]

        def token_sums(src, kts, tiles, dst, after, scale, eps):
            bs = [bank() for _ in tiles]
            toks = [None] * len(tiles)
            for kt in range(kts):
                for i, (c, n) in enumerate(tiles):
                    toks[i] = mm(banks[bs[i]][0:n, 0:1], src[:, kt, c:c + n], ones[:, 0:1], kt == 0, kt == kts - 1,
                                 after[kt], free[bs[i]])
            outs = []
            for i, (c, n) in enumerate(tiles):
                free[bs[i]] = V([toks[i]], nc.vector.tensor_scalar, dst[0:n, i:i + 1], banks[bs[i]][0:n, 0:1], scale, eps, ALU.mult, ALU.add)
                outs.append(free[bs[i]])
            return outs

        def along_columns(col, tiles, dst, after, wait_dst):
            b = bank()
            for i, (c, n) in enumerate(tiles):
                d = V([after, dg_read], nc.vector.tensor_scalar, DG[0:n, i, 0:n], ident[0:n, 0:n], col[0:n, i:i + 1], None, ALU.mult)
                tok = mm(banks[b][:, c:c + n], ones[0:n, :], DG[0:n, i, 0:n], True, True, d, free[b])
            dg_read.append(tok)
            lo = min(c for c, _ in tiles)
            free[b] = AC([tok, wait_dst], nc.scalar.activation, dst[:, lo:T], banks[b][:, lo:T], ACT.Copy)
            return free[b]

        dg_read = []

        def rms_input(gname, layer, after, xwait):
            return tuple(zip(*[rms_tile(gname, layer, kt, after[kt], xwait) for kt in range(KD)]))

        def rms_tile(gname, layer, kt, after, xwait):
            g = small(gname, layer * 8 + kt)
            r = RES[:, kt, M:T]
            h = AC([after, xwait], nc.scalar.activation, XH[:, kt, M:T], r, ACT.Copy, scale=g)
            l = V([h], nc.vector.scalar_tensor_tensor, XL[:, kt, M:T], r, g, XH[:, kt, M:T].bitcast(F32), ALU.mult, ALU.subtract)
            return [h, l], G([after, xwait], nc.gpsimd.tensor_tensor, SQ[:, kt, M:T], r, r, ALU.mult)

        res_t = dma(RES[:, :, M:T], x_d, "s_x")
        after_s = dma(SM[:, :], small_d, "s_s")
        after_c = dma(CS[:, :], const_d, "s_c")
        first = ExitStack()
        LOOK = sb("look", [33, 6 * JB], F32, first)
        base = [after_c, after_s]
        for q in (PE, AC, V, G):
            q(base, None)
        for _ in range(NS):
            load_unit()
        split_unit()
        dw_all = SM[:, OFF["dw"]:OFF["dw"] + 248]
        prep = [V(base, nc.vector.tensor_scalar, small("gains", 2 * l), small("gains", 2 * l), SCALE, None, ALU.mult) for l in range(2)]
        prep.append(V(base, nc.vector.tensor_scalar, dw_all, dw_all, 0.5, None, ALU.mult))
        lt = [side_dma(T1[:, :], tab1_d, "s_t1"), side_dma(T2[:, :], tab2_d, "s_t2"), side_dma(LOOK[:, :], look_d, "s_lk")]
        meta_t = side_dma(RES[:, :, 0:M], meta_d, "s_m")

        bias_t = []
        bufs = [sb(f"bb{i}", [16, JB], F32, first) for i in range(6)]

        def prepare_bias():
            for i, (tab, c0, n, row) in enumerate([(T1, 0, 8, 0), (T1, 8, 8, 8), (T1, 16, 8, 16), (T1, 0, 16, 24),
                                                   (T2, 0, 8, 40), (T2, 0, 8, 48)]):
                b = bank()
                tok = mm(banks[b][0:n, 0:JB], tab[0:33, c0:c0 + n], LOOK[:, i * JB:(i + 1) * JB], True, True, lt, free[b])
                buf = bufs[i]
                free[b] = AC([tok], nc.scalar.activation, buf[0:n, :], banks[b][0:n, 0:JB], ACT.Copy)
                bias_t.append(side_dma(bias_d[row:row + n, :], buf[0:n, :], f"s_bw{i}", free[b]))

        first.close()

        def toeplitz(dst, row, heads, at, n, rows, name, *after):
            src = bass.AP(bias_d.tensor, row * JB + at - (rows - 1), [[1, rows], [JB, heads], [1, n]])
            return side_dma(dst, src, name, after)

        LAG = 2

        def attention(jobs, st, NKmax, NCH, tag):
            
            L = [sb(f"L{tag}{i}", [P, NKmax], F32, st) for i in range(2)]
            PT = [sb(f"PT{tag}{i}", [P, NCH, P], F32, st) for i in range(2)]
            z = sb(f"z{tag}", [P, 2 * LAG + 1, 8], F32, st)
            lread, ptread, zread = [None, None], [None, None], [None] * (2 * LAG + 1)
            keep = {}
            outs = []

            def added(i, j):
                k, kz = i % 2, i % (2 * LAG + 1)
                nk, bias = j["nk"], j["add"]
                nb = bias.shape[1]
                w = nk // nb
                nm, r, ri = z[:, kz, 0:1], z[:, kz, 3:4], z[:, kz, 4:5]
                adds = []
                for s0 in range(0, nb, 512 // w):
                    s1 = min(nb, s0 + 512 // w)
                    b = bank()
                    for n in range(s0, s1):
                        lhs, rhs = j["segs"][n]
                        tok = mm(banks[b][:, (n - s0) * w:(n - s0 + 1) * w], lhs, rhs, True, True, free[b], j["after"])
                    free[b] = V([tok, lread[k]], nc.vector.tensor_tensor, L[k][:, s0 * w:s1 * w].rearrange("p (a b) -> p a b", a=s1 - s0),
                                banks[b][:, 0:(s1 - s0) * w].rearrange("p (a b) -> p a b", a=s1 - s0), bias[:, s0:s1, :], ALU.add)
                    adds.append(free[b])
                t = V([adds, zread[kz]], nc.vector.tensor_reduce, nm, L[k][:, 0:nk], AX, ALU.max, negate=True)
                x = AC([t], nc.scalar.activation, L[k][:, 0:nk], L[k][:, 0:nk], ACT.Exp, bias=nm, accum_out=r)
                keep[i] = ([x], V([x], nc.vector.reciprocal, ri, r))

            def front(i, j):
                k, kz = i % 2, i % (2 * LAG + 1)
                nq, nk = j["nq"], j["nk"]
                if "add" in j:
                    added(i, j)
                    return
                groups, col = [], 512
                for lhs, rhs, bias, o in j["segs"]:
                    w = rhs.shape[1]
                    if col + w > 512:
                        groups.append([bank(), o, 0, None])
                        col = 0
                    b = groups[-1][0]
                    src = banks[b][0:nq, col:col + w]
                    mm(src, lhs, rhs, True, False, free[b], j["after"])
                    groups[-1][3] = mm(src, flip[0:nq, P - nq:P], bias, False, True)
                    col += w
                    groups[-1][2] = col
                nm, r, ri = z[0:nq, kz, 0:1], z[0:nq, kz, 3:4], z[0:nq, kz, 4:5]
                parts = []
                one = len(groups) == 1 and j["sink"] is None
                for n, (b, o, w, tok) in enumerate(groups):
                    parts.append(V([tok, zread[kz]], nc.vector.tensor_reduce, nm if one else z[0:nq, kz, 1 + n:2 + n],
                                   banks[b][0:nq, 0:w], AX, ALU.max, negate=True))
                t = parts
                if not one:
                    other = j["sink"] if j["sink"] is not None else z[0:nq, kz, 2:3]
                    t = V(parts, nc.vector.tensor_tensor, nm, z[0:nq, kz, 1:2], other, ALU.min)
                xs = []
                for n, (b, o, w, _) in enumerate(groups):
                    x = AC([t, lread[k]], nc.scalar.activation, L[k][0:nq, o:o + w], banks[b][0:nq, 0:w], ACT.Exp, bias=nm,
                           accum_out=r if one else z[0:nq, kz, 5 + n:6 + n])
                    free[b] = x
                    xs.append(x)
                y = xs
                if j["sink"] is not None:
                    y = [xs, AC([t], nc.scalar.activation, z[0:nq, kz, 6:7], j["sink"], ACT.Exp, bias=nm, scale=-1.0)]
                if not one:
                    y = V([y], nc.vector.tensor_tensor, r, z[0:nq, kz, 5:6], z[0:nq, kz, 6:7], ALU.add)
                y = V([y], nc.vector.reciprocal, ri, r)
                keep[i] = (xs, y)

            def turn_over(i, j):
                k = i % 2
                nq, ch = j["nq"], j["chunks"]
                x, y = keep[i]
                pt = []
                for g in range(0, len(ch), 4):
                    four = ch[g:g + 4]
                    b = bank()
                    for c, (at, wide, _) in enumerate(four):
                        tok = PE([x, free[b]], nc.tensor.transpose, banks[b][0:wide, c * P:c * P + nq],
                                 L[k][0:nq, at:at + wide], ident[0:nq, 0:nq])
                    n0, read = 0, []
                    while n0 < len(four):
                        wide = four[n0][1]
                        n1 = n0 + 1
                        while n1 < len(four) and four[n1][1] == wide and nq == P:
                            n1 += 1
                        if nq == P:
                            dst, src = PT[k][0:wide, g + n0:g + n1, :].rearrange("p a b -> p (a b)"), banks[b][0:wide, n0 * P:n1 * P]
                        else:
                            dst, src = PT[k][0:wide, g + n0, 0:nq], banks[b][0:wide, n0 * P:n0 * P + nq]
                        read.append(AC([tok, ptread[k]], nc.scalar.activation, dst, src, ACT.Copy))
                        n0 = n1
                    free[b] = read
                    pt += read
                lread[k] = tok
                keep[i] = (pt, y)

            def values(i, j):
                k, kz = i % 2, i % (2 * LAG + 1)
                nq, ch = j["nq"], j["chunks"]
                pt, y = keep.pop(i)
                b = bank()
                for c, (_, wide, vap) in enumerate(ch):
                    tok = mm(banks[b][0:nq, 0:64], PT[k][0:wide, c, 0:nq], vap, c == 0, c == len(ch) - 1, pt, free[b], j["vafter"])
                ptread[k] = tok
                free[b] = AC([tok, y], nc.scalar.activation, j["out"], banks[b][0:nq, 0:64], ACT.Copy, scale=z[0:nq, kz, 4:5])
                zread[kz] = free[b]
                outs.append(free[b])

            def step(i):
                if i >= 2 * LAG:
                    values(i - 2 * LAG, jobs[i - 2 * LAG])
                if LAG <= i < len(jobs) + LAG:
                    turn_over(i - LAG, jobs[i - LAG])
                if i < len(jobs):
                    front(i, jobs[i])

            return step, outs

        def to_features(O, NT, tiles, n, after, xwait, order):
            xt = []
            for nt in range(NT):
                b = bank()
                for i, (c, w) in enumerate(tiles):
                    tok = mm(banks[b][:, c:c + w], O[0:w, i, nt * P:(nt + 1) * P], order[0:w, 0:w], True, True, after, free[b])
                lo = min(c for c, _ in tiles)
                h = AC([tok, xwait], nc.scalar.activation, XH[:, nt, lo:T], banks[b][:, lo:T], ACT.Copy)
                l = V([h], nc.vector.tensor_tensor, XL[:, nt, lo:T], banks[b][:, lo:T], XH[:, nt, lo:T].bitcast(F32), ALU.subtract)
                free[b] = [l]
                xt.append([h, l])
            return xt

        xh_f = lambda kt: XH[:, kt, M:T]
        xl_f = lambda kt: XL[:, kt, M:T]
        xh_t = lambda kt, tt: XH[:, kt, M + tt * P:M + (tt + 1) * P]
        xl_t = lambda kt, tt: XL[:, kt, M + tt * P:M + (tt + 1) * P]

        def last(q):
            return q.ops[-1][-1]

        def everyone():
            return [last(q) for q in (PE, AC, V, G) if q.ops]

        res_after = [res_t] * KD

        def feature_sum(X, kts):
            b = bank()
            held.add(b)
            return b, lambda kt, after: mm(banks[b][:, 0:T], ones, X[:, kt, 0:T], kt == 0, kt == kts - 1, after, free[b])

        def running_sum(new):
            total = feature_sum(RES, KD)
            return (total, KD - 2), lambda nt: total[1](nt - 2, new[nt - 2]) if nt >= 2 else None

        def mixer(layer, NGR, HG, row0, fed=None):
            nonlocal res_after
            st = ExitStack()
            nh = NGR * 8
            BT = sb(f"BT{layer}", [P, nh, S], F32, st)
            bt = []
            QT = sb(f"QT{layer}", [P, 2, NGR * 4, S], F32, st)
            VT = sb(f"VT{layer}", [P, 2, NGR, 512], F32, st)
            O = sb(f"O{layer}", [P, 2, HG * 64], F32, st)
            NK, NCH = (768, 6) if layer == 0 else (256, 2)
            jobs, ready = [], []
            step, outs = attention(jobs, st, NK, NCH, f"m{layer}")
            xt, sq = fed if fed is not None else rms_input("nmix", layer, res_after, phase_end)
            stt = st6[:, 0, 0:2]
            rst = st6[:, 1, 0:2]
            rstd = []
            ssq, rr, rtmp = st6[:, 3, :], st6[:, 4, :], st6[:, 5, :]
            flat = lambda b: b[:, :, :].rearrange("p a b -> p (a b)")
            raw = [flat(XC)[:, i * 256:(i + 1) * 256] for i in range(8)]
            sqr = [flat(SQ)[:, i * 256:(i + 1) * 256] for i in range(8)]
            rawread, sqread = [None] * 8, [None] * 8
            ssread = [None, None]
            sums, pend = [], []
            done = [0]

            def evac(kind, g, half, tt, ps, tok, turn):
                if kind == 2:
                    t = AC([tok, rstd, bt], nc.scalar.activation, VT[:, tt, g, half * 256:(half + 1) * 256], ps, ACT.Copy,
                           scale=rst[:, tt:tt + 1])
                    ready.append(t)
                    return t
                i = turn * 4 + kind * 2 + tt
                a = AC([tok, rstd, rawread[i]], nc.scalar.activation, raw[i], ps, ACT.Copy, scale=rst[:, tt:tt + 1])
                q = G([a, sqread[i], rstd], nc.gpsimd.tensor_tensor, sqr[i], raw[i], raw[i], ALU.mult)
                so = turn * 16 + kind * 8 + tt * 4
                r = V([q, ssread[turn]], nc.vector.reduce_sum, ssq[:, so:so + 4], sqr[i].rearrange("p (h d) -> p h d", h=4), AX)
                sqread[i] = r
                sums.append(r)
                return a

            def head_norms(g, half, turn):
                o = turn * 16
                t = V([sums], nc.vector.tensor_scalar, ssq[:, o:o + 16], ssq[:, o:o + 16], 1.0 / 64, EPS, ALU.mult, ALU.add)
                t = rsqrt(ssq[:, o:o + 16], rr[:, o:o + 16], rtmp[:, o:o + 16], t)
                sums.clear()
                ns = []
                for kind in range(2):
                    for tt in range(2):
                        i = turn * 4 + kind * 2 + tt
                        v = raw[i].rearrange("p (h d) -> p h d", h=4)
                        rb = rr[:, o + kind * 8 + tt * 4:o + kind * 8 + tt * 4 + 4].unsqueeze(2).to_broadcast([P, 4, 64])
                        n = V([t], nc.vector.tensor_tensor, v, v, rb, ALU.mult)
                        ns.append(n)
                        pend.append((kind, g, half, tt, i, n))
                ssread[turn] = ns

            def transposes():
                while pend:
                    kind, g, half, tt, i, n = pend.pop(0)
                    b = bank()
                    for c in range(2):
                        src, out = raw[i][:, c * P:(c + 1) * P], banks[b][:, c * P:(c + 1) * P]
                        if kind == 0:
                            tok = mm(out, src, flip, True, True, n, free[b])
                        else:
                            tok = PE([n, free[b]], nc.tensor.transpose, out, src, ident)
                    rawread[i] = tok
                    p0 = g * 4 + half * 2
                    free[b] = AC([tok, bt, prep], nc.scalar.activation, QT[:, kind, p0:p0 + 2, tt * P:(tt + 1) * P],
                                 banks[b][:, 0:256].rearrange("p (c n) -> p c n", c=2), ACT.Copy,
                                 scale=small("gains", 2 * layer + kind))
                    ready.append(free[b])

            def make_jobs(hq):
                after = [list(ready), bt]
                for hh in range(4 * hq, 4 * hq + 4):
                    lst = [(g, hh) for g in range(3)] if layer == 0 else [(hh // 8, hh % 8)]
                    for tt in range(2):
                        nk = P * (tt + 1)
                        segs, chunks = [], []
                        bias = BT.rearrange("p (g h) s -> p g h s", h=8)[:, lst[0][0]:lst[-1][0] + 1, lst[0][1], S - nk:S]
                        for si, (g, h) in enumerate(lst):
                            po, pr = 64 * (h % 2), g * 4 + h // 2
                            segs.append((QT[po:po + 64, 0, pr, tt * P:(tt + 1) * P], QT[po:po + 64, 1, pr, 0:nk]))
                            for c in range(tt + 1):
                                chunks.append((si * nk + c * P, P, VT[:, c, g, h * 64:(h + 1) * 64]))
                        jobs.append(dict(nq=P, nk=nk * len(lst), segs=segs, add=bias, chunks=chunks, sink=None,
                                         out=O[:, tt, hh * 64:(hh + 1) * 64], after=after, vafter=after))

            def advance(n):
                for _ in range(n):
                    if done[0] < len(jobs):
                        step(done[0])
                        done[0] += 1

            if layer == 0:
                groups = [(half, g, half) for half in range(2) for g in range(3)]
            else:
                groups = [(hq, hq // 2, hq % 2) for hq in range(4)]
            steps_at = (2, 5) if layer == 0 else (1, 3, 5, 7)
            for gi, (hq, g, half) in enumerate(groups):
                for kind in range(3):
                    bs = [bank(), bank()]
                    held.update(bs)
                    toks = [None, None]
                    for kt in range(KD):
                        wh, wl, wt = tile_of(2)
                        start_, lastk = kt == 0, kt == KD - 1
                        for tt in range(2):
                            out = banks[bs[tt]][:, 0:256]
                            mm(out, xh_t(kt, tt), wh, start_, False, wt, free[bs[tt]], xt[kt])
                            mm(out, xl_t(kt, tt), wh, False, False)
                            toks[tt] = mm(out, xh_t(kt, tt), wl, False, lastk)
                        tile_done(toks[1])
                        if kt in steps_at:
                            advance(1)
                    if gi == 0 and kind == 0:
                        t = token_sums(SQ, KD, tiles1, stt, sq, 1.0 / D, EPS)
                        rstd.append(rsqrt(stt, rst, st6[:, 2, 0:2], t))
                    transposes()
                    for tt in range(2):
                        free[bs[tt]] = evac(kind, g, half, tt, banks[bs[tt]][:, 0:256], toks[tt], gi % 2)
                    held.clear()
                    if gi == 0 and kind == 0:
                        if layer == 0:
                            prepare_bias()
                            for g3 in range(3):
                                bt.append(toeplitz(BT[:, g3 * 8:(g3 + 1) * 8, :], row0 + g3 * 8, 8, 127, S, P, f"s_bt{layer}{g3}", bias_t))
                        else:
                            bt.append(toeplitz(BT[:, :, :], row0, 16, 127, S, P, f"s_bt{layer}", bias_t, phase_end))
                    if kind == 1:
                        head_norms(g, half, gi % 2)
                if layer == 1 or g == 2:
                    make_jobs(hq)
            last_jobs = len(jobs)
            while done[0] < last_jobs + 2 * LAG:
                step(done[0])
                done[0] += 1
            ot = to_features(O, HG // 2, tiles1, S, outs, None, flip)
            new = []

            def evac_o(nt, ps, tok):
                t = V([tok], nc.vector.tensor_tensor, RES[:, nt, M:T], RES[:, nt, M:T], ps, ALU.add)
                new.append(t)
                return t

            gemm(HG // 2, KD, xh_f, xl_f, lambda kt: ot[kt], S, evac_o)
            res_after = new
            st.close()

        def ffn1(layer):
            nonlocal res_after
            st = ExitStack()
            HH = sb(f"HH{layer}", [P, 32, S], F32R, st)
            HL = sb(f"HL{layer}", [P, 32, S], F32R, st)
            NR = 3
            tmp = [sb(f"ft{layer}{i}", [P, S], F32, st) for i in range(NR)]
            tm2 = [sb(f"fu{layer}{i}", [P, S], F32, st) for i in range(NR)]
            pend = everyone()
            xt, sq = rms_input("nffn", layer, res_after, pend)
            ht = []
            tr, sr = [None] * NR, [None] * NR

            def evac_h(nt, ps, tok):
                i = nt % NR
                a = AC([tok, tr[i], pend], nc.scalar.activation, tmp[i][:, :], ps, ACT.Relu)
                h = AC([a], nc.scalar.activation, HH[:, nt, :], tmp[i][:, :], ACT.Square)
                s = G([a, sr[i]], nc.gpsimd.tensor_tensor, tm2[i][:, :], tmp[i][:, :], tmp[i][:, :], ALU.mult)
                l = V([s, h], nc.vector.tensor_tensor, HL[:, nt, :], tm2[i][:, :], HH[:, nt, :].bitcast(F32), ALU.subtract)
                tr[i] = [h, s]
                sr[i] = l
                ht.append([h, l])
                return a

            bc = []

            def norm(nt):
                if nt == 8:
                    b = bank()
                    for kt in range(KD):
                        tok = mm(banks[b][:, 0:S], ones, SQ[:, kt, M:T], kt == 0, kt == KD - 1, sq[kt], free[b])
                    free[b] = V([tok], nc.vector.tensor_scalar, BC[:, M:T], banks[b][:, 0:S], 1.0 / D, EPS, ALU.mult, ALU.add)
                    bc.append(V([free[b]], nc.vector.reciprocal, BC[:, M:T], BC[:, M:T]))

            gemm(KD, 32, xh_f, xl_f, lambda kt: xt[kt], S, evac_h, norm)
            xdone = last(PE)
            new, fed = [], []

            def evac_y(nt, ps, tok):
                t = V([tok, bc, res_xc], nc.vector.tensor_tensor, XC[:, nt, M:T], ps, BC[:, M:T], ALU.mult)
                new.append([V([t], nc.vector.tensor_tensor, RES[:, nt, M:T], RES[:, nt, M:T], XC[:, nt, M:T], ALU.add), meta_t])
                return t

            res_xc = None
            begun, pump = None, lambda nt: fed.append(rms_tile("nmix", 1, nt, new[nt], xdone))
            if layer == 1:
                begun, pump = running_sum(new)
            gemm(32, KD, lambda kt: HH[:, kt, :], lambda kt: HL[:, kt, :], lambda kt: ht[kt], S, evac_y, pump)
            res_after = new
            st.close()
            return begun if layer == 1 else list(zip(*fed))

        phase_end = None
        mixer(0, 3, 8, 0)
        if upto >= 2:
            fed = ffn1(0)
        if upto >= 3:
            phase_end = everyone()
            mixer(1, 2, 16, 24, fed)
        if upto >= 4:
            begun = ffn1(1)

        def layer_norm(*args):
            *_, out = layer_norm_parts(*args)
            return out

        def layer_norm_parts(X, kts, gname, bname, li, eps, after, wait, post, begun=None):
            (b, add), k0 = begun if begun is not None else (feature_sum(X, kts), 0)
            for kt in range(k0, kts):
                tok = add(kt, after[kt])
            held.discard(b)
            mu = AC([tok, wait], nc.scalar.activation, BC[:, :], banks[b][:, 0:T], ACT.Copy, scale=1.0 / (kts * P))
            free[b] = mu
            sq, xc = [], []
            for kt in range(kts):
                c = V([mu, wait, after[kt]], nc.vector.tensor_tensor, XC[:, kt, :], X[:, kt, 0:T], BC[:, :], ALU.subtract)
                xc.append(c)
                sq.append(AC([c, wait], nc.scalar.activation, SQ[:, kt, :], XC[:, kt, :], ACT.Square))
            yield None
            t = token_sums(SQ, kts, tiles2, st6[:, 0, 0:3], sq, 1.0 / (kts * P), eps)
            pe_sq = last(PE)
            t = rsqrt(st6[:, 0, 0:3], st6[:, 1, 0:3], st6[:, 2, 0:3], [t, st_init])
            yield None
            bc = along_columns(st6[:, 1, 0:3], tiles2, BC, t, xc)
            ys, out = [], []

            def finish(kt):
                out.append(post(kt, SQ[:, kt, :], small(bname, li * kts + kt), ys[kt]))

            for kt in range(kts):
                y = V([bc, pe_sq], nc.vector.scalar_tensor_tensor, SQ[:, kt, :], XC[:, kt, :], small(gname, li * kts + kt), BC[:, :], ALU.mult, ALU.mult)
                ys.append(y)
                if kt > 0:
                    finish(kt - 1)
            finish(kts - 1)
            yield out

        st_init = V([everyone()], nc.vector.memset, st6[:, 0:2, 0:8], 1.0)

        def plain_norm(wait):
            return lambda kt, y, bias, tok: AC([tok, wait], nc.scalar.activation, RES[:, kt, :], y, ACT.Identity, bias=bias)

        def split_norm(X, wait):
            done, biases = [], []

            def post(kt, y, bias, tok):
                biases.append(bias)
                h = AC([tok, wait], nc.scalar.activation, XH[:, kt, :], y, ACT.Identity, bias=bias)
                l = V([h], nc.vector.scalar_tensor_tensor, XL[:, kt, :], y, bias, XH[:, kt, :].bitcast(F32), ALU.add, ALU.subtract)
                done.append([h, l])
                if kt == KD - 1:
                    for k, d in enumerate(done):
                        d.append(AC([tok, d], nc.scalar.activation, X[:, k, :], SQ[:, k, :], ACT.Identity, bias=biases[k]))
                return done[-1]
            return post

        res_after = [[t, meta_t] for t in res_after]
        xt = None
        if upto >= 5:
            pend = everyone()
            xt = layer_norm(RES, KD, "embg", "embb", 0, LN_EPS, res_after, pend, split_norm(RES, pend), begun)
        xh_a = lambda kt: XH[:, kt, :]
        xl_a = lambda kt: XL[:, kt, :]

        def mix_layer(li, xt):
            st = ExitStack()
            pend = everyone()
            BB = [sb(f"BB{li}{i}", [P, 8, M + P * (i + 1)], F32, st) for i in range(2)]
            BM = sb(f"BM{li}", [M, 8, M], F32, st)
            bt = [toeplitz(BB[1][:, :, M:T], 40, 8, 127, S, P, f"s_bw1{li}", bias_t, pend),
                  toeplitz(BB[1][:, :, 0:M], 48, 8, 271 - 144, M, P, f"s_bm1{li}", bias_t, pend),
                  toeplitz(BB[0][:, :, M:M + P], 40, 8, 127 + P, P, P, f"s_bw0{li}", bias_t, pend),
                  toeplitz(BB[0][:, :, 0:M], 48, 8, 271 - 16, M, P, f"s_bm0{li}", bias_t, pend),
                  toeplitz(BM[:, :, :], 48, 8, 271, M, M, f"s_bm2{li}", bias_t, pend)]
            QT = sb(f"Q2{li}", [P, 4, T], F32, st)
            KT = sb(f"K2{li}", [P, T], F32, st)
            VF = sb(f"VF{li}", [P, T], F32, st)
            V2 = sb(f"V2{li}", [P, 3, P], F32, st)
            HC = sb(f"HC{li}", [P, 4, 30 + T], F32, st)
            AC4 = sb(f"CA{li}", [P, 4, T], F32, st)
            SG = sb(f"SG{li}", [P, 2, KD, T], F32, st)
            MH = sb(f"MH{li}", [P, KD, T], F32R, st)
            ML = sb(f"ML{li}", [P, KD, T], F32R, st)
            O = sb(f"O2{li}", [P, 3, 512], F32, st)
            nsink = sb(f"ns{li}", [P, 8], F32, st)
            nst = V([pend], nc.vector.tensor_scalar, nsink[:, :], small("sinks", li * 8, 8), -1.0, None, ALU.mult)
            zt = G([pend], nc.gpsimd.memset, HC[:, :, 0:30], 0.0)
            qk, vt, sgt = [], [], {}
            lo = 0 if li == 0 else M
            n = T - lo
            tiles = tiles2 if li == 0 else tiles1
            xh_n = lambda kt: XH[:, kt, lo:T]
            xl_n = lambda kt: XL[:, kt, lo:T]

            tg = [None] * 4

            def evac(nt, ps, tok):
                if nt < 8:
                    c = nt // 2
                    if nt % 2 == 0:
                        tg[c] = AC([tok, pend], nc.scalar.activation, HC[:, c, 30:30 + T], ps, ACT.Tanh, scale=0.5)
                        return tg[c]
                    hc[c] = V([tok, tg[c], zt], nc.vector.scalar_tensor_tensor, HC[:, c, 30:30 + T], HC[:, c, 30:30 + T], 1.0, ps,
                              ALU.add, ALU.mult)
                    return hc[c]
                if nt < 12:
                    t = AC([tok, pend], nc.scalar.activation, QT[:, nt - 8, :], ps, ACT.Copy, scale=SCALE)
                    qk.append(t)
                elif nt == 12:
                    t = AC([tok, pend], nc.scalar.activation, KT[:, :], ps, ACT.Copy)
                    qk.append(t)
                elif nt == 13:
                    t = AC([tok, pend], nc.scalar.activation, VF[:, :], ps, ACT.Copy)
                    vt.append(t)
                else:
                    w, c = divmod(nt - 14, 8)
                    t = AC([tok, pend], nc.scalar.activation, SG[:, w, c, lo:T], ps, ACT.Tanh, scale=0.5)
                    sgt[(w, c)] = t
                return t

            acc, taps = [None] * 4, [0] * 4
            NPR = 4
            PR = SQ[:, :, :].rearrange("p (c i) t -> p c i t", c=2)
            prr = [[None] * NPR, [None] * NPR]

            def tap(c):
                k = taps[c]
                if k == 31:
                    return
                taps[c] += 1
                w = small("dw", (li * 4 + c) * 31 + k)
                src = HC[:, c, k:k + T]
                cb = small("cb", li * 4 + c)
                if c < VC:
                    if k == 0:
                        acc[c] = V([hc[c], pend, prep], nc.vector.tensor_scalar, AC4[:, c, :], src, w, cb, ALU.mult, ALU.add)
                    else:
                        acc[c] = V([acc[c]], nc.vector.scalar_tensor_tensor, AC4[:, c, :], src, w, AC4[:, c, :], ALU.mult, ALU.add)
                elif k == 0:
                    acc[c] = AC([hc[c], pend, prep], nc.scalar.activation, AC4[:, c, :], src, ACT.Identity, scale=w, bias=cb)
                else:
                    i = k % NPR
                    a = AC([hc[c], pend, prr[c - VC][i]], nc.scalar.activation, PR[:, c - VC, i, :], src, ACT.Copy, scale=w)
                    acc[c] = G([a, acc[c]], nc.gpsimd.tensor_tensor, AC4[:, c, :], AC4[:, c, :], PR[:, c - VC, i, :], ALU.add)
                    prr[c - VC][i] = acc[c]

            VC, TAPS_END = 2, 28
            hc = [None] * 4
            jobs = []
            step, outs = attention(jobs, st, T, 3, f"b{li}")
            done = [0]

            def make_jobs():
                b = bank()
                for i, (c, w) in enumerate(tiles2):
                    tok = PE([vt, free[b]], nc.tensor.transpose, banks[b][0:w, i * P:(i + 1) * P], VF[:, c:c + w], ident)
                v1 = AC([tok, pend], nc.scalar.activation, V2[:, 0:2, :].rearrange("p a b -> p (a b)"), banks[b][:, 0:2 * P], ACT.Copy)
                v2 = AC([tok, pend], nc.scalar.activation, V2[0:M, 2, :], banks[b][0:M, 2 * P:3 * P], ACT.Copy)
                free[b] = [v1, v2]
                for h in range(8):
                    po, pr = 64 * (h // 4), h % 4
                    vh = slice(64 * (h // 4), 64 * (h // 4) + 64)
                    for tt, (c0, nq) in ((2, tiles2[2]), (0, tiles2[0]), (1, tiles2[1]))[3 - len(tiles):]:
                        q = QT[po:po + 64, pr, c0:c0 + nq]
                        chunks = [(0, M, V2[0:M, 2, vh])]
                        nk = M
                        if tt < 2:
                            chunks += [(M + c * P, P, V2[:, c, vh]) for c in range(tt + 1)]
                            nk += P * (tt + 1)
                        segs = [(q, KT[po:po + 64, 0:nk], BB[tt][:, h, :] if tt < 2 else BM[:, h, :], 0)]
                        jobs.append(dict(nq=nq, nk=nk, segs=segs, chunks=chunks, sink=nsink[0:nq, h:h + 1],
                                         out=O[0:nq, tt, h * 64:(h + 1) * 64], after=[qk, bt, nst], vafter=[v1, v2]))

            def advance():
                if done[0] < len(jobs) + 2 * LAG:
                    step(done[0])
                    done[0] += 1

            def pump(nt):
                for c in range(4):
                    while hc[c] is not None and taps[c] < min(31, 31 * (nt - 2 * c) // (TAPS_END - 2 * c)):
                        tap(c)
                if nt == 14:
                    make_jobs()
                if nt >= 14:
                    advance()
                    advance()

            gemm(KD, 14, xh_a, xl_a, lambda kt: xt[kt][:2], T, evac, pump)
            gemm(KD, 16, xh_n, xl_n, lambda kt: xt[kt][:2], n, lambda nt, ps, tok: evac(nt + 14, ps, tok), lambda nt: pump(nt + 14))
            xdone = last(PE)
            while min(taps) < 31:
                for c in range(4):
                    tap(c)
            def post(kt, y, bias, tok):
                r = AC([tok], nc.scalar.activation, XC[:, kt, :], y, ACT.Silu, bias=bias)
                h = AC([r, xdone], nc.scalar.activation, XH[:, 4 + kt, :], XC[:, kt, :], ACT.Copy)
                l = V([h], nc.vector.tensor_tensor, XL[:, 4 + kt, :], XC[:, kt, :], XH[:, 4 + kt, :].bitcast(F32), ALU.subtract)
                return [h, l]

            conv_norm = layer_norm_parts(AC4, 4, "clg", "clb", li, LN_EPS, acc, None, post)
            next(conv_norm)
            while done[0] < len(jobs) + 2 * LAG:
                step(done[0])
                done[0] += 1
            ot = to_features(O, 4, tiles, T, outs, xdone, ident)
            next(conv_norm)
            ct = []
            mt = []

            def evac_a(nt, ps, tok):
                sgt[(0, nt)] = V([tok, sgt[(0, nt)]], nc.vector.scalar_tensor_tensor, SG[:, 0, nt, lo:T], SG[:, 0, nt, lo:T], 1.0, ps,
                                 ALU.add, ALU.mult)
                return sgt[(0, nt)]

            gemm(4, KD, xh_n, xl_n, lambda kt: ot[kt], n, evac_a, lambda nt: ct.extend(next(conv_norm)) if nt == 1 else None)

            def evac_c(nt, ps, tok):
                t = V([tok, sgt[(1, nt)]], nc.vector.scalar_tensor_tensor, SG[:, 1, nt, lo:T], SG[:, 1, nt, lo:T], 1.0, ps, ALU.add, ALU.mult)
                m = V([t, sgt[(0, nt)]], nc.vector.tensor_tensor, SG[:, 0, nt, lo:T], SG[:, 0, nt, lo:T], SG[:, 1, nt, lo:T], ALU.add)
                h = AC([m, pend], nc.scalar.activation, MH[:, nt, lo:T], SG[:, 0, nt, lo:T], ACT.Copy, scale=0.5)
                mt.append([h])
                if nt > 0:
                    low(nt - 1)
                return t

            def low(nt):
                mt[nt].append(V(mt[nt], nc.vector.scalar_tensor_tensor, ML[:, nt, lo:T], SG[:, 0, nt, lo:T], 0.5,
                                MH[:, nt, lo:T].bitcast(F32), ALU.mult, ALU.subtract))

            gemm(4, KD, lambda kt: XH[:, 4 + kt, lo:T], lambda kt: XL[:, 4 + kt, lo:T], lambda kt: ct[kt], n, evac_c)
            low(KD - 1)
            new = []

            def evac_o(nt, ps, tok):
                t = V([tok, xt[nt]], nc.vector.scalar_tensor_tensor, RES[:, nt, lo:T], RES[:, nt, lo:T], ALPHA, ps, ALU.mult, ALU.add)
                new.append(t)
                return t

            begun, sum_up = running_sum(new)
            gemm(KD, KD, lambda kt: MH[:, kt, lo:T], lambda kt: ML[:, kt, lo:T], lambda kt: mt[kt], n, evac_o, sum_up)
            st.close()
            pend = everyone()
            post = split_norm(RES, pend) if li == 0 else plain_norm(pend)
            return layer_norm(RES, KD, "ln1g", "ln1b", li, LN_EPS, new, pend, post, begun)

        def swiglu_hidden(NT, lo, xt, HH, HL, tmp, tm2, pend, ht, rd):
            n = T - lo

            def evac(i, ps, tok):
                nt, up = divmod(i, 2)
                k = nt % len(tmp)
                if not up:
                    t = AC([tok, rd[k], pend], nc.scalar.activation, tmp[k][:, 0:n], ps, ACT.Silu)
                    rd[k] = [t]
                    return t
                t = V([tok, rd[k]], nc.vector.tensor_tensor, tm2[k][:, 0:n], tmp[k][:, 0:n], ps, ALU.mult)
                h = AC([t, pend], nc.scalar.activation, HH[:, nt, 0:n], tm2[k][:, 0:n], ACT.Copy)
                l = V([h], nc.vector.tensor_tensor, HL[:, nt, 0:n], tm2[k][:, 0:n], HH[:, nt, 0:n].bitcast(F32), ALU.subtract)
                ht.append([h, l])
                rd[k] = [h, l]
                return t

            gemm(KD, 2 * NT, lambda kt: XH[:, kt, lo:T], lambda kt: XL[:, kt, lo:T], lambda kt: xt[kt][:2], n, evac)

        def dense(xt):
            st = ExitStack()
            HH = sb("DHH", [P, 22, T], F32R, st)
            HL = sb("DHL", [P, 22, T], F32R, st)
            tmp = [sb(f"dt{i}", [P, T], F32, st) for i in range(3)]
            tm2 = [sb(f"du{i}", [P, T], F32, st) for i in range(3)]
            ht, new = [], []
            swiglu_hidden(22, 0, xt, HH, HL, tmp, tm2, xt, ht, [None] * 3)

            def evac(nt, ps, tok):
                t = V([tok, xt[nt]], nc.vector.scalar_tensor_tensor, RES[:, nt, :], RES[:, nt, :], ALPHA, ps, ALU.mult, ALU.add)
                new.append(t)
                return t

            begun, sum_up = running_sum(new)
            gemm(22, KD, lambda kt: HH[:, kt, :], lambda kt: HL[:, kt, :], lambda kt: ht[kt], T, evac, sum_up)
            st.close()
            pend = everyone()
            return layer_norm(RES, KD, "ln2g", "ln2b", 0, LN_EPS, new, pend, split_norm(RES, pend), begun)

        def moe(xt):
            st = ExitStack()
            C8 = sb("C8", [P, 10, 2, 8], F32, st)
            CNT = sb("CNT", [P, 9], F32, st)
            CNI = sb("CNI", [P, 1], I32, st)
            XTH = sb("XTH", [P, 2, D], F32R, st)
            XTL = sb("XTL", [P, 2, D], F32R, st)
            b = bank()
            for tt in range(2):
                for kt in range(KD):
                    tok = mm(banks[b][:, tt * 8:tt * 8 + 8], RES[:, kt, M + tt * P:M + (tt + 1) * P], small("router", kt * 8, 8),
                             kt == 0, kt == KD - 1, xt[kt], free[b])
            turned, held_x = [], []
            for tt in range(2):
                for q in range(2):
                    bx = bank()
                    for c in range(4):
                        tx = PE([xt, free[bx]], nc.tensor.transpose, banks[bx][:, c * P:(c + 1) * P],
                                RES[:, q * 4 + c, M + tt * P:M + (tt + 1) * P], ident)
                    turned.append(tx)
                    held_x.append((tt, slice(q * 512, (q + 1) * 512), bx,
                                   AC([tx, xt], nc.scalar.activation, XTH[:, tt, q * 512:(q + 1) * 512], banks[bx][:, :], ACT.Copy)))
            lg, e1, e2, q1, q2, cm = (C8[:, i, :, :] for i in range(6))
            s1 = C8[:, 6, :, :]
            s2 = C8[:, 7, :, :]
            io = iota[:, 0:8].unsqueeze(1).to_broadcast([P, 2, 8])
            msk, rk = C8[:, 8, :, :], C8[:, 9, :, :]
            t = V([tok, xt], nc.vector.tensor_copy, lg, banks[b][:, 0:16].rearrange("p (a b) -> p a b", a=2))
            free[b] = t

            def pick(src, val, onehot, t):
                bc = lambda a: a.to_broadcast([P, 2, 8])
                t = V([t], nc.vector.tensor_reduce, val, src, AX, ALU.max)
                t = V([t], nc.vector.tensor_tensor, q1, src, bc(val), ALU.is_lt)
                t = V([t], nc.vector.scalar_tensor_tensor, q1, q1, 100.0, io, ALU.mult, ALU.add)
                t = V([t], nc.vector.tensor_reduce, s2[:, :, 0:1], q1, AX, ALU.min)
                return V([t], nc.vector.tensor_tensor, onehot, io, bc(s2[:, :, 0:1]), ALU.is_equal)

            v1, v2, g1, g2, den = (s1[:, :, i:i + 1] for i in range(5))
            t = pick(lg, v1, e1, t)
            t = V([t], nc.vector.scalar_tensor_tensor, q2, e1, -3.0e38, lg, ALU.mult, ALU.add)
            t = pick(q2, v2, e2, t)
            m_t = V([t], nc.vector.tensor_tensor, msk, e1, e2, ALU.add)
            b = bank()
            mm(banks[b][:, 0:8], upper, msk[:, 0, :], True, True, m_t, free[b])
            mm(banks[b][:, 8:16], ones, msk[:, 0, :], True, False)
            mm(banks[b][:, 8:16], upper, msk[:, 1, :], False, True)
            mm(banks[b][:, 16:24], ones, msk[:, 0, :], True, False)
            tok = mm(banks[b][:, 16:24], ones, msk[:, 1, :], False, True)
            rk_t = V([tok], nc.vector.tensor_copy, rk, banks[b][:, 0:16].rearrange("p (a b) -> p a b", a=2))
            t = V([tok], nc.vector.reduce_max, CNT[:, 8:9], banks[b][:, 16:24], AX)
            free[b] = [rk_t, t]
            cnt_t = V([t], nc.vector.tensor_copy, CNI[:, :], CNT[:, 8:9])
            xtt = []
            for tt, sl, bx, h in held_x:
                free[bx] = V([h], nc.vector.tensor_tensor, XTL[:, tt, sl], banks[bx][:, :], XTH[:, tt, sl].bitcast(F32), ALU.subtract)
                xtt.append([h, free[bx]])
            t = V([m_t], nc.vector.tensor_tensor, den, v2, v1, ALU.subtract)
            t = AC([t], nc.scalar.activation, g2, den, ACT.Exp)
            t = V([t], nc.vector.tensor_scalar, den, g2, 1.0, None, ALU.add)
            t = V([t], nc.vector.reciprocal, g1, den)
            t = V([t], nc.vector.tensor_tensor, g2, g2, g1, ALU.mult)
            t = V([t, m_t], nc.vector.tensor_tensor, e1, e1, g1.to_broadcast([P, 2, 8]), ALU.mult)
            t = V([t], nc.vector.tensor_tensor, e2, e2, g2.to_broadcast([P, 2, 8]), ALU.mult)
            comb = V([t], nc.vector.tensor_tensor, cm, e1, e2, ALU.add)
            ready = [xt, rk_t, cnt_t, m_t]

            flat = lambda b: b[:, :, :].rearrange("p a b -> p (a b)")
            tmp = [flat(XC)[:, i * 512:(i + 1) * 512] for i in range(2)]
            tm2 = [flat(XC)[:, 1024 + i * 512:1024 + (i + 1) * 512] for i in range(2)]

            def gate_up(nT, lh, ll, lt, HH, HL, hread, rd, between={}):
                ht = [[] for _ in range(11)]
                pend = []

                def turn():
                    while pend:
                        n0, nn, i, j, t = pend.pop(0)
                        b = bank()
                        for c in range(nn):
                            tok = PE([t, free[b]], nc.tensor.transpose, banks[b][:, c * P:(c + 1) * P], tm2[j][:, c * P:(c + 1) * P], ident)
                        src = banks[b][:, 0:nn * P].rearrange("p (a b) -> p a b", a=nn)
                        hh = HH[:, n0:n0 + nn, i * P:(i + 1) * P]
                        h = AC([tok, hread], nc.scalar.activation, hh, src, ACT.Copy)
                        l = V([h, hread], nc.vector.tensor_tensor, HL[:, n0:n0 + nn, i * P:(i + 1) * P], src, hh.bitcast(F32), ALU.subtract)
                        free[b] = l
                        rd[j] = [rd[j], tok]
                        for n in range(n0, n0 + nn):
                            ht[n] += [h, l]

                for gi, (n0, nn) in enumerate(((0, 4), (4, 4), (8, 3))):
                    w = nn * P
                    two = []
                    for up in range(2):
                        bs = [bank() for _ in range(nT)]
                        toks = [None] * nT
                        for kt in range(KD):
                            pieces = run_of(nn)
                            for i in range(nT):
                                for wh, wl, wt, o, m in pieces:
                                    out = banks[bs[i]][:, o:o + m]
                                    mm(out, lh(kt, i), wh, kt == 0, False, wt, free[bs[i]], lt(kt))
                                    mm(out, ll(kt, i), wh, False, False)
                                    toks[i] = mm(out, lh(kt, i), wl, False, kt == KD - 1)
                            run_done(nn, toks[-1])
                        two.append((bs, toks))
                        if up == 0:
                            turn()
                            for f in between.get((gi, 0), ()):
                                f()
                    (gb, gt), (ub, ut) = two
                    for i in range(nT):
                        j = i if nT == 2 else gi % 2
                        t = AC([gt[i], rd[j], ready], nc.scalar.activation, tmp[j][:, 0:w], banks[gb[i]][:, 0:w], ACT.Silu)
                        free[gb[i]] = t
                        t = V([ut[i], t, rd[j]], nc.vector.tensor_tensor, tm2[j][:, 0:w], tmp[j][:, 0:w], banks[ub[i]][:, 0:w], ALU.mult)
                        free[ub[i]] = t
                        rd[j] = t
                        pend.append((n0, nn, i, j, t))
                    for f in between.get((gi, 1), ()):
                        f()
                return ht, toks[-1], turn

            def sparse():
                sp = ExitStack()
                SE = [sb(f"SE{i}", [P, 2, P], F32R, sp) for i in range(2)]
                ST = [sb(f"ST{i}", [P, S], F32R, sp) for i in range(2)]
                GH = [sb(f"GH{i}", [P, KD, P], F32R, sp) for i in range(2)]
                GL = [sb(f"GL{i}", [P, KD, P], F32R, sp) for i in range(2)]
                HH = [sb(f"SHH{i}", [P, 11, P], F32R, sp) for i in range(2)]
                HL = [sb(f"SHL{i}", [P, 11, P], F32R, sp) for i in range(2)]
                CO = sb("CO", [P, 2], F32, sp)
                OF = SQ[:, :, :].rearrange("p a b -> p (a b)")
                OH = XH[:, :, :].rearrange("p a b -> p (a b)")
                OL = XL[:, :, :].rearrange("p a b -> p (a b)")
                sread, stread, gread, hread, coread = ([None, None] for _ in range(5))
                oread, ofread, rd = [None, None], [None, None], [None, None]
                chosen, selected = {}, {}

                def choose(x):
                    k = x % 2
                    s_t = [V([ready, sread[k]], nc.vector.tensor_scalar, SE[k][:, tt, :], iota, rk[:, tt, x:x + 1], msk[:, tt, x:x + 1],
                             ALU.is_equal, ALU.mult) for tt in range(2)]
                    chosen[x] = s_t

                def select(x):
                    k = x % 2
                    s_t = chosen.pop(x)
                    b = bank()
                    for tt in range(2):
                        tok = PE([s_t, free[b]], nc.tensor.transpose, banks[b][:, tt * P:(tt + 1) * P], SE[k][:, tt, :].bitcast(F32), ident)
                    for tt in range(2):
                        tok = mm(banks[b][:, 256:257], SE[k][:, tt, :].bitcast(F32), cm[:, tt, x:x + 1], tt == 0, tt == 1, comb)
                    st_t = AC([tok, stread[k]], nc.scalar.activation, ST[k][:, :], banks[b][:, 0:256], ACT.Copy)
                    co_t = AC([tok, coread[k]], nc.scalar.activation, CO[:, k:k + 1], banks[b][:, 256:257], ACT.Copy)
                    free[b] = [st_t, co_t]
                    selected[x] = (s_t, st_t, co_t, [])

                def gather(x, q):
                    k = x % 2
                    s_t, st_t, co_t, gt = selected[x]
                    two = []
                    for src, dst in ((XTH, GH), (XTL, GL)):
                        b = bank()
                        for c in range(4):
                            kt = q * 4 + c
                            for tt in range(2):
                                tok = mm(banks[b][:, c * P:(c + 1) * P], src[:, tt, kt * P:(kt + 1) * P], SE[k][:, tt, :],
                                         tt == 0, tt == 1, xtt, s_t, free[b])
                        out = dst[k][:, q * 4:q * 4 + 4, :].rearrange("p a b -> p (a b)")
                        if src is XTH:
                            free[b] = AC([tok, gread[k]], nc.scalar.activation, out, banks[b][:, :], ACT.Copy)
                        else:
                            free[b] = V([tok, gread[k]], nc.vector.tensor_copy, out, banks[b][:, :])
                        two.append(free[b])
                    gt += [two] * 4
                    sread[k] = tok

                def scatter(x, ot, st_t, js):
                    k = x % 2
                    for j in js:
                        b = bank()
                        for i in range(2):
                            nt = 2 * j + i
                            o = k * 1024 + nt * P
                            mm(banks[b][:, i * S:(i + 1) * S], OH[:, o:o + P], ST[k][:, :], True, False, ot[nt // 4], st_t, free[b])
                            tok = mm(banks[b][:, i * S:(i + 1) * S], OL[:, o:o + P], ST[k][:, :], False, True)
                        r = RES[:, 2 * j:2 * j + 2, M:T]
                        acc[j] = V([tok, acc[j]], nc.vector.tensor_tensor, r, r, banks[b][:, :].rearrange("p (a b) -> p a b", a=2), ALU.add)
                        free[b] = acc[j]
                    oread[k] = tok
                    stread[k] = tok

                choose(0)
                select(0)
                gather(0, 0)
                gather(0, 1)
                acc = [V([ready, turned], nc.vector.tensor_scalar, RES[:, 2 * i:2 * i + 2, M:T], RES[:, 2 * i:2 * i + 2, M:T], ALPHA, None, ALU.mult)
                       for i in range(4)]
                late = None
                for x in range(8):
                    k = x % 2
                    _, st_t, co_t, gt = selected.pop(x)
                    between = {(0, 0): [], (0, 1): []}
                    if late is not None:
                        between[(0, 0)].append(lambda: scatter(*late, (0, 1)))
                        between[(0, 1)].append(lambda: scatter(*late, (2, 3)))
                    if x < 7:
                        between[(0, 0)].append(lambda: choose(x + 1))
                        between[(1, 0)] = [lambda: select(x + 1)]
                        between[(1, 1)] = [lambda: gather(x + 1, 0)]
                        between[(2, 0)] = [lambda: gather(x + 1, 1)]
                    ht, gread[k], turn = gate_up(1, lambda kt, i: GH[k][:, kt, :], lambda kt, i: GL[k][:, kt, :], lambda kt: gt[kt],
                                                 HH[k], HL[k], hread[k], rd, between)
                    ot = []
                    for g in range(2):
                        b = bank()
                        for kt in range(11):
                            if g == 0 and kt == 8:
                                turn()
                            wh, wl, wt = tile_of(4)
                            mm(banks[b][:, :], HH[k][:, kt, :], wh, kt == 0, False, wt, free[b], ht[kt])
                            mm(banks[b][:, :], HL[k][:, kt, :], wh, False, False)
                            tok = mm(banks[b][:, :], HH[k][:, kt, :], wl, False, kt == 10)
                            tile_done(tok)
                        o = slice(k * 1024 + g * 512, k * 1024 + (g + 1) * 512)
                        f = AC([tok, co_t, ofread[g]], nc.scalar.activation, OF[:, g * 512:(g + 1) * 512], banks[b][:, :], ACT.Copy, scale=CO[:, k:k + 1])
                        free[b] = f
                        h = AC([f, oread[k], ready], nc.scalar.activation, OH[:, o], OF[:, g * 512:(g + 1) * 512], ACT.Copy)
                        l = V([h, oread[k]], nc.vector.tensor_tensor, OL[:, o], OF[:, g * 512:(g + 1) * 512], OH[:, o].bitcast(F32), ALU.subtract)
                        ofread[g] = [h, l]
                        coread[k] = f
                        ot.append([h, l])
                    hread[k] = tok
                    late = (x, ot, st_t)
                scatter(*late, range(4))
                sp.close()

            def every_token():
                sp = ExitStack()
                HH = [sb(f"EHH{i}", [P, 11, S], F32R, sp) for i in range(2)]
                HL = [sb(f"EHL{i}", [P, 11, S], F32R, sp) for i in range(2)]
                ACC = sb("ACC", [P, 2, D], F32, sp)
                hread = [None, None]
                rd = [None, None]
                acc = {}
                xs, scaled = [], []
                for kt in range(KD):
                    h = AC([ready], nc.scalar.activation, XH[:, kt, :], RES[:, kt, :], ACT.Copy)
                    xs.append([h, V([h], nc.vector.tensor_tensor, XL[:, kt, :], RES[:, kt, :], XH[:, kt, :].bitcast(F32), ALU.subtract)])
                    scaled.append(V([xs, turned], nc.vector.tensor_scalar, RES[:, kt, M:T], RES[:, kt, M:T], ALPHA, None, ALU.mult))
                for x in range(8):
                    k = x % 2
                    ht, _, turn = gate_up(2, xh_t, xl_t, lambda kt: xs[kt], HH[k], HL[k], hread[k], rd)
                    turn()
                    for g in range(2):
                        bs = [bank(), bank()]
                        toks = [None, None]
                        for kt in range(11):
                            wh, wl, wt = tile_of(4)
                            for tt in range(2):
                                hh, hl = (a[k][:, kt, tt * P:(tt + 1) * P] for a in (HH, HL))
                                mm(banks[bs[tt]][:, :], hh, wh, kt == 0, False, wt, free[bs[tt]], ht[kt])
                                mm(banks[bs[tt]][:, :], hl, wh, False, False)
                                toks[tt] = mm(banks[bs[tt]][:, :], hh, wl, False, kt == 10)
                            tile_done(toks[1])
                        for tt in range(2):
                            a = ACC[:, tt, g * 512:(g + 1) * 512]
                            c = cm[:, tt, x:x + 1]
                            if x == 0:
                                t = V([toks[tt], ready, comb], nc.vector.tensor_scalar, a, banks[bs[tt]][:, :], c, None, ALU.mult)
                            else:
                                t = V([toks[tt], acc[(g, tt)]], nc.vector.scalar_tensor_tensor, a, banks[bs[tt]][:, :], c, a, ALU.mult, ALU.add)
                            acc[(g, tt)] = t
                            free[bs[tt]] = t
                    hread[k] = toks[1]
                for tt in range(2):
                    for g in range(2):
                        b = bank()
                        for c in range(4):
                            tok = PE([acc[(g, tt)], free[b]], nc.tensor.transpose, banks[b][:, c * P:(c + 1) * P],
                                     ACC[:, tt, (g * 4 + c) * P:(g * 4 + c + 1) * P], ident)
                        r = RES[:, g * 4:g * 4 + 4, M + tt * P:M + (tt + 1) * P]
                        free[b] = V([tok, scaled], nc.vector.tensor_tensor, r, r, banks[b][:, :].rearrange("p (a b) -> p a b", a=4), ALU.add)
                sp.close()

            joined = branch(CNI[0:1, 0:1], ready, sparse, every_token)
            st.close()
            return layer_norm(RES, KD, "ln2g", "ln2b", 1, LN_EPS, [joined] * KD, joined, plain_norm(None))

        if upto >= 6:
            xt = mix_layer(0, xt)
        if upto >= 7:
            xt = dense(xt)
        if upto >= 8:
            xt = mix_layer(1, xt)
        if upto >= 9:
            xt = moe(xt)

        end = everyone()
        out_t = dma(out_d, RES[:, :, M:T], "s_out", end, xt, res_after)
        SP([out_t], None)

        for q in (PE, AC, V, G, SP):
            q.count()

        @block.sync
        def _(eng):
            SP.emit(eng)

        @block.gpsimd
        def _(eng):
            G.emit(eng)

        @block.scalar
        def _(eng):
            AC.emit(eng)

        @block.vector
        def _(eng):
            V.emit(eng)

        @block.tensor
        def _(eng):
            PE.emit(eng)


def feature_tiles(w):
    k, n = w.shape
    return w.reshape(k // P, P, n // P, P).transpose(2, 0, 1, 3).reshape(-1, P, P)


def head_tiles(w, groups, order):
    k, n = w.shape
    t = w.reshape(k // P, P, 3, groups, 2, 2, P)
    return np.concatenate([t[:, :, kind, g, half].transpose(0, 2, 1, 3).reshape(-1, P, P)
                           for g, half in order for kind in range(3)])


def token_tiles(w):
    k, n = w.shape
    return w.reshape(k // P, P, n // 512, 4, P).transpose(2, 0, 3, 1, 4).reshape(-1, P, P)


def gate_up_tiles(a, b):
    parts = []
    for n0, n1 in ((0, 4), (4, 8), (8, 11)):
        for w in (a, b):
            t = w[:, n0 * P:n1 * P]
            parts.append(t.reshape(KD, P, n1 - n0, P).transpose(0, 2, 1, 3).reshape(-1, P, P))
    return np.concatenate(parts)


def paired_tiles(a, b):
    k, n = a.shape
    return np.stack([feature_tiles(a).reshape(n // P, k // P, P, P), feature_tiles(b).reshape(n // P, k // P, P, P)],
                    axis=1).reshape(-1, P, P)


def weight_stream(i):
    parts = [head_tiles(i["a_w_qkv"][0], 3, [(g, h) for h in range(2) for g in range(3)]), feature_tiles(i["a_w_o"][0]),
             feature_tiles(i["ffn_w1"][0]), feature_tiles(i["ffn_w2"][0]),
             head_tiles(i["b_w_qkv"][0], 2, [(g, h) for g in range(2) for h in range(2)]), feature_tiles(i["b_w_o"][0]),
             feature_tiles(i["ffn_w1"][1]), feature_tiles(i["ffn_w2"][1])]
    heads = np.arange(512).reshape(2, 4, 64).transpose(1, 0, 2).reshape(-1)
    for l in range(2):
        w = i["w_in_2"][l]
        parts += [paired_tiles(w[:, 1280:1792], w[:, 768:1280]), feature_tiles(w[:, heads]), feature_tiles(w[:, 512:768]),
                  feature_tiles(w[:, 1792:])]
        parts += [feature_tiles(i["w_attn_proj_2"][l]), feature_tiles(i["w_conv_proj_2"][l]), feature_tiles(i["w_out_2"][l])]
        if l == 0:
            parts += [paired_tiles(i["ffn_w_gate_2"][0], i["ffn_w_up_2"][0]), feature_tiles(i["ffn_w_down_2"][0])]
        else:
            for e in range(8):
                parts += [gate_up_tiles(i["moe_w_gate_2"][0, e], i["moe_w_up_2"][0, e]), token_tiles(i["moe_w_down_2"][0, e])]
    w = np.concatenate(parts)
    return np.ascontiguousarray(w.reshape(-1, UT, P, P).transpose(0, 2, 1, 3)).reshape(-1, P, UT * P)


def columns(v):
    return v.reshape(-1, P).T


def small_params(i):
    c = [columns(i["norm_mix"]), columns(i["norm_ffn"]), columns(i["emb_ln_g_2"]), columns(i["emb_ln_b_2"]),
         columns(i["ln1_g_2"]), columns(i["ln1_b_2"]), columns(i["ln2_g_2"]), columns(i["ln2_b_2"]),
         i["conv_dw_2"].reshape(2, 31, 4, P).transpose(3, 0, 2, 1).reshape(P, -1),
         columns(i["conv_b_2"]), columns(i["conv_ln_g_2"]), columns(i["conv_ln_b_2"]),
         np.stack([np.tile(i[n][0], 2) for n in ("a_q_gain", "a_k_gain", "b_q_gain", "b_k_gain")], axis=1),
         np.broadcast_to(i["sinks_2"].reshape(1, -1), (P, 16)),
         i["router_2"][0].reshape(KD, P, 8).transpose(1, 0, 2).reshape(P, -1)]
    return np.ascontiguousarray(np.concatenate(c, axis=1))


def layout(i):
    ident = np.eye(P, dtype=np.float32)
    consts = np.concatenate([ident, np.ones((P, P), np.float32),
                             np.broadcast_to(np.arange(P, dtype=np.float32), (P, P)), ident[::-1],
                             np.triu(np.ones((P, P), np.float32), 1)], axis=1)
    one = np.ones((1, 24), np.float32)
    feat = lambda a: np.ascontiguousarray(a.T.reshape(KD, P, -1).transpose(1, 0, 2))
    return {"w": weight_stream(i), "x": feat(i["x"][0]), "meta": feat(i["meta_tokens_2"]),
            "small": small_params(i), "consts": consts, "look": lookups(),
            "tab1": np.concatenate([i["rel_bias"], one]), "tab2": np.concatenate([i["rel_bias_2"], one[:, :8]])}


def kernel(**inputs):
    import concourse.bacc as _bacc
    from concourse.bass_utils import run_bass_kernel_spmd as _run

    arrays = layout({k: np.asarray(v) for k, v in inputs.items()})
    nc = _bacc.Bacc("TRN2", target_bir_lowering=False, num_devices=1)
    args = [nc.dram_tensor(f"in_{n}", a.shape, F32, kind="ExternalInput").ap() for n, a in arrays.items()]
    out = nc.dram_tensor("out", (P, KD, S), F32, kind="ExternalOutput").ap()
    model_kernel(nc, *args, out)
    r = _run(nc, [{f"in_{n}": np.ascontiguousarray(a) for n, a in arrays.items()}], core_ids=[0])
    y = r.results[0]["out"]
    return np.ascontiguousarray(y.transpose(2, 1, 0).reshape(1, S, D))
```
